# Optimizing a Trainium2 kernel written in Bass

```python
import math
import jax, jax.numpy as jnp
from jax import lax
import numpy as np

D_MODEL = 1024
BATCH = 1
SEQ = 512
DEPTH = 2

HEAD_DIM = 64
MLA_HEADS = 8
MLA_NOPE = 64
MLA_ROPE = 32
MLA_V = 64
MLA_Q_LORA = 384
MLA_KV_LORA = 256
ROPE_THETA = 10000.0
SWA_HEADS = 8
SWA_KV_HEADS = 2
SWA_WINDOW = 128
REL_BUCKETS = 32
REL_MAX_DIST = 128
FOX_HEADS = 16
D_FF = 4 * D_MODEL
D_PLE = 256
BLOCK_Q = 128
DN_ALPHA = (2 * DEPTH) ** 0.25
DN_BETA = (8 * DEPTH) ** -0.25
NORM_EPS = 1e-5
NEG_INF = -1e30
N_EVEN = (DEPTH + 1) // 2
N_ODD = DEPTH // 2
EVEN_SPLIT = (MLA_Q_LORA, MLA_KV_LORA, MLA_ROPE, SWA_HEADS * HEAD_DIM,
              SWA_KV_HEADS * HEAD_DIM, SWA_KV_HEADS * HEAD_DIM)
EVEN_IN = MLA_Q_LORA + MLA_KV_LORA + MLA_ROPE + (SWA_HEADS + 2 * SWA_KV_HEADS) * HEAD_DIM
EVEN_MIX = MLA_HEADS * MLA_V + SWA_HEADS * HEAD_DIM
ODD_SPLIT = (FOX_HEADS * HEAD_DIM, FOX_HEADS * HEAD_DIM, FOX_HEADS * HEAD_DIM, FOX_HEADS)
ODD_IN = 3 * FOX_HEADS * HEAD_DIM + FOX_HEADS
ODD_MIX = FOX_HEADS * HEAD_DIM


def _split(h, sizes):
    out, o = [], 0
    for n in sizes:
        out.append(h[..., o:o + n])
        o += n
    return out

def _layer_norm(x, g, b):
    xf = x.astype(jnp.float32)
    mu = jnp.mean(xf, -1, keepdims=True)
    var = jnp.mean(jnp.square(xf - mu), -1, keepdims=True)
    y = (xf - mu) * lax.rsqrt(var + NORM_EPS)
    return (y * g.astype(jnp.float32) + b.astype(jnp.float32)).astype(x.dtype)

def _rms_norm(x, g):
    xf = x.astype(jnp.float32)
    y = xf * lax.rsqrt(jnp.mean(jnp.square(xf), -1, keepdims=True) + NORM_EPS)
    return (y * g.astype(jnp.float32)).astype(x.dtype)

def _rope_tables(seq_len, dim):
    inv = 1.0 / (ROPE_THETA ** (jnp.arange(0, dim, 2, dtype=jnp.float32) / dim))
    ang = jnp.arange(seq_len, dtype=jnp.float32)[:, None] * inv[None, :]
    return jnp.cos(ang), jnp.sin(ang)

def _apply_rope(x, cos, sin):
    x1, x2 = jnp.split(x.astype(jnp.float32), 2, axis=-1)
    c = cos[:, None, :]
    s = sin[:, None, :]
    return jnp.concatenate([x1 * c - x2 * s, x2 * c + x1 * s], -1).astype(x.dtype)

def _t5_bucket(dist):
    exact = REL_BUCKETS // 2
    d = jnp.maximum(dist, 1).astype(jnp.float32)
    large = exact + (jnp.log(d / exact) / math.log(REL_MAX_DIST / exact)
                     * (REL_BUCKETS - exact)).astype(jnp.int32)
    large = jnp.minimum(large, REL_BUCKETS - 1)
    return jnp.where(dist < exact, dist, large)

def _mla_attend(q_nope, q_rope, k_nope, k_rope, v):
    B, S, H, _ = q_nope.shape
    nb = S // BLOCK_Q
    scale = (MLA_NOPE + MLA_ROPE) ** -0.5
    qn = q_nope.reshape(B, nb, BLOCK_Q, H, MLA_NOPE).transpose(1, 0, 2, 3, 4)
    qr = q_rope.reshape(B, nb, BLOCK_Q, H, MLA_ROPE).transpose(1, 0, 2, 3, 4)
    kpos = jnp.arange(S)

    def block(args):
        i, qn_b, qr_b = args
        s = (jnp.einsum('bqhd,bkhd->bhqk', qn_b, k_nope, preferred_element_type=jnp.float32)
             + jnp.einsum('bqhd,bkd->bhqk', qr_b, k_rope, preferred_element_type=jnp.float32)) * scale
        qpos = i * BLOCK_Q + jnp.arange(BLOCK_Q)
        s = jnp.where(kpos[None, :] <= qpos[:, None], s, NEG_INF)
        w = jax.nn.softmax(s, axis=-1).astype(v.dtype)
        return jnp.einsum('bhqk,bkhd->bqhd', w, v)

    out = lax.map(block, (jnp.arange(nb), qn, qr))
    return out.transpose(1, 0, 2, 3, 4).reshape(B, S, H * MLA_V)

def _swa_attend(q, k, v, sinks, rel_bias):
    B, S, H, d = q.shape
    KVH = k.shape[2]
    G = H // KVH
    nb = S // BLOCK_Q
    qb = q.reshape(B, nb, BLOCK_Q, KVH, G, d)

    def band(t):
        tb = t.reshape(B, nb, BLOCK_Q, KVH, d)
        prev = jnp.pad(tb, ((0, 0), (1, 0), (0, 0), (0, 0), (0, 0)))[:, :-1]
        return jnp.concatenate([prev, tb], axis=2)

    kb, vb = band(k), band(v)
    s = jnp.einsum('bnqkgd,bnskd->bnkgqs', qb, kb, preferred_element_type=jnp.float32) * (d ** -0.5)
    a = jnp.arange(BLOCK_Q)[:, None]
    col = jnp.arange(2 * BLOCK_Q)[None, :]
    dist = a + BLOCK_Q - col
    in_win = (dist >= 0) & (dist < SWA_WINDOW)
    pad = (jnp.arange(nb)[:, None, None] == 0) & (col < BLOCK_Q)[None]
    valid = in_win[None] & ~pad
    bias = rel_bias[_t5_bucket(jnp.maximum(dist, 0))].astype(jnp.float32)
    bias = bias.transpose(2, 0, 1).reshape(KVH, G, BLOCK_Q, 2 * BLOCK_Q)
    s = jnp.where(valid[None, :, None, None], s + bias, NEG_INF)
    sink = jnp.broadcast_to(sinks.astype(jnp.float32).reshape(1, 1, KVH, G, 1, 1), s.shape[:-1] + (1,))
    w = jax.nn.softmax(jnp.concatenate([s, sink], axis=-1), axis=-1)[..., :-1].astype(v.dtype)
    out = jnp.einsum('bnkgqs,bnskd->bnqkgd', w, vb)
    return out.reshape(B, S, H * d)

def _fox_attend(q, k, v, log_f):
    B, S, H, d = q.shape
    nb = S // BLOCK_Q
    c = jnp.cumsum(log_f, axis=1)
    cq = c.reshape(B, nb, BLOCK_Q, H).transpose(1, 0, 3, 2)
    ck = c.transpose(0, 2, 1)
    qb = q.reshape(B, nb, BLOCK_Q, H, d).transpose(1, 0, 2, 3, 4)
    kpos = jnp.arange(S)

    def block(args):
        i, q_b, cq_b = args
        s = jnp.einsum('bqhd,bkhd->bhqk', q_b, k, preferred_element_type=jnp.float32) * (d ** -0.5)
        s = s + cq_b[..., :, None] - ck[:, :, None, :]
        qpos = i * BLOCK_Q + jnp.arange(BLOCK_Q)
        s = jnp.where(kpos[None, :] <= qpos[:, None], s, NEG_INF)
        w = jax.nn.softmax(s, axis=-1).astype(v.dtype)
        return jnp.einsum('bhqk,bkhd->bqhd', w, v)

    out = lax.map(block, (jnp.arange(nb), qb, cq))
    return out.transpose(1, 0, 2, 3, 4).reshape(B, S, H * d)

def _even_mixer(x, w_in, q_norm, w_uq, kv_norm, w_ukv, sinks, w_out, rel_bias, cos, sin):
    B, S, _ = x.shape
    h = x @ w_in
    c_q, c_kv, k_rope, q_s, k_s, v_s = _split(h, EVEN_SPLIT)
    q = (_rms_norm(c_q, q_norm) @ w_uq).reshape(B, S, MLA_HEADS, MLA_NOPE + MLA_ROPE)
    q_nope = q[..., :MLA_NOPE]
    q_rope = _apply_rope(q[..., MLA_NOPE:], cos, sin)
    kv = (_rms_norm(c_kv, kv_norm) @ w_ukv).reshape(B, S, MLA_HEADS, MLA_NOPE + MLA_V)
    k_nope, v = kv[..., :MLA_NOPE], kv[..., MLA_NOPE:]
    k_rope = _apply_rope(k_rope[:, :, None, :], cos, sin)[:, :, 0]
    o_mla = _mla_attend(q_nope, q_rope, k_nope, k_rope, v)
    o_swa = _swa_attend(q_s.reshape(B, S, SWA_HEADS, HEAD_DIM),
                        k_s.reshape(B, S, SWA_KV_HEADS, HEAD_DIM),
                        v_s.reshape(B, S, SWA_KV_HEADS, HEAD_DIM), sinks, rel_bias)
    return jnp.concatenate([o_mla, o_swa], axis=-1) @ w_out

def _odd_mixer(x, w_in, b_f, w_out):
    B, S, _ = x.shape
    q, k, v, f = _split(x @ w_in, ODD_SPLIT)
    log_f = jax.nn.log_sigmoid((f + b_f).astype(jnp.float32))
    o = _fox_attend(q.reshape(B, S, FOX_HEADS, HEAD_DIM), k.reshape(B, S, FOX_HEADS, HEAD_DIM),
                    v.reshape(B, S, FOX_HEADS, HEAD_DIM), log_f)
    return o @ w_out

def _sq_relu_mlp(x, w_up, w_down):
    return jnp.square(jax.nn.relu(x @ w_up)) @ w_down

def first_inputs(seed: int = 0) -> dict:
    key = jax.random.key(seed)
    ks = jax.random.split(key, 24)
    nrm = jax.random.normal
    f32 = jnp.float32
    return {
        "x": nrm(ks[0], (BATCH, SEQ, D_MODEL), f32),
        "p": nrm(ks[1], (DEPTH, BATCH, SEQ, D_PLE), f32),
        "rel_bias": 0.5 * nrm(ks[2], (REL_BUCKETS, SWA_HEADS), f32),
        "ev_w_in": nrm(ks[3], (N_EVEN, D_MODEL, EVEN_IN), f32) * D_MODEL ** -0.5,
        "ev_q_norm": 1.0 + 0.02 * nrm(ks[4], (N_EVEN, MLA_Q_LORA), f32),
        "ev_w_uq": nrm(ks[5], (N_EVEN, MLA_Q_LORA, MLA_HEADS * (MLA_NOPE + MLA_ROPE)), f32) * MLA_Q_LORA ** -0.5,
        "ev_kv_norm": 1.0 + 0.02 * nrm(ks[6], (N_EVEN, MLA_KV_LORA), f32),
        "ev_w_ukv": nrm(ks[7], (N_EVEN, MLA_KV_LORA, MLA_HEADS * (MLA_NOPE + MLA_V)), f32) * MLA_KV_LORA ** -0.5,
        "ev_sinks": 0.5 * nrm(ks[8], (N_EVEN, SWA_HEADS), f32),
        "ev_w_out": nrm(ks[9], (N_EVEN, EVEN_MIX, D_MODEL), f32) * (EVEN_MIX ** -0.5 * DN_BETA),
        "od_w_in": nrm(ks[10], (N_ODD, D_MODEL, ODD_IN), f32) * D_MODEL ** -0.5,
        "od_b_f": jax.random.uniform(ks[11], (N_ODD, FOX_HEADS), f32, 1.0, 4.0),
        "od_w_out": nrm(ks[12], (N_ODD, ODD_MIX, D_MODEL), f32) * (ODD_MIX ** -0.5 * DN_BETA),
        "ln1_g": 1.0 + 0.02 * nrm(ks[13], (DEPTH, D_MODEL), f32),
        "ln1_b": 0.02 * nrm(ks[14], (DEPTH, D_MODEL), f32),
        "w_up": nrm(ks[15], (DEPTH, D_MODEL, D_FF), f32) * D_MODEL ** -0.5,
        "w_down": nrm(ks[16], (DEPTH, D_FF, D_MODEL), f32) * (D_FF ** -0.5 * DN_BETA),
        "ln2_g": 1.0 + 0.02 * nrm(ks[17], (DEPTH, D_MODEL), f32),
        "ln2_b": 0.02 * nrm(ks[18], (DEPTH, D_MODEL), f32),
        "ple_w_proj": nrm(ks[19], (DEPTH, D_PLE, D_MODEL), f32) * D_PLE ** -0.5,
        "ple_w_gate": nrm(ks[20], (DEPTH, D_MODEL, D_MODEL), f32) * D_MODEL ** -0.5,
        "ple_b_gate": 0.02 * nrm(ks[21], (DEPTH, D_MODEL), f32),
    }

def first_block(x, p, rel_bias, ev_w_in, ev_q_norm, ev_w_uq, ev_kv_norm, ev_w_ukv, ev_sinks, ev_w_out,
              od_w_in, od_b_f, od_w_out, ln1_g, ln1_b, w_up, w_down, ln2_g, ln2_b,
              ple_w_proj, ple_w_gate, ple_b_gate):
    S = x.shape[1]
    cos, sin = _rope_tables(S, MLA_ROPE)
    for i in range(DEPTH):
        j = i // 2
        if i % 2 == 0:
            m = _even_mixer(x, ev_w_in[j], ev_q_norm[j], ev_w_uq[j], ev_kv_norm[j], ev_w_ukv[j],
                            ev_sinks[j], ev_w_out[j], rel_bias, cos, sin)
        else:
            m = _odd_mixer(x, od_w_in[j], od_b_f[j], od_w_out[j])
        x = _layer_norm(DN_ALPHA * x + m, ln1_g[i], ln1_b[i])
        x = _layer_norm(DN_ALPHA * x + _sq_relu_mlp(x, w_up[i], w_down[i]), ln2_g[i], ln2_b[i])
        gate = jax.nn.sigmoid(x @ ple_w_gate[i] + ple_b_gate[i])
        x = x + gate * (p[i] @ ple_w_proj[i])
    return x


DEPTH_2 = 1

GLA_HEADS = 4
GLA_DK = 64
GLA_DV = 128
GLA_QK_WIDTH = GLA_HEADS * GLA_DK
GLA_WIDTH = GLA_HEADS * GLA_DV
GATE_RANK = 16
GATE_NORMALIZER = 16.0
CHUNK = 64
CONV_WIDTH = D_MODEL // 2
CONV_GROUPS = 8
CONV_K = 3
MIX_WIDTH = GLA_WIDTH + CONV_WIDTH
D_FF_2 = int(math.ceil(8 * D_MODEL / 3 / 256) * 256)
NORM_EPS_2 = 1e-6

COL_Q = GLA_QK_WIDTH
COL_K = GLA_QK_WIDTH
COL_V = GLA_WIDTH
COL_G = GLA_WIDTH
COL_A = GATE_RANK
COL_CB = CONV_WIDTH
COL_CC = CONV_WIDTH
COL_CH = CONV_WIDTH
IN_COLS = COL_Q + COL_K + COL_V + COL_G + COL_A + COL_CB + COL_CC + COL_CH


def rmsnorm(x, g):
    xf = x.astype(jnp.float32)
    y = xf * lax.rsqrt(jnp.mean(xf * xf, axis=-1, keepdims=True) + NORM_EPS_2)
    return (y * g.astype(jnp.float32)).astype(x.dtype)

def gla_chunked(q, k, v, log_a):
    bsz, seq, heads, dk = q.shape
    dv = v.shape[-1]
    n_chunks = seq // CHUNK

    def to_chunks(t):
        return t.astype(jnp.float32).reshape(bsz, n_chunks, CHUNK, heads, t.shape[-1]).transpose(1, 0, 3, 2, 4)

    q, k, v, log_a = to_chunks(q), to_chunks(k), to_chunks(v), to_chunks(log_a)
    b = jnp.cumsum(log_a, axis=-2)
    b_last = b[..., -1:, :]
    q_i = q * jnp.exp(b)
    k_i = k * jnp.exp(-b)
    k_s = k * jnp.exp(b_last - b)

    causal = jnp.tril(jnp.ones((CHUNK, CHUNK), dtype=bool))
    scores = jnp.einsum('nbhck,nbhsk->nbhcs', q_i, k_i)
    scores = jnp.where(causal, scores, 0.0)
    o_intra = jnp.einsum('nbhcs,nbhsv->nbhcv', scores, v)

    chunk_kv = jnp.einsum('nbhsk,nbhsv->nbhkv', k_s, v)
    chunk_decay = jnp.exp(b_last[..., 0, :])

    def step(state, inp):
        dec, kv_c = inp
        return dec[..., None] * state + kv_c, state

    state0 = jnp.zeros((bsz, heads, dk, dv), jnp.float32)
    _, state_prev = lax.scan(step, state0, (chunk_decay, chunk_kv))
    o_inter = jnp.einsum('nbhck,nbhkv->nbhcv', q_i, state_prev)

    o = o_intra + o_inter
    return o.transpose(1, 0, 3, 2, 4).reshape(bsz, seq, heads, dv)

def causal_depthwise_conv(u, w):
    seq = u.shape[1]
    u_pad = jnp.pad(u, ((0, 0), (CONV_K - 1, 0), (0, 0)))
    y = w[0] * u_pad[:, 0:seq]
    for j in range(1, CONV_K):
        y = y + w[j] * u_pad[:, j:j + seq]
    return y

def second_inputs(seed: int = 0) -> dict:
    key = jax.random.key(seed)
    ks = jax.random.split(key, 16)
    f32 = jnp.float32
    n = lambda k, shape, scale: (jax.random.normal(k, shape, f32) * scale)
    return {
        "x": n(ks[0], (BATCH, SEQ, D_MODEL), 1.0),
        "norm1_g": 1.0 + n(ks[1], (DEPTH_2, D_MODEL), 0.02),
        "w_in": n(ks[2], (DEPTH_2, D_MODEL, IN_COLS), D_MODEL ** -0.5),
        "w_gate_up": n(ks[3], (DEPTH_2, GATE_RANK, GLA_QK_WIDTH), GATE_RANK ** -0.5),
        "b_gate": n(ks[4], (DEPTH_2, GLA_QK_WIDTH), 0.01),
        "gla_norm_g": 1.0 + n(ks[5], (DEPTH_2, GLA_DV), 0.02),
        "conv_w": n(ks[6], (DEPTH_2, CONV_K, CONV_WIDTH), CONV_K ** -0.5),
        "w_out": n(ks[7], (DEPTH_2, MIX_WIDTH, D_MODEL), MIX_WIDTH ** -0.5),
        "norm2_g": 1.0 + n(ks[8], (DEPTH_2, D_MODEL), 0.02),
        "w_ffn_gate": n(ks[9], (DEPTH_2, D_MODEL, D_FF_2), D_MODEL ** -0.5),
        "w_ffn_up": n(ks[10], (DEPTH_2, D_MODEL, D_FF_2), D_MODEL ** -0.5),
        "w_ffn_down": n(ks[11], (DEPTH_2, D_FF_2, D_MODEL), D_FF_2 ** -0.5),
        "norm_f_g": 1.0 + n(ks[12], (D_MODEL,), 0.02),
    }

def second_block(x, norm1_g, w_in, w_gate_up, b_gate, gla_norm_g, conv_w, w_out,
              norm2_g, w_ffn_gate, w_ffn_up, w_ffn_down, norm_f_g):
    bsz, seq, _ = x.shape
    splits = np.cumsum([COL_Q, COL_K, COL_V, COL_G, COL_A, COL_CB, COL_CC])
    for l in range(DEPTH_2):
        h = rmsnorm(x, norm1_g[l])
        proj = h @ w_in[l]
        p_q, p_k, p_v, p_g, p_a, c_b, c_c, c_h = jnp.split(proj, splits, axis=-1)

        q = p_q.reshape(bsz, seq, GLA_HEADS, GLA_DK) * (GLA_DK ** -0.5)
        k = p_k.reshape(bsz, seq, GLA_HEADS, GLA_DK)
        v = p_v.reshape(bsz, seq, GLA_HEADS, GLA_DV)
        gate_logits = (p_a @ w_gate_up[l] + b_gate[l]).astype(jnp.float32)
        log_a = (jax.nn.log_sigmoid(gate_logits) / GATE_NORMALIZER).reshape(bsz, seq, GLA_HEADS, GLA_DK)
        o = gla_chunked(q, k, v, log_a)
        o = rmsnorm(o, gla_norm_g[l]).astype(x.dtype)
        o = o * jax.nn.silu(p_g.reshape(bsz, seq, GLA_HEADS, GLA_DV))
        o_gla = o.reshape(bsz, seq, GLA_WIDTH)

        u = c_c * c_h
        o_conv = c_b * causal_depthwise_conv(u, conv_w[l])

        mixed = jnp.concatenate([o_gla, o_conv], axis=-1) @ w_out[l]
        x = x + mixed

        h2 = rmsnorm(x, norm2_g[l])
        ffn = (jax.nn.silu(h2 @ w_ffn_gate[l]) * (h2 @ w_ffn_up[l])) @ w_ffn_down[l]
        x = x + ffn
    return rmsnorm(x, norm_f_g)


def setup_inputs(seed=0):
    out = dict(first_inputs(seed))
    for name, value in second_inputs(seed + 1).items():
        if name != "x":
            out[name + "_2"] = value
    return out


def reference(
    x, p, rel_bias, ev_w_in, ev_q_norm, ev_w_uq, ev_kv_norm, ev_w_ukv, ev_sinks, ev_w_out,
    od_w_in, od_b_f, od_w_out, ln1_g, ln1_b, w_up, w_down, ln2_g, ln2_b, ple_w_proj, ple_w_gate,
    ple_b_gate, norm1_g_2, w_in_2, w_gate_up_2, b_gate_2, gla_norm_g_2, conv_w_2, w_out_2,
    norm2_g_2, w_ffn_gate_2, w_ffn_up_2, w_ffn_down_2, norm_f_g_2,
):
    x = first_block(
        x, p, rel_bias, ev_w_in, ev_q_norm, ev_w_uq, ev_kv_norm, ev_w_ukv, ev_sinks, ev_w_out,
        od_w_in, od_b_f, od_w_out, ln1_g, ln1_b, w_up, w_down, ln2_g, ln2_b, ple_w_proj,
        ple_w_gate, ple_b_gate,
    )
    return second_block(
        x, norm1_g_2, w_in_2, w_gate_up_2, b_gate_2, gla_norm_g_2, conv_w_2, w_out_2, norm2_g_2,
        w_ffn_gate_2, w_ffn_up_2, w_ffn_down_2, norm_f_g_2,
    )


_drawn_inputs = setup_inputs


def setup_inputs(seed=0):
    import zlib

    import numpy as np

    out = dict(_drawn_inputs(seed))
    spreads = {}
    factors = {'ev_q_norm': 8.0,
     'ev_kv_norm': 8.0,
     'ev_sinks': 32.602,
     'ple_b_gate': 7.487,
     'b_gate_2': 8.0,
     'gla_norm_g_2': 7.882,
     'norm2_g_2': 4.797,
     'norm_f_g_2': 22.575,
     'rel_bias': 3.003}
    for name, (base, spread) in spreads.items():
        noise = np.random.default_rng([zlib.crc32(name.encode()), seed]).standard_normal(out[name].shape)
        drawn = base * np.exp(spread * noise) if base else spread * noise
        out[name] = __import__('jax').numpy.asarray(drawn.astype(out[name].dtype))
    for name, factor in factors.items():
        out[name] = (out[name] * factor).astype(out[name].dtype)
    return out
```

```python
from contextlib import ExitStack

import numpy as np

import concourse.bass as bass
from concourse import mybir

F32 = mybir.dt.float32
F32R = mybir.dt.float32r
ALU = mybir.AluOpType
ACT = mybir.ActivationFunctionType

P = 128
S = 512
T = S // P
D = 1024
KD = D // P
UNIT = 512
CHUNK = 2 * UNIT
RAW = 4
WS = 2
DEPTH = 2
ALPHA = (2 * DEPTH) ** 0.25
LN_EPS, RMS_EPS = 1e-5, 1e-6
BIG = 1e30
HD = 64
MLA_H, SWA_H, FOX_H = 8, 8, 16
ROPE = 32
MLA_SCALE = (HD + ROPE) ** -0.5
Q_LORA, KV_LORA = 384, 256
BUCKETS, MAX_DIST, WINDOW = 32, 128, 128
D_FF, D_FF2 = 4096, 2816
HT_TILES = D_FF // P
PLE_K = 2
GLA_H, DK, DV, GCH = 4, 64, 128, 64
NCH = S // GCH
RANK = 16
GATE_NORM = 16.0

STAGES = [("qs", 4), ("cq", 4), ("ckv", 4), ("uq", 3), ("kn", 1), ("vm", 1), ("out0", 8),
          ("up0", 32), ("down0", 32), ("ple0", 10),
          ("fox", 24), ("out1", 8), ("up1", 32), ("down1", 32), ("ple1", 10),
          ("gla", 24), ("out2", 8), ("ffn", 44), ("down2", 22)]
FIRST, CHUNKS = {}, 0
for _name, _n in STAGES:
    FIRST[_name] = CHUNKS
    CHUNKS += _n

CAUSAL_AT = [0, 128, 384, 768]
WINDOW_AT = [0, 128, 384, 640]
CAUSAL_S = [(0, 0), (2, 0), (0, 128), (1, 0)]
WINDOW_S = [(0, 0), (0, 128), (1, 0), (1, 256)]
CAUSAL_ORDER = [(3, 1), (0, 3), (2, 3), (1, 4)]
WINDOW_ORDER = [(0, 2), (1, 2), (2, 4), (3, 4)]
CAUSAL_T = [0, 512, 1024, 896]
WINDOW_T = [0, 256, 512, 768]


CONST_ALL = 16 * 10
E_FIRST = 7
E_FOX = 13
FOX0 = 16


def kind_of(h):
    return "mla" if h < MLA_H else "swa" if h < FOX0 else "fox"


def block_order(kind):
    return WINDOW_ORDER if kind == "swa" else CAUSAL_ORDER


def item_slot(h):
    return h % 2 if h < MLA_H else h // 2 % 2


def staged_count(h):
    return 2 * (h + 1) if h < MLA_H else 2 * (MLA_H + (h - MLA_H) // 2 + 1)


def swa_head(h):
    j = (h - MLA_H) // 2
    return j + 4 * (h % 2)


def out_tile(h):
    return h // 2 if h < FOX0 else (h - FOX0) // 2


class Order:

    def __init__(self, engine, sem):
        self.engine, self.sem, self.n, self.extra = engine, sem, 0, 0

    def __call__(self, instruction):
        self.n += 1
        instruction.then_inc(self.sem, 1)
        self.engine.wait_ge(self.sem, self.n + self.extra)

    def stand(self):
        self.n += 1
        self.engine.sem_inc(self.sem, 1)


def over_chunks(engine, a, b, body):
    n = (b - a) // RAW
    if n > 1:
        with engine.Fori(0, n) as i:
            for j in range(a, a + RAW):
                body(i, j)
    elif n:
        for j in range(a, a + RAW):
            body(0, j)
    for j in range(a + n * RAW, b):
        body(0, j)


def program(nc, d, out, stop=None):
    ctx = ExitStack()
    with ctx:
        def sb(name, shape, dt=F32, at=ctx):
            return at.enter_context(nc.sbuf_tensor(name, shape, dt))

        def sem(name):
            return ctx.enter_context(nc.semaphore(name))

        X = sb("X", [P, T, D])
        XTH = sb("XTH", [P, KD, S], F32R)
        XTL = sb("XTL", [P, KD, S], F32R)
        RW = sb("RW", [P, RAW, CHUNK])
        WH = sb("WH", [P, WS, CHUNK], F32R)
        WL = sb("WL", [P, WS, CHUNK], F32R)
        IDENT = sb("IDENT", [P, P])
        MASKROW = sb("MASKROW", [P, S])
        CHUNKTRI = sb("CHUNKTRI", [P, P])
        IDENT_R = sb("IDENT_R", [P, P], F32R)
        TRI_R = sb("TRI_R", [P, P], F32R)
        CHUNKTRI_R = sb("CHUNKTRI_R", [P, P], F32R)
        EPS = sb("EPS", [P, 2])
        ONE = sb("ONE", [P, 1])
        MV = sb("MV", [P, T, 2])
        BNS = sb("BNS", [P, T, 12])
        STD = sb("STD", [P, T])
        RSTD = sb("RSTD", [P, T])
        NMR = sb("NMR", [P, T])
        MN = sb("MN", [P, 2, T])
        SM = sb("SM", [P, 2, T])
        ES = sb("ES", [P, T])
        NB = sb("NB", [P, 2, T])
        PS = ctx.enter_context(nc.psum_tensor("PS", [P, 8, S], F32))
        PSF = PS[:, :, :].rearrange("p b n -> p (b n)")
        TRI = MASKROW[:, S - P:S]

        prepare = ExitStack()
        XS = sb("XS", [P, KD, S], at=prepare)
        CQ = sb("CQ", [P, T, Q_LORA + KV_LORA], at=prepare)
        CTH = sb("CTH", [P, 5, S], F32R, at=prepare)
        CTL = sb("CTL", [P, 5, S], F32R, at=prepare)
        ROT = sb("ROT", [P, 4, S], at=prepare)
        ONEHOT = sb("ONEHOT", [BUCKETS + 1, 3 * P], at=prepare)
        REL = sb("REL", [BUCKETS + 1, SWA_H], at=prepare)
        prepare.close()
        attend = ExitStack()
        AQH = sb("AQH", [P, 2, S], F32R, at=attend)
        AQL = sb("AQL", [P, 2, S], F32R, at=attend)
        AKH = sb("AKH", [P, 2, S], F32R, at=attend)
        AKL = sb("AKL", [P, 2, S], F32R, at=attend)
        AVH = sb("AVH", [P, 2, T, P], F32R, at=attend)
        AVL = sb("AVL", [P, 2, T, P], F32R, at=attend)
        PB = sb("PB", [P, 2, 1280], at=attend)
        PTH = sb("PTH", [P, 2, 1280], F32R, at=attend)
        PTL = sb("PTL", [P, 2, 1280], F32R, at=attend)
        BC = sb("BC", [P, 2, S], at=attend)
        first = ExitStack()
        QM = sb("QM", [P, MLA_H, S], at=first)
        KM = sb("KM", [P, MLA_H, S], at=first)
        VM = sb("VM", [P, T, 512], at=first)
        QS = sb("QS", [P, T, S], at=first)
        KS = sb("KS", [P, S], at=first)
        VS = sb("VS", [P, T, P], at=first)
        BIAS = sb("BIAS", [P, SWA_H, 2 * P], at=first)
        ROPET = sb("ROPET", [P, S], at=first)
        GAIN = sb("GAIN", [P, 5], at=first)
        SINK = sb("SINK", [P, SWA_H], at=first)
        NSINK = sb("NSINK", [P, SWA_H], at=first)
        CMV = sb("CMV", [P, 8, 2], at=first)
        CBN = sb("CBN", [P, 8, 6], at=first)
        CSTD = sb("CSTD", [P, 8], at=first)
        CRS = sb("CRS", [P, 8], at=first)
        first.close()
        second = ExitStack()
        QF = sb("QF", [P, KD, S], at=second)
        KF = sb("KF", [P, KD, S], at=second)
        VF = sb("VF", [P, T, D], at=second)
        STEPS = sb("STEPS", [P, 7 * P], at=second)
        SWR = sb("SWR", [P, KD, RANK], at=second)
        SWH = sb("SWH", [P, KD, RANK], F32R, at=second)
        SWL = sb("SWL", [P, KD, RANK], F32R, at=second)
        BF = sb("BF", [P, RANK], at=second)
        LZ = sb("LZ", [P, T * RANK], at=second)
        LA = sb("LA", [P, T * RANK], at=second)
        LF = sb("LF", [P, T * RANK], at=second)
        CC_ROWS = sb("CC_ROWS", [RANK, S], at=second)
        CTOK = sb("CTOK", [P, T, RANK], at=second)
        second.close()
        attend.close()
        dense = ExitStack()
        G = sb("G", [P, 2, D], at=dense)
        BG = sb("BG", [P, D], at=dense)
        Y = sb("Y", [P, 2, D], at=dense)
        HT = sb("HT", [P, HT_TILES, S], at=dense)
        HSH = sb("HSH", [P, 2, S], F32R, at=dense)
        HSL = sb("HSL", [P, 2, S], F32R, at=dense)
        GT = sb("GT", [P, 2, S], at=dense)
        dense.close()
        embed = ExitStack()
        _keep = sb("KEEP_DENSE", [P, 5, D], at=embed)
        SG = sb("SG", [P, T, S], at=embed)
        ER = sb("ER", [P, PLE_K, S], at=embed)
        EH = sb("EH", [P, PLE_K, S], F32R, at=embed)
        EL = sb("EL", [P, PLE_K, S], F32R, at=embed)
        embed.close()
        third = ExitStack()
        QG = sb("QG", [P, 2, S], at=third)
        KG = sb("KG", [P, 2, S], at=third)
        VH = sb("VH", [P, T, 512], F32R, at=third)
        VL = sb("VL", [P, T, 512], F32R, at=third)
        GG = sb("GG", [P, T, 512], at=third)
        CB = sb("CB", [P, T, S], at=third)
        CW = sb("CW", [P, T, 3], at=third)
        U = sb("U", [P, T, S + 2], at=third)
        CV = sb("CV", [P, T, S], at=third)
        TWR = sb("TWR", [P, KD, RANK], at=third)
        TWH = sb("TWH", [P, KD, RANK], F32R, at=third)
        TWL = sb("TWL", [P, KD, RANK], F32R, at=third)
        PA = sb("PA", [P, T, RANK], at=third)
        PAT = sb("PAT", [32, S], at=third)
        WG = sb("WG", [RANK + 1, 2 * P], at=third)
        GL = sb("GL", [P, T, 2 * P], at=third)
        GA = sb("GA", [P, T, 2 * P], at=third)
        GLH = sb("GLH", [P, T, 2 * P], F32R, at=third)
        GLL = sb("GLL", [P, T, 2 * P], F32R, at=third)
        BT = sb("BT", [P, 2, S], at=third)
        QI = sb("QI", [P, 2, S], at=third)
        KI = sb("KI", [P, 2, S], at=third)
        KK = sb("KK", [P, 2, S], at=third)
        QIH = sb("QIH", [P, 2, P], F32R, at=third)
        QIL = sb("QIL", [P, 2, P], F32R, at=third)
        QEH = sb("QEH", [P, 2, 2, P], F32R, at=third)
        QEL = sb("QEL", [P, 2, 2, P], F32R, at=third)
        KIH = sb("KIH", [P, 2, P], F32R, at=third)
        KIL = sb("KIL", [P, 2, P], F32R, at=third)
        SMF = sb("SMF", [P, 512], at=third)
        SMH = sb("SMH", [P, 512], F32R, at=third)
        SML = sb("SML", [P, 512], F32R, at=third)
        KTH = sb("KTH", [P, 2 * P], F32R, at=third)
        KTL = sb("KTL", [P, 2 * P], F32R, at=third)
        DEC = sb("DEC", [P, 2, NCH], at=third)
        ST = sb("ST", [P, 2, 2 * DV], at=third)
        STH = sb("STH", [P, 2, 2, 2 * DV], F32R, at=third)
        STL = sb("STL", [P, 2, 2, 2 * DV], F32R, at=third)
        GN = sb("GN", [P, DV], at=third)
        OBN = sb("OBN", [P, 16, 6], at=third)
        OMV = sb("OMV", [P, 16, 2], at=third)
        OSTD = sb("OSTD", [P, 16], at=third)
        ORS = sb("ORS", [P, 16], at=third)
        third.close()

        landed = [sem(f"raw_landed{j}") for j in range(RAW)]
        hi_split = sem("hi_split")
        lo_split = sem("lo_split")
        chunk_used = sem("chunk_used")
        const_landed = sem("const_landed")
        vec_landed = sem("vec_landed")
        gate_landed = sem("gate_landed")
        bias_out = sem("bias_out")
        bias_stored = sem("bias_stored")
        bias_landed = sem("bias_landed")
        consts_made = sem("consts_made")
        xt_hi = sem("xt_hi")
        xt_lo = sem("xt_lo")
        proj = sem("projected")
        evac = sem("evacuated")
        lat_sq = sem("latent_squares")
        lat_std = sem("latent_std")
        lat_normed = sem("latent_normed")
        lat_turned = sem("latent_turned")
        lat_hi = sem("latent_hi")
        lat_lo = sem("latent_lo")
        staged = sem("staged")
        vstaged = sem("values_staged")
        scored = sem("scored")
        masked = sem("masked")
        sunk = sem("sinks_exp")
        expd = sem("exponentials")
        normed = sem("normalised")
        turned = sem("probs_turned")
        pt_hi = sem("probs_hi")
        pt_lo = sem("probs_lo")
        o_ready = sem("head_out")
        o_hi = sem("head_out_hi")
        o_lo = sem("head_out_lo")
        bc_landed = [sem(f"bc_landed{j}") for j in range(2)]
        gates_logit = sem("fgate_logits")
        gates_ln = sem("fgate_ln")
        gates_z = sem("fgate_z")
        gates_log = sem("fgate_log")
        gates_sum = sem("fgate_sums")
        gates_rows = sem("fgate_rows")
        rows_stored = sem("fgate_rows_stored")
        fox_landed = sem("fgate_weights_landed")
        tile_done = sem("tile_done")
        var_ready = sem("var_ready")
        std_ready = sem("std_ready")
        scale_ready = sem("scale_ready")
        centred = sem("centred")
        y_ready = sem("y_ready")
        x_turned = sem("x_turned")
        gated = sem("gated")
        relued = sem("hidden_out")
        hs_ready = sem("hidden_ready")
        emb_ready = sem("emb_ready")
        emb_z = sem("emb_z")
        emb_sig = sem("emb_sig")
        emb_x = sem("emb_x")
        gla_const = sem("gla_landed")
        gla_small = sem("gla_small")
        gla_prep = sem("gla_prep")
        gla_act = sem("gla_act")
        gla_pe = sem("gla_pe")
        gla_ve = sem("gla_ve")
        conv_hi = sem("conv_hi")
        conv_lo = sem("conv_lo")
        out_stored = sem("out_stored")
        act_own = sem("act_own")
        ve_own = sem("ve_own")
        pool_own = sem("pool_own")

        block = ctx.enter_context(nc.Block())
        boundaries = 8 if stop is None else stop + 1

        BOUND = [(True, "layer", 0), (True, "layer", 1), (False, None, None), (True, "layer", 2),
                 (True, "layer", 3), (False, "rms", 4), (True, "rms", 5), (True, "rms", 6)]
        NORMS = [b for b in range(8) if BOUND[b][1]]

        def fox_heads(engine, body):
            for h in (FOX0, FOX0 + 1):
                body(h, 0)
            with engine.Fori(0, 3) as r:
                for h in range(FOX0 + 2, FOX0 + 6):
                    body(h, r)
            for h in (FOX0 + 14, FOX0 + 15):
                body(h, 0)

        @block.sync
        def _(sp):
            def load(i, j):
                if j >= RAW:
                    sp.wait_ge(lo_split, j - RAW + 1 + RAW * i)
                sp.dma_start(RW[:, j % RAW, :], d["stream"][RAW * i + j]).then_inc(landed[j % RAW], 16)

            for j in range(RAW):
                load(0, j)
            ends = [FIRST["out0"], FIRST["up0"], FIRST["ple0"], FIRST["fox"], FIRST["up1"], FIRST["ple1"],
                    FIRST["gla"], FIRST["ffn"], CHUNKS]
            last = ends[boundaries] if boundaries < 8 else CHUNKS
            cut = FIRST["out1"] + RAW
            over_chunks(sp, RAW, min(cut, last), load)
            if boundaries > 3:
                def load_row(h, r):
                    if h == FOX0:
                        sp.wait_ge(rows_stored, 16)
                    if h >= FOX0 + 2:
                        sp.wait_ge(masked, 4 * (h - 1) + 16 * r)
                    src = d["gate_rows"][bass.ds(h - FOX0 + 4 * r, 1), :].to_broadcast([P, S])
                    sp.dma_start(BC[:, h % 2, :], src).then_inc(bc_landed[h % 2], 16)

                fox_heads(sp, load_row)
                over_chunks(sp, cut, last, load)
            if boundaries == 8:
                for t in range(T):
                    sp.wait_ge(y_ready, 28 + t + 1)
                    sp.dma_start(out[:, t, :], X[:, t, :]).then_inc(out_stored, 16)
                sp.wait_ge(out_stored, 16 * T)
            if stop is not None:
                if boundaries in (2, 5):
                    sp.wait_ge(gate_landed, 32 if boundaries == 2 else 64)
                sp.wait_ge(y_ready, 4 * boundaries)
                sp.wait_ge(centred, 4 * sum(b < boundaries for b in NORMS))
                sp.dma_start(out, X[:, :, :]).then_inc(out_stored, 16)
                sp.wait_ge(out_stored, 16)

        @block.gpsimd
        def _(pool):
            own = Order(pool, pool_own)

            def cut(i, j):
                pool.wait_ge(landed[j % RAW], 16 * (j // RAW + 1) + 16 * i)
                if j >= WS:
                    pool.wait_ge(chunk_used, j - WS + 1 + RAW * i)
                pool.sem_inc(hi_split, 1)
                pool.tensor_scalar(WH[:, j % WS, :], RW[:, j % RAW, :], 1.0, 1.0,
                                   ALU.mult, ALU.mult).then_inc(hi_split, 1)
                pool.wait_ge(hi_split, 2 * (j + 1) + 2 * RAW * i)
                pool.tensor_tensor(WL[:, j % WS, :], RW[:, j % RAW, :], WH[:, j % WS, :].bitcast(F32),
                                   ALU.subtract).then_inc(lo_split, 1)

            def stage(hi, lo, src, done):
                own(pool.tensor_scalar(hi, src, 1.0, 1.0, ALU.mult, ALU.mult))
                pool.tensor_tensor(lo, src, hi.bitcast(F32), ALU.subtract).then_inc(done, 1)

            def stage_looped(hi, lo, src, done):
                own.stand()
                own(pool.tensor_tensor(hi, src, ONE[:, 0:1].to_broadcast([P, S]), ALU.mult))
                own.stand()
                pool.tensor_tensor(lo, src, hi.bitcast(F32), ALU.subtract).then_inc(done, 1)

            def stage_mla(h):
                s = h % 2
                stage(AQH[0:96, s, :], AQL[0:96, s, :], QM[0:96, h, :], staged)
                stage(AKH[0:96, s, :], AKL[0:96, s, :], KM[0:96, h, :], staged)

            def stage_pair(s, q, k):
                stage(AQH[:, s, :], AQL[:, s, :], q, staged)
                stage(AKH[:, s, :], AKL[:, s, :], k, staged)

            def stage_values(s, v):
                stage(AVH[:, s, :, :], AVL[:, s, :, :], v, vstaged)

            own(pool.memset(ONE[:, :], 1.0))
            for j in range(RAW):
                cut(0, j)
            over_chunks(pool, RAW, FIRST["out0"] + WS - 1, cut)
            pool.wait_ge(evac, E_FIRST)
            pool.wait_ge(chunk_used, FIRST["out0"])
            stage_mla(0)
            stage_values(0, VM[:, :, 0:P])
            stage_mla(1)
            for h in range(16):
                if h % 2 == 0 and h >= 6 and h < 14:
                    pool.wait_ge(scored, 4 * (h + 1) if h == 6 else 4 * h)
                    stage_pair(h // 2 % 2 ^ 1, QS[:, (h - 6) // 2, :], KS[:, :])
                elif h < 6:
                    pool.wait_ge(scored, 4 * (h + 1))
                    stage_mla(h + 2)
                if h % 2 == 1 and h < 15:
                    if h >= 3:
                        pool.wait_ge(o_ready, h - 1)
                    p = (h + 1) // 2
                    stage_values(p % 2, VM[:, :, p * P:(p + 1) * P] if p < 4 else VS[:, :, :])
            if boundaries <= 3:
                over_chunks(pool, FIRST["out0"] + WS - 1,
                            [0, FIRST["up0"], FIRST["ple0"], FIRST["fox"]][boundaries], cut)
                return
            over_chunks(pool, FIRST["out0"] + WS - 1, FIRST["out1"] + WS - 1, cut)
            pool.wait_ge(evac, E_FOX)
            stage_pair(0, QF[:, 0, :], KF[:, 0, :])
            stage_values(0, VF[:, :, 0:P])

            def fox_stage(h, r):
                if h % 2 == 0 and h < FOX0 + 14:
                    n = (h + 2 - FOX0) // 2
                    if h > FOX0:
                        pool.wait_ge(scored, 4 * h + 16 * r)
                    s = n % 2
                    stage_looped(AQH[:, s, :], AQL[:, s, :], QF[:, n + 2 * r, :], staged)
                    stage_looped(AKH[:, s, :], AKL[:, s, :], KF[:, n + 2 * r, :], staged)
                if h % 2 == 1 and h < FOX0 + 14:
                    if h >= FOX0 + 3:
                        pool.wait_ge(o_ready, h - 1 + 4 * r)
                    n = (h + 1 - FOX0) // 2
                    s, v = n % 2, VF[:, :, bass.ds(n * P + 2 * P * r, P)]
                    own.stand()
                    own(pool.tensor_tensor(AVH[:, s, :, :], v, ONE[:, 0:1].unsqueeze(1).to_broadcast([P, T, P]), ALU.mult))
                    own.stand()
                    pool.tensor_tensor(AVL[:, s, :, :], v, AVH[:, s, :, :].bitcast(F32), ALU.subtract).then_inc(vstaged, 1)

            for h in (FOX0, FOX0 + 1):
                fox_stage(h, 0)
            n1 = own.n
            with pool.Fori(0, 3) as r:
                own.extra = 18 * r
                for h in range(FOX0 + 2, FOX0 + 6):
                    fox_stage(h, r)
            own.extra = 0
            assert own.n == n1 + 18
            own.n += 36
            for h in (FOX0 + 14, FOX0 + 15):
                fox_stage(h, 0)
            last = [FIRST["up1"], FIRST["ple1"], FIRST["gla"], FIRST["ffn"], CHUNKS][boundaries - 4]
            over_chunks(pool, FIRST["out1"] + WS - 1, last, cut)

        @block.tensor
        def _(pe):
            def mm(o, a, b, start, stop):
                return pe.matmul(o, a, b, start=start, stop=stop)

            def mm3(o, ah, al, bh, bl, start, stop):
                mm(o, ah, bh, start, False)
                mm(o, ah, bl, False, False)
                return mm(o, al, bh, False, stop)

            def chunk(c, r=0, ready=True):
                if ready:
                    pe.wait_ge(lo_split, c + 1 + r)

            def features(c, bank, r=0, columns=(0, 128, 256, 384), k_tiles=KD):
                for k in range(k_tiles):
                    cc, u = c + k // 2, UNIT * (k % 2)
                    if k % 2 == 0:
                        chunk(cc, r)
                    for m, col in enumerate(columns):
                        w = slice(u + col, u + col + P)
                        x = mm3(PS[:, bank + m, :], WH[:, cc % WS, w], WL[:, cc % WS, w],
                                XTH[:, k, :], XTL[:, k, :], k == 0, k == k_tiles - 1)
                    if k % 2:
                        x.then_inc(chunk_used, 1)

            def tokens(c, bank, h=XTH, l=XTL, k_tiles=KD):
                for k in range(k_tiles):
                    cc, u = c + k // 2, UNIT * (k % 2)
                    if k % 2 == 0:
                        chunk(cc)
                    for t in range(T):
                        ts = slice(t * P, (t + 1) * P)
                        w = slice(u, u + UNIT)
                        x = mm3(PS[:, bank + t, :], h[:, k, ts], l[:, k, ts],
                                WH[:, cc % WS, w], WL[:, cc % WS, w], k == 0, k == k_tiles - 1)
                    if k % 2:
                        x.then_inc(chunk_used, 1)

            def wide(c, r, h, l, first, last):
                chunk(c, r)
                for t in range(T):
                    ts = slice(t * P, (t + 1) * P)
                    for n in range(2):
                        w = slice(UNIT * n, UNIT * (n + 1))
                        x = mm3(PS[:, 2 * t + n, :], h[:, ts], l[:, ts],
                                WH[:, c % WS, w], WL[:, c % WS, w], first, last)
                    if last and t < T - 1:
                        x.then_inc(tile_done, 1)
                x.then_inc(chunk_used, 1)

            def outward(c):
                for k in range(KD):
                    wide(c + k, 0, XTH[:, k, :], XTL[:, k, :], k == 0, k == KD - 1)

            def input_ready(n):
                pe.wait_ge(xt_hi, 4 * n)
                pe.wait_ge(xt_lo, 4 * n)

            def qk(h, r):
                kind, s = kind_of(h), item_slot(h)
                pe.wait_ge(staged, staged_count(h) + (4 * r if h >= FOX0 else 0))
                if h:
                    pe.wait_ge(masked, 4 * h + 16 * r)
                a = 0 if kind == "mla" else HD * (h % 2)
                rows = slice(a, a + (96 if kind == "mla" else HD))
                for i, _ in block_order(kind):
                    k0 = max(0, i - 1) * P if kind == "swa" else 0
                    n = (i + 1) * P - k0
                    bank, col = (WINDOW_S if kind == "swa" else CAUSAL_S)[i]
                    q = slice(i * P, (i + 1) * P)
                    o = PS[:, bank, col:col + n]
                    x = mm3(o, AQH[rows, s, q], AQL[rows, s, q], AKH[rows, s, k0:k0 + n],
                            AKL[rows, s, k0:k0 + n], True, kind != "fox")
                    if kind == "fox":
                        x = mm(PS[:, bank, col + n - P:col + n], IDENT_R[:, :], TRI_R[:, :], False, True)
                    x.then_inc(scored, 1)

            def turn(h, r):
                window = kind_of(h) == "swa"
                pe.wait_ge(normed, h + 1 + 4 * r)
                if h:
                    pe.wait_ge(pt_lo, h + 4 * r)
                at, to = (WINDOW_AT, WINDOW_T) if window else (CAUSAL_AT, CAUSAL_T)
                for i in range(T):
                    k0 = max(0, i - 1) if window else 0
                    for kb in range(k0, i + 1):
                        o = 3 * S + to[kb] + P * (i - kb)
                        p = at[i] + P * (kb - k0)
                        x = pe.transpose(PSF[:, o:o + P], PB[:, h % 2, p:p + P], IDENT[:, :])
                x.then_inc(turned, 1)

            def pv(h, r):
                window = kind_of(h) == "swa"
                s, v, bank = h % 2, h // 2 % 2, 6 + h % 2
                pe.wait_ge(pt_lo, h + 1 + 4 * r)
                pe.wait_ge(vstaged, h // 2 + 1 + 2 * r)
                if h >= 2:
                    pe.wait_ge(o_lo, h - 1 + 4 * r)
                if window:
                    for i in range(T):
                        for kb in range(max(0, i - 1), i + 1):
                            p = slice(WINDOW_T[kb] + P * (i - kb), WINDOW_T[kb] + P * (i - kb + 1))
                            x = mm3(PS[:, bank, i * P:(i + 1) * P], AVH[:, v, kb, :], AVL[:, v, kb, :],
                                    PTH[:, s, p], PTL[:, s, p], kb == max(0, i - 1), kb == i)
                else:
                    for kb in range(T):
                        n = S - kb * P
                        p = slice(CAUSAL_T[kb], CAUSAL_T[kb] + n)
                        x = mm3(PS[:, bank, kb * P:S], AVH[:, v, kb, :], AVL[:, v, kb, :],
                                PTH[:, s, p], PTL[:, s, p], kb == 0, kb == T - 1)
                x.then_inc(o_ready, 1)

            def attend_step(h, r, last):
                if h < last:
                    qk(h + 1, r)
                turn(h, r)
                if h not in (0, FOX0):
                    pv(h - 1, r)
                if h == last:
                    pv(h, r)

            def boundary(b):
                for t in range(T):
                    pe.wait_ge(y_ready, 4 * b + t + 1)
                    src = Y[:, t % 2, :] if BOUND[b][1] == "rms" else X[:, t, :]
                    for k in range(KD):
                        x = pe.transpose(PS[:, 2 * t + k // 4, P * (k % 4):P * (k % 4 + 1)],
                                         src[:, k * P:(k + 1) * P], IDENT[:, :])
                    x.then_inc(x_turned, 1)

            def hidden(c, groups, g0):
                def one(g, r):
                    if g >= 2:
                        pe.wait_ge(relued, g0 + g - 1 + 2 * r)
                    features(c + 4 * g, 4 * (g % 2), 8 * r)

                n = 2 + groups % 2
                for g in range(n):
                    one(g, 0)
                with pe.Fori(0, (groups - n) // 2) as r:
                    one(n, r)
                    one(n + 1, r)

            def down(c, k_tiles, g_done, k0):
                pe.wait_ge(relued, g_done)

                def one(k, r, first, last):
                    pe.wait_ge(hs_ready, k0 + k + 1 + 4 * r)
                    wide(c + k, 4 * r, HSH[:, k % 2, :], HSL[:, k % 2, :], first, last)

                for k in range(4):
                    one(k, 0, k == 0, False)
                n = (k_tiles - 8) // 4
                with pe.Fori(0, n) as r:
                    for k in range(4, 8):
                        one(k, r, False, False)
                for k in range(4 + 4 * n, k_tiles):
                    one(k, 0, False, k == k_tiles - 1)

            def embedding(c, layer):
                tokens(c, 0)
                pe.wait_ge(emb_ready, layer + 1)
                tokens(c + 4, 4, EH, EL, PLE_K)
                pe.wait_ge(emb_z, 2 * layer + 1)
                tokens(c + 5, 0)
                pe.wait_ge(emb_x, 2 * layer + 1)
                tokens(c + 9, 4, EH, EL, PLE_K)

            pe.wait_ge(const_landed, CONST_ALL)
            pe.wait_ge(consts_made, 1)
            for h in range(SWA_H):
                x = mm(PS[:, h, 0:3 * P], REL[:, h:h + 1].to_broadcast([BUCKETS + 1, P]), ONEHOT[:, :], True, True)
            x.then_inc(proj, 1)
            pe.wait_ge(bias_out, 1)
            input_ready(1)
            features(FIRST["qs"], 0)
            pe.wait_ge(evac, 1)
            c = FIRST["cq"]
            for k in range(KD):
                cc, u = c + k // 2, UNIT * (k % 2)
                if k % 2 == 0:
                    chunk(cc)
                for t in range(T):
                    ts = slice(t * P, (t + 1) * P)
                    mm3(PS[:, 4 + t, 0:Q_LORA], XTH[:, k, ts], XTL[:, k, ts],
                        WH[:, cc % WS, u:u + Q_LORA], WL[:, cc % WS, u:u + Q_LORA], k == 0, k == KD - 1)
                w = slice(u + Q_LORA, u + UNIT)
                x = mm3(PS[:, 0, :], WH[:, cc % WS, w], WL[:, cc % WS, w], XTH[:, k, :], XTL[:, k, :],
                        k == 0, k == KD - 1)
                if k % 2:
                    x.then_inc(chunk_used, 1)
            pe.wait_ge(evac, 2)
            c = FIRST["ckv"]
            for k in range(KD):
                cc, u = c + k // 2, UNIT * (k % 2)
                if k % 2 == 0:
                    chunk(cc)
                for t in range(T):
                    ts = slice(t * P, (t + 1) * P)
                    mm3(PS[:, 1 + t, 0:384], XTH[:, k, ts], XTL[:, k, ts],
                        WH[:, cc % WS, u:u + 384], WL[:, cc % WS, u:u + 384], k == 0, k == KD - 1)
                w = slice(u + 320, u + 448)
                x = mm3(PS[:, 5, :], WH[:, cc % WS, w], WL[:, cc % WS, w], XTH[:, k, :], XTL[:, k, :],
                        k == 0, k == KD - 1)
                if k % 2:
                    x.then_inc(chunk_used, 1)
            pe.wait_ge(evac, 3)
            pe.wait_ge(lat_normed, 1)
            for f in range(5):
                for t in range(T):
                    x = pe.transpose(PS[:, f, t * P:(t + 1) * P], CQ[:, t, f * P:(f + 1) * P], IDENT[:, :])
                x.then_inc(lat_turned, 1)
            pe.wait_ge(lat_lo, 5)
            for n in range(6):
                half, k = n // 3, n % 3
                cc, u = FIRST["uq"] + n // 2, UNIT * (n % 2)
                if n % 2 == 0:
                    chunk(cc)
                for m in range(4):
                    w = slice(u + P * m, u + P * (m + 1))
                    x = mm3(PS[:, 4 * half + m, :], WH[:, cc % WS, w], WL[:, cc % WS, w],
                            CTH[:, k, :], CTL[:, k, :], k == 0, k == 2)
                if n % 2:
                    x.then_inc(chunk_used, 1)
            pe.wait_ge(evac, 4)
            chunk(FIRST["kn"])
            for k in range(2):
                for m in range(4):
                    w = slice(UNIT * k + P * m, UNIT * k + P * (m + 1))
                    x = mm3(PS[:, m, :], WH[:, FIRST["kn"] % WS, w], WL[:, FIRST["kn"] % WS, w],
                            CTH[:, 3 + k, :], CTL[:, 3 + k, :], k == 0, k == 1)
            x.then_inc(chunk_used, 1)
            pe.wait_ge(evac, 5)
            tokens(FIRST["vm"], 4, CTH[:, 3:5, :], CTL[:, 3:5, :], 2)

            pe.wait_ge(evac, E_FIRST)
            qk(0, 0)
            for h in range(16):
                attend_step(h, 0, 15)

            def block_end(b, name_out, name_up, name_down, groups, g0, k_tiles, k0):
                outward(FIRST[name_out])
                boundary(b)
                if boundaries == b + 1:
                    return
                input_ready(b + 2)
                hidden(FIRST[name_up], groups, g0)
                down(FIRST[name_down], k_tiles, g0 + groups, k0)

            pe.wait_ge(o_lo, 16)
            pe.wait_ge(o_hi, 16)
            block_end(0, "out0", "up0", "down0", 8, 0, 32, 0)
            if boundaries <= 1:
                return
            boundary(1)
            if boundaries <= 2:
                return
            input_ready(3)
            embedding(FIRST["ple0"], 0)
            boundary(2)
            if boundaries <= 3:
                return

            input_ready(4)
            chunk0 = FIRST["fox"]
            pe.wait_ge(gates_z, 1)
            for t in range(T):
                for k in range(KD):
                    ts = slice(t * P, (t + 1) * P)
                    x = mm3(PS[:, 4, RANK * t:RANK * (t + 1)], XTH[:, k, ts], XTL[:, k, ts],
                            SWH[:, k, :], SWL[:, k, :], k == 0, k == KD - 1)
            x.then_inc(gates_logit, 1)
            features(chunk0, 0)
            pe.wait_ge(gates_z, 2)
            features(chunk0 + 4, 4)
            pe.wait_ge(evac, 8)
            features(chunk0 + 8, 0)
            pe.wait_ge(evac, 9)
            pe.wait_ge(gates_log, 1)
            for t in range(T):
                mm(PS[0:RANK, 4, :], LF[:, RANK * t:RANK * (t + 1)],
                   STEPS[:, 3 * P - t * P:3 * P - t * P + S], t == 0, t == T - 1)
            for u in range(T):
                for t in range(u + 1):
                    x = mm(PS[:, 5, RANK * u:RANK * (u + 1)], STEPS[:, 3 * P + (u - t) * P:3 * P + (u - t + 1) * P],
                           LF[:, RANK * t:RANK * (t + 1)], t == 0, t == u)
            x.then_inc(gates_sum, 1)
            pe.wait_ge(gates_rows, 2)
            features(chunk0 + 12, 4)
            pe.wait_ge(evac, 10)
            tokens(chunk0 + 16, 0)
            pe.wait_ge(evac, 11)
            tokens(chunk0 + 20, 4)

            pe.wait_ge(evac, E_FOX)
            qk(FOX0, 0)
            for h in (FOX0, FOX0 + 1):
                attend_step(h, 0, FOX0 + 15)
            with pe.Fori(0, 3) as r:
                for h in range(FOX0 + 2, FOX0 + 6):
                    attend_step(h, r, FOX0 + 15)
            for h in (FOX0 + 14, FOX0 + 15):
                attend_step(h, 0, FOX0 + 15)
            pe.wait_ge(o_lo, 32)
            pe.wait_ge(o_hi, 32)
            block_end(3, "out1", "up1", "down1", 8, 8, 32, 32)
            if boundaries <= 4:
                return
            boundary(4)
            if boundaries <= 5:
                return
            input_ready(6)
            embedding(FIRST["ple1"], 1)
            boundary(5)
            if boundaries <= 6:
                return
            c = FIRST["gla"]
            input_ready(7)
            pe.wait_ge(gla_prep, 1)
            for t in range(T):
                for k in range(KD):
                    ts = slice(t * P, (t + 1) * P)
                    x = mm3(PS[:, 4, RANK * t:RANK * (t + 1)], XTH[:, k, ts], XTL[:, k, ts],
                            TWH[:, k, :], TWL[:, k, :], k == 0, k == KD - 1)
            x.then_inc(gla_small, 1)
            features(c, 0)
            pe.wait_ge(gla_prep, 2)
            for t in range(T):
                x = pe.transpose(PS[0:RANK, 5, t * P:(t + 1) * P], PA[:, t, :], IDENT[:, :])
            x.then_inc(gla_small, 1)
            pe.wait_ge(gla_prep, 3)
            tokens(c + 4, 4)
            pe.wait_ge(evac, 14)
            for t in range(T):
                x = mm(PSF[:, 2 * P * t:2 * P * (t + 1)], PAT[0:RANK + 1, t * P:(t + 1) * P],
                       WG[:, :], True, True)
            x.then_inc(gla_small, 1)
            pe.wait_ge(gla_prep, 4)
            tokens(c + 8, 0)
            pe.wait_ge(evac, 15)
            pe.wait_ge(gla_prep, 6)
            for f in range(2):
                for t in range(T):
                    o = PS[:, 4 + f, t * P:(t + 1) * P]
                    mm(o, GLH[:, t, f * P:(f + 1) * P], CHUNKTRI_R[:, :], True, False)
                    x = mm(o, GLL[:, t, f * P:(f + 1) * P], CHUNKTRI_R[:, :], False, True)
            x.then_inc(gla_small, 1)
            pe.wait_ge(gla_prep, 7)
            features(c + 12, 4)
            pe.wait_ge(evac, 16)
            features(c + 16, 0)
            pe.wait_ge(evac, 17)
            features(c + 20, 4)
            pe.wait_ge(evac, 19)
            for t in range(T):
                pe.wait_ge(gla_ve, 3 * t + 1)
                for h in range(GLA_H):
                    rows, p = slice(DK * (h % 2), DK * (h % 2 + 1)), h // 2
                    mm3(PS[:, h % 2, P * p:P * (p + 1)], KIH[rows, p, :], KIL[rows, p, :],
                        QIH[rows, p, :], QIL[rows, p, :], True, True)
                for p in range(2):
                    x = pe.transpose(PS[:, 1, P * (p + 2):P * (p + 3)], KK[:, p, t * P:(t + 1) * P], IDENT[:, :])
                x.then_inc(gla_pe, 1)
                pe.wait_ge(gla_ve, 3 * t + 2)
                for e in range(2):
                    rows = slice(GCH * e, GCH * (e + 1))
                    for p in range(2):
                        w = slice(2 * DV * p, 2 * DV * (p + 1))
                        x = mm3(PS[:, 2 + e, w], KTH[rows, P * p:P * (p + 1)], KTL[rows, P * p:P * (p + 1)],
                                VH[rows, t, w], VL[rows, t, w], True, True)
                x.then_inc(gla_pe, 1)
                pe.wait_ge(gla_ve, 3 * t + 3)
                for p in range(2):
                    w = slice(2 * DV * p, 2 * DV * (p + 1))
                    for e in range(2):
                        mm3(PS[:, 4 + t, w], QEH[:, e, p, :], QEL[:, e, p, :],
                            STH[:, e, p, :], STL[:, e, p, :], e == 0, False)
                    for h in (2 * p, 2 * p + 1):
                        w = slice(DV * h, DV * (h + 1))
                        x = mm3(PS[:, 4 + t, w], SMH[:, w], SML[:, w], VH[:, t, w], VL[:, t, w],
                                False, h % 2 == 1)
                x.then_inc(gla_pe, 1)
            pe.wait_ge(gla_ve, 13)
            for f in range(GLA_H):
                for t in range(T):
                    x = pe.transpose(PS[:, f, t * P:(t + 1) * P], CV[:, t, f * P:(f + 1) * P], IDENT[:, :])
            x.then_inc(gla_pe, 1)
            pe.wait_ge(conv_lo, 1)
            pe.wait_ge(gla_ve, 14)
            outward(FIRST["out2"])
            boundary(6)
            if boundaries <= 7:
                return
            input_ready(8)
            hidden(FIRST["ffn"], 11, 16)
            down(FIRST["down2"], 22, 27, 64)

        @block.vector
        def _(ve):
            own = Order(ve, ve_own)
            M, A, SUB, MAX, MIN = ALU.mult, ALU.add, ALU.subtract, ALU.max, ALU.min

            def spread(ap, n, at=1):
                shape = list(ap.shape)
                return ap.unsqueeze(at).to_broadcast(shape[:at] + [n] + shape[at:])

            ve.memset(EPS[:, 0:1], LN_EPS)
            ve.memset(EPS[:, 1:2], RMS_EPS)
            ve.wait_ge(const_landed, CONST_ALL)
            ve.tensor_copy(IDENT_R[:, :], IDENT[:, :])
            ve.tensor_copy(TRI_R[:, :], TRI)
            ve.tensor_copy(CHUNKTRI_R[:, :], CHUNKTRI[:, :])
            ve.tensor_scalar(NSINK[:, :], SINK[:, :], -1.0, None, M).then_inc(consts_made, 1)
            for j in range(4):
                w = slice(2 * j, 2 * j + 2)
                ve.wait_ge(xt_hi, j + 1)
                ve.tensor_tensor(XTL[:, w, :], XS[:, w, :], XTH[:, w, :].bitcast(F32), SUB).then_inc(xt_lo, 1)
            ve.wait_ge(proj, 1)
            ve.tensor_scalar(QM[:, :, 0:3 * P], PS[:, :, 0:3 * P], -1.0, None, M).then_inc(bias_out, 1)

            ve.wait_ge(chunk_used, FIRST["cq"])
            ve.tensor_scalar(QS[:, :, :], PS[:, 0:4, :], -HD ** -0.5, None, M).then_inc(evac, 1)
            ve.wait_ge(chunk_used, FIRST["ckv"])
            ve.tensor_copy(KS[:, :], PS[:, 0, :])
            ve.tensor_copy(CQ[:, :, 0:Q_LORA], PS[:, 4:8, 0:Q_LORA]).then_inc(evac, 1)
            ve.wait_ge(evac, 2)
            for t in range(T):
                ve.bn_stats(CBN[:, t, :], CQ[:, t, 0:Q_LORA])
            ve.wait_ge(chunk_used, FIRST["uq"])
            rope_k, rope_s = ROPET[HD:96, :], ROPET[96:P, :]
            ve.tensor_copy(VS[:, :, :], PS[:, 1:5, KV_LORA:384])
            ve.tensor_tensor(ROT[HD:96, 0, :], PS[HD:96, 5, :], rope_k, M)
            ve.tensor_tensor(ROT[HD:96, 1, :], PS[96:P, 5, :], rope_s, M)
            ve.tensor_copy(CQ[:, :, Q_LORA:], PS[:, 1:5, 0:KV_LORA]).then_inc(evac, 1)
            ve.wait_ge(evac, 3)
            ve.wait_ge(bias_landed, 16)
            ve.tensor_tensor(KM[HD:96, :, :], spread(ROT[HD:96, 0, :], MLA_H), spread(ROT[HD:96, 1, :], MLA_H), A)
            for t in range(T):
                x = ve.bn_stats(CBN[:, T + t, :], CQ[:, t, Q_LORA:])
            own(x)
            for j in range(8):
                x = ve.bn_aggr(CMV[:, j, :], CBN[:, j, :])
            own(x)
            own(ve.tensor_tensor(CMV[:, :, 0], CMV[:, :, 0], CMV[:, :, 0], M))
            ve.tensor_tensor(CMV[:, :, 1], CMV[:, :, 0], CMV[:, :, 1], A).then_inc(lat_sq, 1)
            ve.wait_ge(lat_std, 1)
            own(ve.reciprocal(CRS[:, :], CSTD[:, :]))
            for j in range(8):
                w = slice(0, Q_LORA) if j < T else slice(Q_LORA, Q_LORA + KV_LORA)
                x = ve.tensor_scalar(CQ[:, j % T, w], CQ[:, j % T, w], CRS[:, j:j + 1], None, M)
            x.then_inc(lat_normed, 1)
            for f in range(5):
                ve.wait_ge(lat_hi, f + 1)
                ve.scalar_tensor_tensor(CTL[:, f, :], PS[:, f, :], GAIN[:, f:f + 1],
                                        CTH[:, f, :].bitcast(F32), M, SUB).then_inc(lat_lo, 1)
            for half in range(2):
                ve.wait_ge(chunk_used, FIRST["uq"] + 2 + half)
                b, hs = slice(4 * half, 4 * half + 4), slice(4 * half, 4 * half + 4)
                ve.tensor_scalar(QM[0:HD, hs, :], PS[0:HD, b, :], -MLA_SCALE, None, M)
                ve.scalar_tensor_tensor(ROT[HD:96, :, :], PS[96:P, b, :], -MLA_SCALE, spread(rope_s, 4), M, M)
                own(ve.scalar_tensor_tensor(QM[HD:96, hs, :], PS[HD:96, b, :], -MLA_SCALE, spread(rope_k, 4), M, M))
                ve.tensor_tensor(QM[HD:96, hs, :], QM[HD:96, hs, :], ROT[HD:96, :, :], A).then_inc(evac, 1)
                if half == 0:
                    ve.wait_ge(evac, 4)
            ve.wait_ge(chunk_used, FIRST["vm"])
            for e in range(2):
                x = ve.tensor_copy(KM[0:HD, e::2, :], PS[HD * e:HD * (e + 1), 0:4, :])
            x.then_inc(evac, 1)
            ve.wait_ge(chunk_used, FIRST["out0"])
            ve.tensor_copy(VM[:, :, :], PS[:, 4:8, :]).then_inc(evac, 1)

            def mask(h, r):
                kind, s = kind_of(h), h % 2
                if h >= 2:
                    ve.wait_ge(turned, h - 1 + 4 * r)
                if kind == "fox":
                    ve.wait_ge(bc_landed[s], 16 * ((h - FOX0) // 2 + 1) + 32 * r)
                for i, in_bank in block_order(kind):
                    n = min(i + 1, 2) * P if kind == "swa" else (i + 1) * P
                    at = (WINDOW_AT if kind == "swa" else CAUSAL_AT)[i]
                    bank, col = (WINDOW_S if kind == "swa" else CAUSAL_S)[i]
                    init = 3e38
                    if kind == "mla":
                        other = MASKROW[:, S - n:S]
                    elif kind == "swa":
                        g = swa_head(h)
                        other, init = BIAS[:, g, 2 * P - n:2 * P], NSINK[:, g:g + 1]
                    else:
                        other = BC[:, s, 0:n]
                    ve.wait_ge(scored, 4 * h + in_bank + 16 * r)
                    if kind == "fox":
                        own.stand()
                    x = ve.tensor_tensor_reduce(out=PB[:, s, at:at + n], in0=PS[:, bank, col:col + n],
                                                in1=other, scale=1.0, scalar=init, op0=A, op1=MIN,
                                                accum_out=MN[:, s, i:i + 1])
                    if kind == "fox":
                        own(x)
                        cq = CTOK[:, i, bass.ds(h - FOX0 + 4 * r, 1)]
                        x = ve.scalar_tensor_tensor(NB[:, s, i:i + 1], MN[:, s, i:i + 1], cq, cq, SUB, A)
                    x.then_inc(masked, 1)

            def normalise(h, r):
                kind, s = kind_of(h), h % 2
                ve.wait_ge(expd, 4 * (h + 1) + 16 * r)
                if kind == "swa":
                    ve.wait_ge(sunk, h - 7)
                    own(ve.tensor_tensor(SM[:, s, :], SM[:, s, :], ES[:, :], A))
                own(ve.reciprocal(SM[:, s, :], SM[:, s, :]))
                at = (WINDOW_AT + [896]) if kind == "swa" else (CAUSAL_AT + [1280])
                for i in range(T):
                    p = PB[:, s, at[i]:at[i + 1]]
                    x = ve.tensor_scalar(p, p, SM[:, s, i:i + 1], None, M)
                x.then_inc(normed, 1)

            def probs_lo(h, r):
                n = 896 if kind_of(h) == "swa" else 1280
                ve.wait_ge(pt_hi, h + 1 + 4 * r)
                ve.tensor_tensor(PTL[:, h % 2, 0:n], PSF[:, 3 * S:3 * S + n],
                                 PTH[:, h % 2, 0:n].bitcast(F32), SUB).then_inc(pt_lo, 1)

            def out_lo(h, r):
                rows, tile = slice(HD * (h % 2), HD * (h % 2 + 1)), out_tile(h)
                ve.wait_ge(o_hi, h + 1 + 4 * r)
                ve.tensor_tensor(XTL[rows, tile + 2 * r, :], PS[rows, 6 + h % 2, :],
                                 XTH[rows, tile + 2 * r, :].bitcast(F32), SUB).then_inc(o_lo, 1)

            def attend_step(h, r, last):
                normalise(h, r)
                if h < last:
                    mask(h + 1, r)
                probs_lo(h, r)
                if h not in (0, FOX0):
                    out_lo(h - 1, r)
                if h == last:
                    out_lo(h, r)

            mask(0, 0)
            for h in range(16):
                attend_step(h, 0, 15)

            added = [0]

            def boundary(b, end):
                add, kind, n = BOUND[b]
                layer = kind == "layer"
                vecs = 0 if n is None else 32 * (n + 1) if n < 4 else 128 + 16 * (n - 3)

                def residual(t):
                    if add:
                        if t < T - 1:
                            ve.wait_ge(tile_done, 3 * added[0] + t + 1)
                        else:
                            ve.wait_ge(chunk_used, end)
                        a = ALPHA if layer else 1.0
                        own(ve.scalar_tensor_tensor(X[:, t, :], X[:, t, :], a,
                                                    PSF[:, D * t:D * (t + 1)], M, A))
                    for j in range(2):
                        x = ve.bn_stats(BNS[:, t, 6 * j:6 * j + 6], X[:, t, UNIT * j:UNIT * (j + 1)])
                    own(x)
                    x = ve.bn_aggr(MV[:, t, :], BNS[:, t, :])
                    if not layer:
                        own(x)
                        x = ve.scalar_tensor_tensor(MV[:, t, 1:2], MV[:, t, 0:1], MV[:, t, 0:1],
                                                    MV[:, t, 1:2], M, A)
                    x.then_inc(var_ready, 1)

                def scale(t):
                    ve.wait_ge(std_ready, 4 * n + t + 1)
                    x = ve.reciprocal(RSTD[:, t:t + 1], STD[:, t:t + 1])
                    if layer:
                        own(x)
                        x = ve.tensor_scalar(NMR[:, t:t + 1], MV[:, t, 0:1], RSTD[:, t:t + 1], -1.0, M, M)
                    x.then_inc(scale_ready, 1)

                def affine(t):
                    ve.wait_ge(centred, 4 * n + t + 1)
                    if t == 0:
                        ve.wait_ge(vec_landed, vecs)
                    y = Y[:, t % 2, :] if kind == "rms" and b < 7 else X[:, t, :]
                    x = ve.tensor_tensor(y, y, G[:, 0, :], M)
                    if layer:
                        own(x)
                        x = ve.tensor_tensor(y, y, G[:, 1, :], A)
                    x.then_inc(y_ready, 1)

                for t in range(T + 3):
                    if kind:
                        if t < T:
                            residual(t)
                        if 1 <= t <= T:
                            scale(t - 1)
                        if 2 <= t <= T + 1:
                            affine(t - 2)
                    if t >= 3 and b < 7:
                        low(b, t - 3)
                added[0] += add

            def low(b, t):
                ve.wait_ge(xt_hi, 4 * (b + 1) + t + 1)
                w = slice(t * P, (t + 1) * P)
                src = PSF[:, D * t:D * (t + 1)].rearrange("p (k n) -> p k n", k=KD)
                ve.tensor_tensor(XTL[:, :, w], src, XTH[:, :, w].bitcast(F32), SUB).then_inc(xt_lo, 1)

            def hidden(c, r0):
                with ve.Fori(0, 4) as r:
                    own.extra = 2 * r
                    for g in range(2):
                        ve.wait_ge(chunk_used, c + 4 * (g + 1) + 8 * r)
                        h = HT[:, bass.ds(4 * g + 8 * r, 4), :]
                        ve.tensor_scalar(h, PS[:, 4 * g:4 * g + 4, :], 0.0, None, MAX).then_inc(relued, 1)
                        ve.wait_ge(relued, r0 + g + 1 + 2 * r)
                        own(ve.tensor_tensor(h, h, h, M))
                own.extra = 0
                own.n += 6

            def gated_hidden(c, r0):
                def one(g, bank, r):
                    ve.wait_ge(gated, g + 1 + 2 * r)
                    h = HT[:, bass.ds(2 * g + 4 * r, 2), :]
                    ve.tensor_tensor(h, PS[:, bank + 2:bank + 4, :], GT[:, :, :], M).then_inc(relued, 1)

                one(0, 0, 0)
                with ve.Fori(0, 5) as r:
                    one(1, 4, r)
                    one(2, 0, r)
                ve.wait_ge(relued, r0 + 11)

            def split_hidden(c, k_tiles):
                with ve.Fori(0, k_tiles // 2) as r:
                    own.extra = 2 * r
                    for k in range(2):
                        ve.wait_ge(chunk_used, c + k - 1 + 2 * r)
                        h = HT[:, k + 2 * r, :]
                        own(ve.tensor_copy(HSH[:, k, :], h))
                        ve.tensor_tensor(HSL[:, k, :], h, HSH[:, k, :].bitcast(F32), SUB).then_inc(hs_ready, 1)
                own.extra = 0
                own.n += k_tiles - 2

            def embedding(c, layer):
                ve.wait_ge(gate_landed, 32 * (layer + 1))
                own(ve.tensor_copy(EH[:, :, :], ER[:, :, :]))
                ve.tensor_tensor(EL[:, :, :], ER[:, :, :], EH[:, :, :].bitcast(F32), SUB).then_inc(emb_ready, 1)
                for half in range(2):
                    w = slice(UNIT * half, UNIT * (half + 1))
                    ve.wait_ge(chunk_used, c + 5 * half + 4)
                    ve.tensor_tensor(SG[:, :, :], PS[:, 0:4, :], spread(BG[:, w], T), A).then_inc(emb_z, 1)
                    ve.wait_ge(chunk_used, c + 5 * half + 5)
                    ve.wait_ge(emb_sig, 2 * layer + half + 1)
                    ve.tensor_tensor(SG[:, :, :], SG[:, :, :], PS[:, 4:8, :], M).then_inc(emb_x, 1)
                    ve.wait_ge(emb_x, 2 * layer + half + 1)
                    for t in range(T):
                        x = ve.tensor_tensor(X[:, t, w], X[:, t, w], SG[:, t, :], A)
                        if half and layer == 0:
                            x.then_inc(y_ready, 1)
                    if half == 0 or layer:
                        own(x)
                if layer == 0:
                    ve.wait_ge(y_ready, 12)

            boundary(0, FIRST["up0"])
            if boundaries <= 1:
                return
            hidden(FIRST["up0"], 0)
            split_hidden(FIRST["down0"], 32)
            boundary(1, FIRST["ple0"])
            if boundaries <= 2:
                return
            embedding(FIRST["ple0"], 0)
            boundary(2, 0)
            if boundaries <= 3:
                return

            ve.wait_ge(fox_landed, 48)
            own(ve.tensor_copy(SWH[:, :, :], SWR[:, :, :]))
            ve.tensor_tensor(SWL[:, :, :], SWR[:, :, :], SWH[:, :, :].bitcast(F32), SUB).then_inc(gates_z, 1)
            ve.wait_ge(gates_logit, 1)
            lz = LZ[:, :].rearrange("p (t h) -> p t h", t=T)
            own(ve.tensor_tensor(lz, PS[:, 4, 0:T * RANK].rearrange("p (t h) -> p t h", t=T),
                                 spread(BF[:, :], T), A))
            ve.scalar_tensor_tensor(LA[:, :], LZ[:, :], -1.0, LZ[:, :], M, MAX).then_inc(gates_z, 1)
            ve.wait_ge(gates_ln, 1)
            ve.scalar_tensor_tensor(LF[:, :], LZ[:, :], 0.0, LA[:, :], MIN, SUB).then_inc(gates_log, 1)
            c = FIRST["fox"]
            ve.wait_ge(chunk_used, c + 4)
            ve.tensor_scalar(QF[:, 0:4, :], PS[:, 0:4, :], -HD ** -0.5, None, M).then_inc(evac, 1)
            ve.wait_ge(chunk_used, c + 8)
            ve.tensor_scalar(QF[:, 4:8, :], PS[:, 4:8, :], -HD ** -0.5, None, M).then_inc(evac, 1)
            ve.wait_ge(gates_sum, 1)
            ve.tensor_copy(CC_ROWS[:, :], PS[0:RANK, 4, :]).then_inc(gates_rows, 1)
            ve.tensor_copy(CTOK[:, :, :].rearrange("p t h -> p (t h)"), PS[:, 5, 0:T * RANK]).then_inc(gates_rows, 1)
            ve.wait_ge(chunk_used, c + 12)
            ve.tensor_copy(KF[:, 0:4, :], PS[:, 0:4, :]).then_inc(evac, 1)
            ve.wait_ge(chunk_used, c + 16)
            ve.tensor_copy(KF[:, 4:8, :], PS[:, 4:8, :]).then_inc(evac, 1)
            for n in range(2):
                ve.wait_ge(chunk_used, c + 20 + 4 * n)
                ve.tensor_copy(VF[:, :, UNIT * n:UNIT * (n + 1)], PS[:, 4 * n:4 * n + 4, :]).then_inc(evac, 1)
            mask(FOX0, 0)
            for h in (FOX0, FOX0 + 1):
                attend_step(h, 0, FOX0 + 15)
            n = own.n
            with ve.Fori(0, 3) as r:
                own.extra = 36 * r
                for h in range(FOX0 + 2, FOX0 + 6):
                    attend_step(h, r, FOX0 + 15)
            own.extra = 0
            assert own.n - n == 36
            own.n += 72
            for h in (FOX0 + 14, FOX0 + 15):
                attend_step(h, 0, FOX0 + 15)
            boundary(3, FIRST["up1"])
            if boundaries <= 4:
                return
            hidden(FIRST["up1"], 8)
            split_hidden(FIRST["down1"], 32)
            boundary(4, FIRST["ple1"])
            if boundaries <= 5:
                return
            embedding(FIRST["ple1"], 1)
            boundary(5, 0)
            if boundaries <= 6:
                return

            c = FIRST["gla"]
            ve.wait_ge(x_turned, 24)
            ve.wait_ge(gla_const, 64)
            own(ve.tensor_copy(TWH[:, :, :], TWR[:, :, :]))
            ve.tensor_tensor(TWL[:, :, :], TWR[:, :, :], TWH[:, :, :].bitcast(F32), SUB).then_inc(gla_prep, 1)
            ve.memset(QEH[:, :, :, :].bitcast(F32), 0.0)
            ve.memset(QEL[:, :, :, :].bitcast(F32), 0.0)
            ve.memset(ST[:, :, :], 0.0)
            ve.memset(U[:, :, 0:2], 0.0)
            own(ve.memset(PAT[:, :], 1.0))
            ve.wait_ge(gla_small, 1)
            ve.tensor_copy(PA[:, :, :].rearrange("p t a -> p (t a)"), PS[:, 4, 0:T * RANK]).then_inc(gla_prep, 1)
            ve.wait_ge(gla_small, 2)
            ve.tensor_copy(PAT[0:RANK, :], PS[0:RANK, 5, :]).then_inc(gla_prep, 1)
            ve.wait_ge(chunk_used, c + 4)
            ve.tensor_scalar(QG[:, :, :], PS[:, 0:2, :], DK ** -0.5, None, M)
            ve.tensor_copy(KG[:, :, :], PS[:, 2:4, :]).then_inc(evac, 1)
            ve.wait_ge(gla_small, 3)
            gl = GL[:, :, :].rearrange("p t n -> p (t n)")
            ga = GA[:, :, :].rearrange("p t n -> p (t n)")
            own(ve.tensor_copy(gl, PSF[:, 0:T * 2 * P]))
            x = ve.scalar_tensor_tensor(ga, gl, -1.0, gl, M, MAX)
            x.then_inc(gla_prep, 1)
            ve.wait_ge(chunk_used, c + 8)
            own(ve.tensor_copy(VH[:, :, :], PS[:, 4:8, :]))
            ve.tensor_tensor(VL[:, :, :], PS[:, 4:8, :], VH[:, :, :].bitcast(F32), SUB).then_inc(evac, 1)
            ve.wait_ge(gla_act, 1)
            own(ve.scalar_tensor_tensor(gl, gl, 0.0, ga, MIN, SUB))
            own(ve.tensor_scalar(gl, gl, 1.0 / GATE_NORM, None, M))
            own(ve.tensor_copy(GLH[:, :, :], GL[:, :, :]))
            ve.tensor_tensor(GLL[:, :, :], GL[:, :, :], GLH[:, :, :].bitcast(F32), SUB).then_inc(gla_prep, 2)
            ve.wait_ge(chunk_used, c + 12)
            ve.tensor_copy(GG[:, :, :], PS[:, 0:4, :]).then_inc(evac, 1)
            ve.wait_ge(gla_small, 4)
            own(ve.tensor_copy(BT[:, :, :], PS[:, 4:6, :]))
            by_chunk = lambda v: v.rearrange("p f (n c) -> p f n c", c=GCH)
            ends = by_chunk(BT[:, :, :])[:, :, :, GCH - 1:GCH]
            ve.tensor_tensor(by_chunk(KK[:, :, :]), ends.to_broadcast([P, 2, NCH, GCH]),
                             by_chunk(BT[:, :, :]), SUB).then_inc(gla_prep, 1)
            ve.wait_ge(gla_act, 2)
            ve.tensor_tensor(QI[:, :, :], QI[:, :, :], QG[:, :, :], M)
            ve.tensor_tensor(KI[:, :, :], KI[:, :, :], KG[:, :, :], M)
            own(ve.tensor_tensor(KK[:, :, :], KK[:, :, :], KG[:, :, :], M))
            ve.wait_ge(chunk_used, c + 16)
            ve.tensor_copy(CB[:, :, :], PS[:, 4:8, :]).then_inc(evac, 1)
            ve.wait_ge(chunk_used, c + 20)
            ve.tensor_copy(CV[:, :, :], PS[:, 0:4, :]).then_inc(evac, 1)
            ve.wait_ge(evac, 18)
            ve.wait_ge(chunk_used, c + 24)
            ve.tensor_tensor(U[:, :, 2:S + 2], PS[:, 4:8, :], CV[:, :, :], M).then_inc(evac, 1)

            def tile_operands(t):
                w = slice(t * P, (t + 1) * P)
                if t:
                    ve.wait_ge(gla_pe, 3 * t)
                ve.tensor_copy(KIH[:, :, :], KI[:, :, w])
                own(ve.tensor_copy(QIH[:, :, :], QI[:, :, w]))
                ve.tensor_tensor(KIL[:, :, :], KI[:, :, w], KIH[:, :, :].bitcast(F32), SUB)
                own(ve.tensor_tensor(QIL[:, :, :], QI[:, :, w], QIH[:, :, :].bitcast(F32), SUB))
                for e in range(2):
                    k = slice(GCH * e, GCH * (e + 1))
                    ve.tensor_copy(QEH[:, e, :, k], QIH[:, :, k].bitcast(F32))
                    x = ve.tensor_copy(QEL[:, e, :, k], QIL[:, :, k].bitcast(F32))
                x.then_inc(gla_ve, 1)

            ve.wait_ge(evac, 19)
            tile_operands(0)
            for f in range(T):
                own(ve.tensor_scalar(CV[:, f, :], U[:, f, 0:S], CW[:, f, 0:1], None, M))
                for j in (1, 2):
                    own(ve.scalar_tensor_tensor(CV[:, f, :], U[:, f, j:j + S], CW[:, f, j:j + 1],
                                                CV[:, f, :], M, A))
            ve.tensor_tensor(CV[:, :, :], CV[:, :, :], CB[:, :, :], M).then_inc(gla_prep, 1)
            ve.wait_ge(conv_hi, 1)
            ve.tensor_tensor(XTL[:, 4:8, :], CV[:, :, :], XTH[:, 4:8, :].bitcast(F32), SUB).then_inc(conv_lo, 1)
            for t in range(T):
                if t:
                    tile_operands(t)
                ve.wait_ge(gla_pe, 3 * t + 1)
                causal = CHUNKTRI[:, :].unsqueeze(1).unsqueeze(1).to_broadcast([P, 2, 2, P])
                own(ve.tensor_tensor(SMF[:, :].rearrange("p (i j n) -> p i j n", i=2, j=2),
                                     PS[:, 0:2, 0:2 * P].rearrange("p j (i n) -> p i j n", i=2), causal, M))
                ve.tensor_copy(KTH[:, :], PS[:, 1, 2 * P:4 * P])
                own(ve.tensor_copy(SMH[:, :], SMF[:, :]))
                ve.tensor_tensor(KTL[:, :], PS[:, 1, 2 * P:4 * P], KTH[:, :].bitcast(F32), SUB)
                ve.tensor_tensor(SML[:, :], SMF[:, :], SMH[:, :].bitcast(F32), SUB).then_inc(gla_ve, 1)
                ve.wait_ge(gla_pe, 3 * t + 2)
                for e in range(2):
                    own(ve.tensor_copy(STH[:, e, :, :], ST[:, :, :]))
                    x = ve.tensor_tensor(STL[:, e, :, :], ST[:, :, :], STH[:, e, :, :].bitcast(F32), SUB)
                    if e:
                        x.then_inc(gla_ve, 1)
                        ve.wait_ge(gla_ve, 3 * t + 3)
                    else:
                        own(x)
                    for p in range(2):
                        for j in range(2):
                            rows, w = slice(DK * j, DK * (j + 1)), slice(DV * j, DV * (j + 1))
                            x = ve.scalar_tensor_tensor(
                                ST[rows, p, w], ST[rows, p, w], DEC[rows, p, 2 * t + e:2 * t + e + 1],
                                PS[rows, 2 + e, 2 * DV * p + DV * j:2 * DV * p + DV * (j + 1)], M, A)
                    own(x)
            ve.wait_ge(gla_pe, 12)
            own(ve.tensor_copy(CV[:, :, :], PS[:, 4:8, :]))
            for t in range(T):
                for h in range(GLA_H):
                    x = ve.bn_stats(OBN[:, 4 * t + h, :], CV[:, t, DV * h:DV * (h + 1)])
            own(x)
            for j in range(16):
                x = ve.bn_aggr(OMV[:, j, :], OBN[:, j, :])
            own(x)
            own(ve.tensor_tensor(OMV[:, :, 0], OMV[:, :, 0], OMV[:, :, 0], M))
            ve.tensor_tensor(OMV[:, :, 1], OMV[:, :, 0], OMV[:, :, 1], A).then_inc(gla_prep, 1)
            ve.wait_ge(gla_act, 4)
            own(ve.reciprocal(ORS[:, :], OSTD[:, :]))
            for t in range(T):
                for h in range(GLA_H):
                    w = slice(DV * h, DV * (h + 1))
                    x = ve.scalar_tensor_tensor(CV[:, t, w], CV[:, t, w], ORS[:, 4 * t + h:4 * t + h + 1],
                                                GN[:, :], M, M)
            own(x)
            ve.tensor_tensor(CV[:, :, :], CV[:, :, :], GG[:, :, :], M).then_inc(gla_ve, 1)
            ve.wait_ge(gla_act, 5)
            ve.tensor_tensor(XTL[:, 0:4, :], PS[:, 0:4, :], XTH[:, 0:4, :].bitcast(F32), SUB).then_inc(gla_ve, 1)
            boundary(6, FIRST["ffn"])
            if boundaries <= 7:
                return
            gated_hidden(FIRST["ffn"], 16)
            split_hidden(FIRST["down2"], 22)
            boundary(7, CHUNKS)

        @block.scalar
        def _(act):
            own = Order(act, act_own)
            F = ACT

            def load(o, i, done):
                act.dma_start(o, i).then_inc(done, 16)

            load(ONEHOT[:, :], d["onehot"], const_landed)
            load(REL[:, :], d["rel"], const_landed)
            load(XS[:, :, :], d["xt"], const_landed)
            load(IDENT[:, :], d["ident"], const_landed)
            load(MASKROW[:, :], d["maskrow"], const_landed)
            load(CHUNKTRI[:, :], d["chunktri"], const_landed)
            load(ROPET[:, :], d["rope"], const_landed)
            load(GAIN[:, :], d["gains"], const_landed)
            load(SINK[:, :], d["sinks"].to_broadcast([P, SWA_H]), const_landed)
            load(X[:, :, :], d["x"], const_landed)
            act.wait_ge(const_landed, CONST_ALL)
            for j in range(4):
                w = slice(2 * j, 2 * j + 2)
                act.copy(XTH[:, w, :], XS[:, w, :]).then_inc(xt_hi, 1)
            act.wait_ge(bias_out, 1)
            act.dma_start(d["bias_rows"], QM[:, :, 0:3 * P]).then_inc(bias_stored, 16)
            act.wait_ge(bias_stored, 16)
            load(BIAS[:, :, :], d["bias_skew"], bias_landed)
            act.wait_ge(lat_sq, 1)
            act.wait_ge(bias_landed, 16)
            act.activation(CSTD[:, :], CMV[:, :, 1], F.Sqrt, bias=EPS[:, 0:1]).then_inc(lat_std, 1)
            for f in range(5):
                act.wait_ge(lat_turned, f + 1)
                act.activation(CTH[:, f, :], PS[:, f, :], F.Copy, scale=GAIN[:, f:f + 1]).then_inc(lat_hi, 1)

            def exps(h, r):
                kind, s = kind_of(h), h % 2
                at = (WINDOW_AT + [896]) if kind == "swa" else (CAUSAL_AT + [1280])
                bias = NB if kind == "fox" else MN
                for done, (i, _) in enumerate(block_order(kind)):
                    act.wait_ge(masked, 4 * h + done + 1 + 16 * r)
                    p = PB[:, s, at[i]:at[i + 1]]
                    act.activation(p, p, F.Exp, bias=bias[:, s, i:i + 1], scale=-1.0,
                                   accum_out=SM[:, s, i:i + 1]).then_inc(expd, 1)
                if kind == "swa":
                    g = swa_head(h)
                    act.activation(ES[:, :], MN[:, s, :], F.Exp, bias=SINK[:, g:g + 1]).then_inc(sunk, 1)

            def probs_hi(h, r):
                n = 896 if kind_of(h) == "swa" else 1280
                act.wait_ge(turned, h + 1 + 4 * r)
                if h >= 2:
                    act.wait_ge(o_ready, h - 1 + 4 * r)
                act.copy(PTH[:, h % 2, 0:n], PSF[:, 3 * S:3 * S + n]).then_inc(pt_hi, 1)

            def out_hi(h, r):
                rows, tile = slice(HD * (h % 2), HD * (h % 2 + 1)), out_tile(h)
                act.wait_ge(o_ready, h + 1 + 4 * r)
                act.copy(XTH[rows, tile + 2 * r, :], PS[rows, 6 + h % 2, :]).then_inc(o_hi, 1)

            def attend_step(h, r, last):
                if h < last:
                    exps(h + 1, r)
                probs_hi(h, r)
                if h not in (0, FOX0):
                    out_hi(h - 1, r)
                if h == last:
                    out_hi(h, r)

            exps(0, 0)
            for h in range(16):
                attend_step(h, 0, 15)

            def vectors(b):
                n = BOUND[b][2]
                load(G[:, 0, :], d["gain_rows"][n:n + 1, :].to_broadcast([P, D]), vec_landed)
                if BOUND[b][1] == "layer":
                    load(G[:, 1, :], d["bias_vecs"][n:n + 1, :].to_broadcast([P, D]), vec_landed)

            def boundary(b):
                add, kind, n = BOUND[b]
                layer = kind == "layer"

                def deviation(t):
                    act.wait_ge(var_ready, 4 * n + t + 1)
                    act.activation(STD[:, t:t + 1], MV[:, t, 1:2], F.Sqrt,
                                   bias=EPS[:, 0 if layer else 1:1 if layer else 2]).then_inc(std_ready, 1)

                def centre(t):
                    act.wait_ge(scale_ready, 4 * n + t + 1)
                    if layer:
                        x = act.activation(X[:, t, :], X[:, t, :], F.Identity, bias=NMR[:, t:t + 1],
                                           scale=RSTD[:, t:t + 1])
                    elif b < 7:
                        if t >= 2:
                            act.wait_ge(x_turned, 4 * b + t - 1)
                        x = act.activation(Y[:, t % 2, :], X[:, t, :], F.Copy, scale=RSTD[:, t:t + 1])
                    else:
                        x = act.activation(X[:, t, :], X[:, t, :], F.Copy, scale=RSTD[:, t:t + 1])
                    x.then_inc(centred, 1)

                def high(t):
                    act.wait_ge(x_turned, 4 * b + t + 1)
                    w = slice(t * P, (t + 1) * P)
                    src = PSF[:, D * t:D * (t + 1)].rearrange("p (k n) -> p k n", k=KD)
                    act.copy(XTH[:, :, w], src).then_inc(xt_hi, 1)

                for t in range(T + 3):
                    if kind:
                        if t < T:
                            deviation(t)
                        if 1 <= t <= T:
                            centre(t - 1)
                    if t >= 3 and b < 7:
                        high(t - 3)

            def embedding_inputs(layer, tiles_split):
                act.wait_ge(hs_ready, tiles_split)
                load(ER[:, :, :], d["pt"][layer], gate_landed)
                load(BG[:, :], d["gate_bias"][layer:layer + 1, :].to_broadcast([P, D]), gate_landed)

            def embedding(layer):
                for half in range(2):
                    act.wait_ge(emb_z, 2 * layer + half + 1)
                    act.activation(SG[:, :, :], SG[:, :, :], F.Sigmoid).then_inc(emb_sig, 1)

            act.wait_ge(o_lo, 16)
            vectors(0)
            boundary(0)
            if boundaries <= 1:
                return
            act.wait_ge(y_ready, 4)
            vectors(1)
            embedding_inputs(0, 32)
            boundary(1)
            if boundaries <= 2:
                return
            embedding(0)
            boundary(2)
            if boundaries <= 3:
                return
            act.wait_ge(y_ready, 12)
            load(SWR[:, :, :], d["w_forget"], fox_landed)
            load(BF[:, :], d["b_forget"].to_broadcast([P, RANK]), fox_landed)
            load(STEPS[:, :], d["steps"], fox_landed)
            act.wait_ge(gates_z, 2)
            own(act.activation(LA[:, :], LA[:, :], F.Exp, scale=-1.0))
            act.activation(LA[:, :], LA[:, :], F.Ln, bias=1.0).then_inc(gates_ln, 1)
            act.wait_ge(gates_rows, 1)
            act.dma_start(d["gate_rows"], CC_ROWS[:, :]).then_inc(rows_stored, 16)
            exps(FOX0, 0)
            for h in (FOX0, FOX0 + 1):
                attend_step(h, 0, FOX0 + 15)
            with act.Fori(0, 3) as r:
                for h in range(FOX0 + 2, FOX0 + 6):
                    attend_step(h, r, FOX0 + 15)
            for h in (FOX0 + 14, FOX0 + 15):
                attend_step(h, 0, FOX0 + 15)
            act.wait_ge(o_lo, 32)
            vectors(3)
            boundary(3)
            if boundaries <= 4:
                return
            act.wait_ge(y_ready, 16)
            vectors(4)
            embedding_inputs(1, 64)
            boundary(4)
            if boundaries <= 5:
                return
            act.wait_ge(y_ready, 20)
            vectors(5)
            embedding(1)
            boundary(5)
            if boundaries <= 6:
                return
            act.wait_ge(y_ready, 24)
            act.wait_ge(x_turned, 24)
            load(TWR[:, :, :], d["w_gate"], gla_const)
            load(WG[:, :], d["w_gate_up"], gla_const)
            load(CW[:, :, :], d["conv_w"], gla_const)
            load(GN[:, :], d["gla_gain"].to_broadcast([P, DV]), gla_const)
            act.wait_ge(gla_prep, 4)
            own(act.activation(GA[:, :, :], GA[:, :, :], F.Exp, scale=-1.0))
            act.activation(GA[:, :, :], GA[:, :, :], F.Ln, bias=1.0).then_inc(gla_act, 1)
            act.wait_ge(gla_prep, 7)
            ends = BT[:, :, :].rearrange("p f (n c) -> p f n c", c=GCH)[:, :, :, GCH - 1]
            act.activation(QI[:, :, :], BT[:, :, :], F.Exp)
            act.activation(KI[:, :, :], BT[:, :, :], F.Exp, scale=-1.0)
            act.activation(DEC[:, :, :], ends, F.Exp)
            act.activation(KK[:, :, :], KK[:, :, :], F.Exp).then_inc(gla_act, 1)
            act.wait_ge(evac, 16)
            act.activation(GG[:, :, :], GG[:, :, :], F.Silu).then_inc(gla_act, 1)
            act.wait_ge(gla_prep, 8)
            act.copy(XTH[:, 4:8, :], CV[:, :, :]).then_inc(conv_hi, 1)
            act.wait_ge(gla_prep, 9)
            act.activation(OSTD[:, :], OMV[:, :, 1], F.Sqrt, bias=EPS[:, 1:2]).then_inc(gla_act, 1)
            act.wait_ge(gla_pe, 13)
            act.copy(XTH[:, 0:4, :], PS[:, 0:4, :]).then_inc(gla_act, 1)
            act.wait_ge(gla_ve, 14)
            vectors(6)
            boundary(6)
            if boundaries <= 7:
                return
            act.wait_ge(y_ready, 28)
            vectors(7)

            def gate(g, bank, r):
                if g:
                    act.wait_ge(relued, 16 + g + 2 * r)
                act.wait_ge(chunk_used, FIRST["ffn"] + 4 * (g + 1) + 8 * r)
                act.activation(GT[:, :, :], PS[:, bank:bank + 2, :], F.Silu).then_inc(gated, 1)

            gate(0, 0, 0)
            with act.Fori(0, 5) as r:
                gate(1, 4, r)
                gate(2, 0, r)
            boundary(7)


def units(w):
    r, n = w.shape
    return w.reshape(r // P, P, n // UNIT, UNIT).transpose(0, 2, 1, 3)


def by_group(w):
    return units(w).transpose(1, 0, 2, 3).reshape(-1, P, UNIT)


def by_row(w):
    return units(w).reshape(-1, P, UNIT)


def stream_of(i):
    w = i["ev_w_in"][0]
    c_q, c_kv, k_r, q_s, k_s, v_s = np.split(w, np.cumsum([Q_LORA, KV_LORA, ROPE, 512, P]), axis=1)
    swap = lambda v: np.concatenate([v[..., ROPE // 2:], v[..., :ROPE // 2]], -1)
    pairs = lambda v, ax: np.take(v, [j for p in range(4) for j in (p, p + 4)], axis=ax)
    q_s = pairs(q_s.reshape(D, SWA_H, HD), 1).reshape(D, 512)
    pad = np.zeros((D, 64), w.dtype)
    parts = [by_group(q_s), by_group(np.concatenate([c_q, k_s], 1)),
             by_group(np.concatenate([c_kv, v_s, k_r, swap(k_r), pad], 1))]
    uq = i["ev_w_uq"][0].reshape(Q_LORA, MLA_H, HD + ROPE)
    uq = np.concatenate([uq, swap(uq[..., HD:])], -1).reshape(Q_LORA, MLA_H * P)
    ukv = i["ev_w_ukv"][0].reshape(KV_LORA, MLA_H, 2, HD)
    parts += [by_group(uq), by_group(ukv[:, :, 0].reshape(KV_LORA, 512)),
              by_group(ukv[:, :, 1].reshape(KV_LORA, 512))]
    wo = i["ev_w_out"][0]
    wo = np.concatenate([wo[:512], pairs(wo[512:].reshape(SWA_H, HD, D), 0).reshape(512, D)], 0)

    def dense(layer):
        up, down = i["w_up"][layer], i["w_down"][layer]
        g, e = i["ple_w_gate"][layer], i["ple_w_proj"][layer]
        out = [by_group(up), by_row(down)]
        for half in range(2):
            w = slice(UNIT * half, UNIT * (half + 1))
            out += [by_group(g[:, w]), by_group(e[:, w])]
        return out

    parts += [by_row(wo)] + dense(0)
    parts += [by_group(i["od_w_in"][0][:, :3 * D]), by_row(i["od_w_out"][0])] + dense(1)
    w = i["w_in_2"][0]
    parts += [by_group(np.concatenate([w[:, :1536], w[:, 1552:]], 1)), by_row(i["w_out_2"][0])]
    gate, up = (i[n][0].reshape(D, D_FF2 // 256, 256) for n in ("w_ffn_gate_2", "w_ffn_up_2"))
    parts += [by_group(np.concatenate([gate, up], 2).reshape(D, 2 * D_FF2)), by_row(i["w_ffn_down_2"][0])]
    s = np.concatenate(parts, 0)
    return np.ascontiguousarray(s.reshape(CHUNKS, 2, P, UNIT).transpose(0, 2, 1, 3).reshape(CHUNKS, P, CHUNK))


def shape_constants():
    f = np.float32
    p, j = np.arange(P)[:, None], np.arange(P)[None, :]
    maskrow = np.zeros((P, S), f)
    maskrow[:, S - P:] = np.where(j > p, f(BIG), f(0))
    chunktri = ((p <= j) & (p // GCH == j // GCH)).astype(f)
    steps = (np.arange(7 * P)[None, :] - 3 * P >= p).astype(f)
    inv = (1.0 / (10000.0 ** (np.arange(0, ROPE, 2, dtype=f) / ROPE))).astype(f)
    ang = inv[:, None] * np.arange(S, dtype=f)[None, :]
    rope = np.zeros((P, S), f)
    rope[64:96] = np.tile(np.cos(ang), (2, 1))
    rope[96:128] = np.concatenate([-np.sin(ang), np.sin(ang)])
    dist = 2 * P - 1 - np.arange(3 * P)
    exact = BUCKETS // 2
    dd = np.maximum(dist, 1).astype(f)
    large = exact + (np.log(dd / f(exact)) / f(np.log(MAX_DIST / exact)) * f(BUCKETS - exact)).astype(np.int32)
    bucket = np.where(dist < exact, np.maximum(dist, 0), np.minimum(large, BUCKETS - 1))
    inside = (dist >= 0) & (dist < WINDOW)
    onehot = np.zeros((BUCKETS + 1, 3 * P), f)
    onehot[bucket[inside], np.nonzero(inside)[0]] = 1
    onehot[BUCKETS, ~inside] = 1
    return {"ident": np.eye(P, dtype=f), "maskrow": maskrow, "chunktri": chunktri, "steps": steps,
            "rope": rope, "onehot": onehot}


def kernel(**inputs):
    import concourse.bacc as bacc
    from concourse.bass_utils import run_bass_kernel_spmd

    i = {k: np.asarray(v) for k, v in inputs.items()}
    f = np.float32
    tiled = lambda w: np.ascontiguousarray(w.reshape(-1, P, w.shape[-1]).transpose(1, 0, 2))
    arrays = dict(shape_constants())
    arrays["stream"] = stream_of(i)
    arrays["x"] = tiled(i["x"][0])
    arrays["xt"] = tiled(i["x"][0].T)
    arrays["pt"] = np.stack([tiled(i["p"][layer, 0].T) for layer in range(DEPTH)])
    arrays["rel"] = np.concatenate([i["rel_bias"], np.full((1, SWA_H), -BIG, f)])
    arrays["sinks"] = i["ev_sinks"]
    arrays["gains"] = np.ascontiguousarray(
        np.concatenate([i["ev_q_norm"][0], i["ev_kv_norm"][0]]).reshape(5, P).T)
    arrays["gain_rows"] = np.stack([i["ln1_g"][0], i["ln2_g"][0], i["ln1_g"][1], i["ln2_g"][1],
                                    i["norm1_g_2"][0], i["norm2_g_2"][0], i["norm_f_g_2"]])
    arrays["bias_vecs"] = np.stack([i["ln1_b"][0], i["ln2_b"][0], i["ln1_b"][1], i["ln2_b"][1]])
    arrays["gate_bias"] = i["ple_b_gate"]
    arrays["w_forget"] = tiled(i["od_w_in"][0][:, 3 * D:])
    arrays["b_forget"] = i["od_b_f"]
    arrays["w_gate"] = tiled(i["w_in_2"][0][:, 1536:1552])
    arrays["w_gate_up"] = np.concatenate([i["w_gate_up_2"][0], i["b_gate_2"]])
    arrays["conv_w"] = np.ascontiguousarray(i["conv_w_2"][0].reshape(3, T, P).transpose(2, 1, 0))
    arrays["gla_gain"] = i["gla_norm_g_2"]
    nc = bacc.Bacc("TRN2", target_bir_lowering=False, num_devices=1)
    d = {n: nc.dram_tensor(n, a.shape, F32, kind="ExternalInput").ap() for n, a in arrays.items()}
    rows = nc.dram_tensor("bias_rows", (P, SWA_H, 3 * P), F32, kind="Internal").ap()
    d["bias_rows"] = rows
    pitch = SWA_H * 3 * P
    d["bias_skew"] = bass.AP(tensor=rows.tensor, offset=P - 1,
                             ap=[[pitch - 1, P], [3 * P, SWA_H], [1, 2 * P]])
    d["gate_rows"] = nc.dram_tensor("gate_rows", (RANK, S), F32, kind="Internal").ap()
    out = nc.dram_tensor("out", (P, T, D), F32, kind="ExternalOutput").ap()
    program(nc, d, out)
    r = run_bass_kernel_spmd(nc, [arrays], core_ids=[0])
    return np.ascontiguousarray(r.results[0]["out"].transpose(1, 0, 2)).reshape(1, S, D)
```

```python
from contextlib import ExitStack

import numpy as np

import concourse.bass as bass
from concourse import mybir

F32 = mybir.dt.float32
F32R = mybir.dt.float32r
ALU = mybir.AluOpType
ACT = mybir.ActivationFunctionType

P = 128
S = 512
T = S // P
D = 1024
KD = D // P
UNIT = 512
CHUNK = 2 * UNIT
RAW = 4
WS = 2
DEPTH = 2
ALPHA = (2 * DEPTH) ** 0.25
LN_EPS, RMS_EPS = 1e-5, 1e-6
BIG = 1e30
HD = 64
MLA_H, SWA_H, FOX_H = 8, 8, 16
ROPE = 32
MLA_SCALE = (HD + ROPE) ** -0.5
Q_LORA, KV_LORA = 384, 256
BUCKETS, MAX_DIST, WINDOW = 32, 128, 128
D_FF, D_FF2 = 4096, 2816
HT_TILES = D_FF // P
PLE_K = 2
GLA_H, DK, DV, GCH = 4, 64, 128, 64
NCH = S // GCH
RANK = 16
GATE_NORM = 16.0

STAGES = [("qs", 4), ("cq", 4), ("ckv", 4), ("uq", 3), ("kn", 1), ("vm", 1), ("out0", 8),
          ("up0", 32), ("down0", 32), ("ple0", 10),
          ("fox", 24), ("out1", 8), ("up1", 32), ("down1", 32), ("ple1", 10),
          ("gla", 24), ("out2", 8), ("ffn", 44), ("down2", 22)]
FIRST, CHUNKS = {}, 0
for _name, _n in STAGES:
    FIRST[_name] = CHUNKS
    CHUNKS += _n

CAUSAL_AT = [0, 128, 384, 768]
WINDOW_AT = [0, 128, 384, 640]
CAUSAL_S = [(0, 0), (2, 0), (0, 128), (1, 0)]
WINDOW_S = [(0, 0), (0, 128), (1, 0), (1, 256)]
CAUSAL_ORDER = [(3, 1), (0, 3), (2, 3), (1, 4)]
WINDOW_ORDER = [(0, 2), (1, 2), (2, 4), (3, 4)]
CAUSAL_T = [0, 512, 1024, 896]
WINDOW_T = [0, 256, 512, 768]


CONST_ALL = 16 * 12
E_FIRST = 7
E_FOX = 13
FOX0 = 16


def kind_of(h):
    return "mla" if h < MLA_H else "swa" if h < FOX0 else "fox"


def block_order(kind):
    return WINDOW_ORDER if kind == "swa" else CAUSAL_ORDER


def item_slot(h):
    return h % 2 if h < MLA_H else h // 2 % 2


def prob_slots(h):
    return 3 if h < FOX0 else 4


def staged_count(h):
    return 2 * (h + 1) if h < MLA_H else 2 * (MLA_H + (h - MLA_H) // 2 + 1)


def swa_head(h):
    j = (h - MLA_H) // 2
    return j + 4 * (h % 2)


def out_tile(h):
    return h // 2 if h < FOX0 else (h - FOX0) // 2


class Order:

    def __init__(self, engine, sem):
        self.engine, self.sem, self.n, self.extra = engine, sem, 0, 0

    def __call__(self, instruction):
        self.n += 1
        instruction.then_inc(self.sem, 1)
        self.engine.wait_ge(self.sem, self.n + self.extra)

    def mark(self, instruction):
        self.n += 1
        instruction.then_inc(self.sem, 1)

    def settled(self):
        self.engine.wait_ge(self.sem, self.n + self.extra)

    def stand(self):
        self.n += 1
        self.engine.sem_inc(self.sem, 1)


def over_chunks(engine, a, b, body):
    n = (b - a) // RAW
    if n > 1:
        with engine.Fori(0, n) as i:
            for j in range(a, a + RAW):
                body(i, j)
    elif n:
        for j in range(a, a + RAW):
            body(0, j)
    for j in range(a + n * RAW, b):
        body(0, j)


def program(nc, d, out, stop=None):
    ctx = ExitStack()
    with ctx:
        def sb(name, shape, dt=F32, at=ctx):
            return at.enter_context(nc.sbuf_tensor(name, shape, dt))

        def sem(name):
            return ctx.enter_context(nc.semaphore(name))

        X = sb("X", [P, T, D])
        XTH = sb("XTH", [P, KD, S], F32R)
        XTL = sb("XTL", [P, KD, S], F32R)
        RW = sb("RW", [P, RAW, CHUNK])
        WH = sb("WH", [P, WS, CHUNK], F32R)
        WL = sb("WL", [P, WS, CHUNK], F32R)
        IDENT = sb("IDENT", [P, P])
        MASKROW = sb("MASKROW", [P, S])
        CHUNKTRI = sb("CHUNKTRI", [P, P])
        IDENT_R = sb("IDENT_R", [P, P], F32R)
        TRI_R = sb("TRI_R", [P, P], F32R)
        CHUNKTRI_R = sb("CHUNKTRI_R", [P, P], F32R)
        EPS = sb("EPS", [P, 2])
        GAINS = sb("GAINS", [P, 7, KD])
        BIASES = sb("BIASES", [P, 4, KD])
        ONE = sb("ONE", [P, 1])
        MV = sb("MV", [P, T, 2])
        BNS = sb("BNS", [P, T, 12])
        STD = sb("STD", [P, T])
        RSTD = sb("RSTD", [P, T])
        NMR = sb("NMR", [P, T])
        MN = sb("MN", [P, 4, T])
        SM = sb("SM", [P, 4, T])
        ES = sb("ES", [P, 4, T])
        NB = sb("NB", [P, 4, T])
        PS = ctx.enter_context(nc.psum_tensor("PS", [P, 8, S], F32))
        PSF = PS[:, :, :].rearrange("p b n -> p (b n)")
        TRI = MASKROW[:, S - P:S]

        prepare = ExitStack()
        XS = sb("XS", [P, KD, S], at=prepare)
        CQ = sb("CQ", [P, T, Q_LORA + KV_LORA], at=prepare)
        CTH = sb("CTH", [P, 5, S], F32R, at=prepare)
        CTL = sb("CTL", [P, 5, S], F32R, at=prepare)
        ROT = sb("ROT", [P, 4, S], at=prepare)
        ONEHOT = sb("ONEHOT", [BUCKETS + 1, 3 * P], at=prepare)
        REL = sb("REL", [BUCKETS + 1, SWA_H], at=prepare)
        ROPET = sb("ROPET", [P, S], at=prepare)
        prepare.close()
        gates = ExitStack()
        STEPS = sb("STEPS", [P, 7 * P], at=gates)
        SWR = sb("SWR", [P, KD, RANK], at=gates)
        SWH = sb("SWH", [P, KD, RANK], F32R, at=gates)
        SWL = sb("SWL", [P, KD, RANK], F32R, at=gates)
        BF = sb("BF", [P, RANK], at=gates)
        LZ = sb("LZ", [P, T * RANK], at=gates)
        LA = sb("LA", [P, T * RANK], at=gates)
        LF = sb("LF", [P, T * RANK], at=gates)
        gates.close()
        attend = ExitStack()
        AQH = sb("AQH", [P, 2, S], F32R, at=attend)
        AQL = sb("AQL", [P, 2, S], F32R, at=attend)
        AKH = sb("AKH", [P, 2, S], F32R, at=attend)
        AKL = sb("AKL", [P, 2, S], F32R, at=attend)
        AVH = sb("AVH", [P, 2, T, P], F32R, at=attend)
        AVL = sb("AVL", [P, 2, T, P], F32R, at=attend)
        PTH = sb("PTH", [P, 2, 1280], F32R, at=attend)
        PTL = sb("PTL", [P, 2, 1280], F32R, at=attend)
        first = ExitStack()
        PB1 = sb("PB1", [P, 3, 1280], at=first)
        QM = sb("QM", [P, MLA_H, S], at=first)
        KM = sb("KM", [P, MLA_H, S], at=first)
        VM = sb("VM", [P, T, 512], at=first)
        QS = sb("QS", [P, T, S], at=first)
        KS = sb("KS", [P, S], at=first)
        VS = sb("VS", [P, T, P], at=first)
        BIAS = sb("BIAS", [P, SWA_H, 2 * P], at=first)
        GAIN = sb("GAIN", [P, 5], at=first)
        SINK = sb("SINK", [P, SWA_H], at=first)
        NSINK = sb("NSINK", [P, SWA_H], at=first)
        CMV = sb("CMV", [P, 8, 2], at=first)
        CBN = sb("CBN", [P, 8, 6], at=first)
        CSTD = sb("CSTD", [P, 8], at=first)
        CRS = sb("CRS", [P, 8], at=first)
        first.close()
        second = ExitStack()
        QF = sb("QF", [P, KD, S], at=second)
        KF = sb("KF", [P, KD, S], at=second)
        VF = sb("VF", [P, T, D], at=second)
        PB2 = sb("PB2", [P, 4, 1280], at=second)
        BC = sb("BC", [P, 2, S], at=second)
        CC_ROWS = sb("CC_ROWS", [RANK, S], at=second)
        CTOK = sb("CTOK", [P, T, RANK], at=second)
        second.close()
        attend.close()
        dense = ExitStack()
        G = sb("G", [P, 2, D], at=dense)
        BG = sb("BG", [P, D], at=dense)
        HT = sb("HT", [P, HT_TILES, S], at=dense)
        HSH = sb("HSH", [P, 2, S], F32R, at=dense)
        HSL = sb("HSL", [P, 2, S], F32R, at=dense)
        GT = sb("GT", [P, 2, S], at=dense)
        YN = HT[:, 16:24, :].rearrange("p (t k) n -> p t (k n)", t=T)
        YT = HT[:, 24:32, :]
        dense.close()
        embed = ExitStack()
        _keep = sb("KEEP_DENSE", [P, 3, D], at=embed)
        SG = sb("SG", [P, T, S], at=embed)
        ER = sb("ER", [P, PLE_K, S], at=embed)
        EH = sb("EH", [P, PLE_K, S], F32R, at=embed)
        EL = sb("EL", [P, PLE_K, S], F32R, at=embed)
        embed.close()
        third = ExitStack()
        QG = sb("QG", [P, 2, S], at=third)
        KG = sb("KG", [P, 2, S], at=third)
        VH = sb("VH", [P, T, 512], F32R, at=third)
        VL = sb("VL", [P, T, 512], F32R, at=third)
        GG = sb("GG", [P, T, 512], at=third)
        CB = sb("CB", [P, T, S], at=third)
        CW = sb("CW", [P, T, 3], at=third)
        U = sb("U", [P, T, S + 2], at=third)
        CV = sb("CV", [P, T, S], at=third)
        TWR = sb("TWR", [P, KD, RANK], at=third)
        TWH = sb("TWH", [P, KD, RANK], F32R, at=third)
        TWL = sb("TWL", [P, KD, RANK], F32R, at=third)
        PA = sb("PA", [P, T, RANK], at=third)
        PAT = sb("PAT", [32, S], at=third)
        WG = sb("WG", [RANK + 1, 2 * P], at=third)
        GL = sb("GL", [P, T, 2 * P], at=third)
        GA = sb("GA", [P, T, 2 * P], at=third)
        GLH = sb("GLH", [P, T, 2 * P], F32R, at=third)
        GLL = sb("GLL", [P, T, 2 * P], F32R, at=third)
        BT = sb("BT", [P, 2, S], at=third)
        QI = sb("QI", [P, 2, S], at=third)
        KI = sb("KI", [P, 2, S], at=third)
        KK = sb("KK", [P, 2, S], at=third)
        QIH = sb("QIH", [P, 2, P], F32R, at=third)
        QIL = sb("QIL", [P, 2, P], F32R, at=third)
        QEH = sb("QEH", [P, 2, 2, P], F32R, at=third)
        QEL = sb("QEL", [P, 2, 2, P], F32R, at=third)
        KIH = sb("KIH", [P, 2, P], F32R, at=third)
        KIL = sb("KIL", [P, 2, P], F32R, at=third)
        SMF = sb("SMF", [P, 512], at=third)
        SMH = sb("SMH", [P, 512], F32R, at=third)
        SML = sb("SML", [P, 512], F32R, at=third)
        KTH = sb("KTH", [P, 2 * P], F32R, at=third)
        KTL = sb("KTL", [P, 2 * P], F32R, at=third)
        DEC = sb("DEC", [P, 2, NCH], at=third)
        ST = sb("ST", [P, 2, 2 * DV], at=third)
        STH = sb("STH", [P, 2, 2, 2 * DV], F32R, at=third)
        STL = sb("STL", [P, 2, 2, 2 * DV], F32R, at=third)
        GN = sb("GN", [P, DV], at=third)
        OBN = sb("OBN", [P, 16, 6], at=third)
        OMV = sb("OMV", [P, 16, 2], at=third)
        OSTD = sb("OSTD", [P, 16], at=third)
        ORS = sb("ORS", [P, 16], at=third)
        third.close()

        def probs(h):
            return (PB1 if h < FOX0 else PB2)[:, h % prob_slots(h), :]

        landed = [sem(f"raw_landed{j}") for j in range(RAW)]
        hi_split = sem("hi_split")
        lo_split = sem("lo_split")
        chunk_used = sem("chunk_used")
        const_landed = sem("const_landed")
        vec_landed = sem("vec_landed")
        gate_landed = sem("gate_landed")
        bias_out = sem("bias_out")
        bias_stored = sem("bias_stored")
        bias_landed = sem("bias_landed")
        consts_made = sem("consts_made")
        xt_hi = sem("xt_hi")
        xt_ready = sem("xt_ready")
        yt_copied = sem("yt_copied")
        yt_ready = sem("yt_ready")
        proj = sem("projected")
        evac = sem("evacuated")
        lat_sq = sem("latent_squares")
        lat_std = sem("latent_std")
        lat_normed = sem("latent_normed")
        lat_turned = sem("latent_turned")
        lat_hi = sem("latent_hi")
        lat_lo = sem("latent_lo")
        staged = sem("staged")
        vstaged = sem("values_staged")
        scored = sem("scored")
        masked = sem("masked")
        sunk = sem("sinks_exp")
        biased = sem("exp_biases")
        expd = sem("exponentials")
        normed = sem("normalised")
        turned = sem("probs_turned")
        pt_hi = sem("probs_hi")
        pt_lo = sem("probs_lo")
        o_ready = sem("head_out")
        o_hi = sem("head_out_hi")
        o_lo = sem("head_out_lo")
        bc_landed = [sem(f"bc_landed{j}") for j in range(2)]
        gates_logit = sem("fgate_logits")
        gates_ln = sem("fgate_ln")
        gates_z = sem("fgate_z")
        gates_log = sem("fgate_log")
        gates_sum = sem("fgate_sums")
        gates_rows = sem("fgate_rows")
        rows_stored = sem("fgate_rows_stored")
        fox_landed = sem("fgate_weights_landed")
        tile_done = sem("tile_done")
        var_ready = sem("var_ready")
        std_ready = sem("std_ready")
        scale_ready = sem("scale_ready")
        centred = sem("centred")
        y_ready = sem("y_ready")
        x_turned = sem("x_turned")
        gated = sem("gated")
        relued = sem("hidden_out")
        hs_ready = sem("hidden_ready")
        emb_ready = sem("emb_ready")
        emb_tile = sem("emb_tile")
        emb_z = sem("emb_z")
        emb_sig = sem("emb_sig")
        emb_x = sem("emb_x")
        gla_const = sem("gla_landed")
        gla_small = sem("gla_small")
        gla_prep = sem("gla_prep")
        gla_act = sem("gla_act")
        gla_pe = sem("gla_pe")
        gla_ve = sem("gla_ve")
        conv_hi = sem("conv_hi")
        conv_lo = sem("conv_lo")
        out_stored = sem("out_stored")
        act_own = sem("act_own")
        ve_own = sem("ve_own")
        pool_own = sem("pool_own")

        block = ctx.enter_context(nc.Block())
        boundaries = 8 if stop is None else stop + 1

        BOUND = [(True, "layer", 0), (True, "layer", 1), (False, None, None), (True, "layer", 2),
                 (True, "layer", 3), (False, "rms", 4), (True, "rms", 5), (True, "rms", 6)]
        NORMS = [b for b in range(8) if BOUND[b][1]]
        Y_BASE = [0, 4, 8, 12, 16, 20, 20, 20]

        def fox_heads(engine, body):
            for h in (FOX0, FOX0 + 1):
                body(h, 0)
            with engine.Fori(0, 3) as r:
                for h in range(FOX0 + 2, FOX0 + 6):
                    body(h, r)
            for h in (FOX0 + 14, FOX0 + 15):
                body(h, 0)

        @block.sync
        def _(sp):
            def load(i, j):
                if j >= RAW:
                    sp.wait_ge(lo_split, j - RAW + 1 + RAW * i)
                sp.dma_start(RW[:, j % RAW, :], d["stream"][RAW * i + j]).then_inc(landed[j % RAW], 16)

            for j in range(RAW):
                load(0, j)
            ends = [FIRST["out0"], FIRST["up0"], FIRST["ple0"], FIRST["fox"], FIRST["up1"], FIRST["ple1"],
                    FIRST["gla"], FIRST["ffn"], CHUNKS]
            last = ends[boundaries] if boundaries < 8 else CHUNKS
            cut = FIRST["out1"] + RAW
            over_chunks(sp, RAW, min(cut, last), load)
            if boundaries > 3:
                def load_row(h, r):
                    if h == FOX0:
                        sp.wait_ge(rows_stored, 16)
                    if h >= FOX0 + 2:
                        sp.wait_ge(masked, 4 * (h - 1) + 16 * r)
                    src = d["gate_rows"][bass.ds(h - FOX0 + 4 * r, 1), :].to_broadcast([P, S])
                    sp.dma_start(BC[:, h % 2, :], src).then_inc(bc_landed[h % 2], 16)

                fox_heads(sp, load_row)
                over_chunks(sp, cut, last, load)
            if boundaries == 8:
                for t in range(T):
                    sp.wait_ge(y_ready, Y_BASE[7] + t + 1)
                    sp.dma_start(out[:, t, :], X[:, t, :]).then_inc(out_stored, 16)
                sp.wait_ge(out_stored, 16 * T)
            if stop is not None:
                if boundaries in (2, 5):
                    sp.wait_ge(gate_landed, 32 if boundaries == 2 else 64)
                sp.wait_ge(y_ready, Y_BASE[boundaries])
                sp.wait_ge(xt_ready, KD * (boundaries + 1))
                sp.wait_ge(centred, 4 * sum(b < boundaries for b in NORMS))
                sp.dma_start(out, X[:, :, :]).then_inc(out_stored, 16)
                sp.wait_ge(out_stored, 16)

        @block.gpsimd
        def _(pool):
            own = Order(pool, pool_own)

            def cut(i, j):
                pool.wait_ge(landed[j % RAW], 16 * (j // RAW + 1) + 16 * i)
                if j >= WS:
                    pool.wait_ge(chunk_used, j - WS + 1 + RAW * i)
                pool.sem_inc(hi_split, 1)
                pool.tensor_scalar(WH[:, j % WS, :], RW[:, j % RAW, :], 1.0, 1.0,
                                   ALU.mult, ALU.mult).then_inc(hi_split, 1)
                pool.wait_ge(hi_split, 2 * (j + 1) + 2 * RAW * i)
                pool.tensor_tensor(WL[:, j % WS, :], RW[:, j % RAW, :], WH[:, j % WS, :].bitcast(F32),
                                   ALU.subtract).then_inc(lo_split, 1)

            def stage(hi, lo, src, done):
                own(pool.tensor_scalar(hi, src, 1.0, 1.0, ALU.mult, ALU.mult))
                pool.tensor_tensor(lo, src, hi.bitcast(F32), ALU.subtract).then_inc(done, 1)

            def stage_looped(hi, lo, src, done):
                own.stand()
                own(pool.tensor_tensor(hi, src, ONE[:, 0:1].to_broadcast([P, S]), ALU.mult))
                own.stand()
                pool.tensor_tensor(lo, src, hi.bitcast(F32), ALU.subtract).then_inc(done, 1)

            def stage_mla(h):
                s = h % 2
                stage(AQH[0:96, s, :], AQL[0:96, s, :], QM[0:96, h, :], staged)
                stage(AKH[0:96, s, :], AKL[0:96, s, :], KM[0:96, h, :], staged)

            def stage_pair(s, q, k):
                stage(AQH[:, s, :], AQL[:, s, :], q, staged)
                stage(AKH[:, s, :], AKL[:, s, :], k, staged)

            def stage_values(s, v):
                stage(AVH[:, s, :, :], AVL[:, s, :, :], v, vstaged)

            own(pool.memset(ONE[:, :], 1.0))
            for j in range(RAW):
                cut(0, j)
            over_chunks(pool, RAW, FIRST["out0"] + WS - 1, cut)
            pool.wait_ge(evac, E_FIRST)
            pool.wait_ge(chunk_used, FIRST["out0"])
            stage_mla(0)
            stage_values(0, VM[:, :, 0:P])
            stage_mla(1)
            for h in range(16):
                if h % 2 == 0 and h >= 6 and h < 14:
                    pool.wait_ge(scored, 4 * (h + 1) if h == 6 else 4 * h)
                    stage_pair(h // 2 % 2 ^ 1, QS[:, (h - 6) // 2, :], KS[:, :])
                elif h < 6:
                    pool.wait_ge(scored, 4 * (h + 1))
                    stage_mla(h + 2)
                if h % 2 == 0 and h >= 2:
                    if h >= 4:
                        pool.wait_ge(o_ready, h - 2)
                    p = h // 2
                    stage_values(p % 2, VM[:, :, p * P:(p + 1) * P] if p < 4 else VS[:, :, :])
            if boundaries <= 3:
                over_chunks(pool, FIRST["out0"] + WS - 1,
                            [0, FIRST["up0"], FIRST["ple0"], FIRST["fox"]][boundaries], cut)
                return
            over_chunks(pool, FIRST["out0"] + WS - 1, FIRST["out1"] + WS - 1, cut)
            pool.wait_ge(evac, E_FOX)
            stage_pair(0, QF[:, 0, :], KF[:, 0, :])
            stage_values(0, VF[:, :, 0:P])

            def fox_stage(h, r):
                if h % 2 == 0 and h < FOX0 + 14:
                    n = (h + 2 - FOX0) // 2
                    if h > FOX0:
                        pool.wait_ge(scored, 4 * h + 16 * r)
                    s = n % 2
                    stage_looped(AQH[:, s, :], AQL[:, s, :], QF[:, n + 2 * r, :], staged)
                    stage_looped(AKH[:, s, :], AKL[:, s, :], KF[:, n + 2 * r, :], staged)
                if h % 2 == 0 and h > FOX0:
                    pool.wait_ge(o_ready, h - 2 + 4 * r)
                    n = (h - FOX0) // 2
                    s, v = n % 2, VF[:, :, bass.ds(n * P + 2 * P * r, P)]
                    own.stand()
                    own(pool.tensor_tensor(AVH[:, s, :, :], v, ONE[:, 0:1].unsqueeze(1).to_broadcast([P, T, P]), ALU.mult))
                    own.stand()
                    pool.tensor_tensor(AVL[:, s, :, :], v, AVH[:, s, :, :].bitcast(F32), ALU.subtract).then_inc(vstaged, 1)

            for h in (FOX0, FOX0 + 1):
                fox_stage(h, 0)
            n1 = own.n
            with pool.Fori(0, 3) as r:
                own.extra = 18 * r
                for h in range(FOX0 + 2, FOX0 + 6):
                    fox_stage(h, r)
            own.extra = 0
            assert own.n == n1 + 18
            own.n += 36
            for h in (FOX0 + 14, FOX0 + 15):
                fox_stage(h, 0)
            last = [FIRST["up1"], FIRST["ple1"], FIRST["gla"], FIRST["ffn"], CHUNKS][boundaries - 4]
            over_chunks(pool, FIRST["out1"] + WS - 1, last, cut)

        @block.tensor
        def _(pe):
            def mm(o, a, b, start, stop):
                return pe.matmul(o, a, b, start=start, stop=stop)

            def mm3(o, ah, al, bh, bl, start, stop):
                mm(o, ah, bh, start, False)
                mm(o, ah, bl, False, False)
                return mm(o, al, bh, False, stop)

            def chunk(c, r=0, ready=True):
                if ready:
                    pe.wait_ge(lo_split, c + 1 + r)

            def features(c, bank, r=0, new=0):
                columns, k_tiles = (0, P, 2 * P, 3 * P), KD
                for k in range(k_tiles):
                    cc, u = c + k // 2, UNIT * (k % 2)
                    if new:
                        pe.wait_ge(xt_ready, KD * (new - 1) + k + 1)
                    if k % 2 == 0:
                        chunk(cc, r)
                    for m, col in enumerate(columns):
                        w = slice(u + col, u + col + P)
                        x = mm3(PS[:, bank + m, :], WH[:, cc % WS, w], WL[:, cc % WS, w],
                                XTH[:, k, :], XTL[:, k, :], k == 0, k == k_tiles - 1)
                    if k % 2:
                        x.then_inc(chunk_used, 1)

            def tokens(c, bank, h=XTH, l=XTL, k_tiles=KD, new=0):
                for k in range(k_tiles):
                    cc, u = c + k // 2, UNIT * (k % 2)
                    if new:
                        pe.wait_ge(xt_ready, KD * (new - 1) + k + 1)
                    if k % 2 == 0:
                        chunk(cc)
                    for t in range(T):
                        ts = slice(t * P, (t + 1) * P)
                        w = slice(u, u + UNIT)
                        x = mm3(PS[:, bank + t, :], h[:, k, ts], l[:, k, ts],
                                WH[:, cc % WS, w], WL[:, cc % WS, w], k == 0, k == k_tiles - 1)
                    if k % 2:
                        x.then_inc(chunk_used, 1)

            def wide(c, r, h, l, first, order=(0, 1, 2, 3), late=None):
                chunk(c, r)
                for t in order:
                    if late and t == order[2]:
                        pe.wait_ge(relued, late)
                    x = wide_tile(t, c, h, l, first, False)
                x.then_inc(chunk_used, 1)

            def wide_tile(t, c, h, l, first, last):
                ts = slice(t * P, (t + 1) * P)
                for n in range(2):
                    w = slice(UNIT * n, UNIT * (n + 1))
                    x = mm3(PS[:, 2 * t + n, :], h[:, ts], l[:, ts],
                            WH[:, c % WS, w], WL[:, c % WS, w], first, last)
                return x

            def wide_end(c, a, b, parts_ready=None):
                chunk(c)
                for t in (0, 1):
                    wide_tile(t, c, *a, False, False)
                if parts_ready:
                    pe.wait_ge(hs_ready, parts_ready)
                chunk(c + 1)
                for t in range(T):
                    if t >= 2:
                        wide_tile(t, c, *a, False, False)
                    x = wide_tile(t, c + 1, *b, False, True)
                    x.then_inc(*((tile_done, 1) if t < T - 1 else (chunk_used, 2)))

            def outward(c):
                for k in range(KD - 2):
                    wide(c + k, 0, XTH[:, k, :], XTL[:, k, :], k == 0)
                wide_end(c + KD - 2, *((XTH[:, k, :], XTL[:, k, :]) for k in (KD - 2, KD - 1)))

            def input_ready(n):
                pe.wait_ge(xt_ready, KD * n)

            def qk(h, r):
                kind, s = kind_of(h), item_slot(h)
                pe.wait_ge(staged, staged_count(h) + (4 * r if h >= FOX0 else 0))
                if h:
                    pe.wait_ge(masked, 4 * h + 16 * r)
                a = 0 if kind == "mla" else HD * (h % 2)
                rows = slice(a, a + (96 if kind == "mla" else HD))
                for i, _ in block_order(kind):
                    k0 = max(0, i - 1) * P if kind == "swa" else 0
                    n = (i + 1) * P - k0
                    bank, col = (WINDOW_S if kind == "swa" else CAUSAL_S)[i]
                    q = slice(i * P, (i + 1) * P)
                    o = PS[:, bank, col:col + n]
                    x = mm3(o, AQH[rows, s, q], AQL[rows, s, q], AKH[rows, s, k0:k0 + n],
                            AKL[rows, s, k0:k0 + n], True, kind != "fox")
                    if kind == "fox":
                        x = mm(PS[:, bank, col + n - P:col + n], IDENT_R[:, :], TRI_R[:, :], False, True)
                    x.then_inc(scored, 1)

            def turn(h, r):
                window = kind_of(h) == "swa"
                pe.wait_ge(normed, h + 1 + 4 * r)
                if h:
                    pe.wait_ge(pt_lo, h + 4 * r)
                at, to = (WINDOW_AT, WINDOW_T) if window else (CAUSAL_AT, CAUSAL_T)
                for i in range(T):
                    k0 = max(0, i - 1) if window else 0
                    for kb in range(k0, i + 1):
                        o = 3 * S + to[kb] + P * (i - kb)
                        p = at[i] + P * (kb - k0)
                        x = pe.transpose(PSF[:, o:o + P], probs(h)[:, p:p + P], IDENT[:, :])
                x.then_inc(turned, 1)

            def pv(h, r):
                window = kind_of(h) == "swa"
                s, v, bank = h % 2, h // 2 % 2, 6 + h % 2
                pe.wait_ge(pt_lo, h + 1 + 4 * r)
                pe.wait_ge(vstaged, h // 2 + 1 + 2 * r)
                if h >= 2:
                    pe.wait_ge(o_lo, h - 1 + 4 * r)
                if window:
                    for i in range(T):
                        for kb in range(max(0, i - 1), i + 1):
                            p = slice(WINDOW_T[kb] + P * (i - kb), WINDOW_T[kb] + P * (i - kb + 1))
                            x = mm3(PS[:, bank, i * P:(i + 1) * P], AVH[:, v, kb, :], AVL[:, v, kb, :],
                                    PTH[:, s, p], PTL[:, s, p], kb == max(0, i - 1), kb == i)
                else:
                    for kb in range(T):
                        n = S - kb * P
                        p = slice(CAUSAL_T[kb], CAUSAL_T[kb] + n)
                        x = mm3(PS[:, bank, kb * P:S], AVH[:, v, kb, :], AVL[:, v, kb, :],
                                PTH[:, s, p], PTL[:, s, p], kb == 0, kb == T - 1)
                x.then_inc(o_ready, 1)

            def attend_step(h, r, last):
                if h + 2 <= last:
                    qk(h + 2, r)
                turn(h, r)
                if h not in (0, FOX0):
                    pv(h - 1, r)
                if h == last:
                    pv(h, r)

            def boundary(b):
                add, kind, n = BOUND[b]
                for t in range(T):
                    if kind:
                        pe.wait_ge(centred, 4 * n + t + 1)
                    else:
                        pe.wait_ge(y_ready, Y_BASE[b] + t + 1)
                    src = YN[:, t, :] if kind == "rms" else X[:, t, :]
                    for k in range(KD):
                        x = pe.transpose(PS[:, 2 * t + k // 4, P * (k % 4):P * (k % 4 + 1)],
                                         src[:, k * P:(k + 1) * P], IDENT[:, :])
                    x.then_inc(x_turned, 1)
                pe.wait_ge(yt_copied, 4 * (b + 1))

            def hidden(c, groups, g0, new):
                def one(g, r):
                    if g >= 2:
                        pe.wait_ge(relued, g0 + g - 1 + 2 * r)
                    features(c + 4 * g, 4 * (g % 2), 8 * r, new if g == 0 else 0)

                n = 2 + groups % 2
                for g in range(n):
                    one(g, 0)
                with pe.Fori(0, (groups - n) // 2) as r:
                    one(n, r)
                    one(n + 1, r)

            def down(c, k_tiles, groups, g0, k0):
                order = (0, 1, 2, 3) if groups % 2 == 0 else (2, 3, 0, 1)
                pe.wait_ge(relued, g0 + groups - 1)

                def one(k, r):
                    pe.wait_ge(hs_ready, k0 + k + 1 + 4 * r)
                    wide(c + k, 4 * r, HSH[:, k % 2, :], HSL[:, k % 2, :], k == 0,
                         order, g0 + groups if k == 0 else None)

                for k in range(4):
                    one(k, 0)
                n = (k_tiles - 8) // 4
                with pe.Fori(0, n) as r:
                    for k in range(4, 8):
                        one(k, r)
                for k in range(4 + 4 * n, k_tiles - 2):
                    one(k, 0)
                pe.wait_ge(hs_ready, k0 + k_tiles - 1)
                wide_end(c + k_tiles - 2, *((HSH[:, k, :], HSL[:, k, :]) for k in (0, 1)),
                         parts_ready=k0 + k_tiles)

            def embedding(c, layer, new):
                for half in range(2):
                    c0 = c + 5 * half
                    if half:
                        pe.wait_ge(emb_z, 8 * layer + 4)
                    tokens(c0, 0, new=0 if half else new)
                    if half:
                        pe.wait_ge(emb_x, 2 * layer + 1)
                    else:
                        pe.wait_ge(emb_ready, layer + 1)
                    chunk(c0 + 4)
                    for t in range(T):
                        ts = slice(t * P, (t + 1) * P)
                        for k in range(PLE_K):
                            w = slice(UNIT * k, UNIT * (k + 1))
                            x = mm3(PS[:, 4 + t, :], EH[:, k, ts], EL[:, k, ts],
                                    WH[:, (c0 + 4) % WS, w], WL[:, (c0 + 4) % WS, w], k == 0, k == 1)
                        x.then_inc(emb_tile, 1)
                    pe.wait_ge(emb_tile, 8 * layer + 4 * half + 4)
                    pe.sem_inc(chunk_used, 1)

            pe.wait_ge(const_landed, CONST_ALL)
            pe.wait_ge(consts_made, 1)
            for h in range(SWA_H):
                x = mm(PS[:, h, 0:3 * P], REL[:, h:h + 1].to_broadcast([BUCKETS + 1, P]), ONEHOT[:, :], True, True)
            x.then_inc(proj, 1)
            pe.wait_ge(bias_out, 1)
            input_ready(1)
            features(FIRST["qs"], 0)
            pe.wait_ge(evac, 1)
            c = FIRST["cq"]
            for k in range(KD):
                cc, u = c + k // 2, UNIT * (k % 2)
                if k % 2 == 0:
                    chunk(cc)
                for t in range(T):
                    ts = slice(t * P, (t + 1) * P)
                    mm3(PS[:, 4 + t, 0:Q_LORA], XTH[:, k, ts], XTL[:, k, ts],
                        WH[:, cc % WS, u:u + Q_LORA], WL[:, cc % WS, u:u + Q_LORA], k == 0, k == KD - 1)
                w = slice(u + Q_LORA, u + UNIT)
                x = mm3(PS[:, 0, :], WH[:, cc % WS, w], WL[:, cc % WS, w], XTH[:, k, :], XTL[:, k, :],
                        k == 0, k == KD - 1)
                if k % 2:
                    x.then_inc(chunk_used, 1)
            pe.wait_ge(evac, 2)
            c = FIRST["ckv"]
            for k in range(KD):
                cc, u = c + k // 2, UNIT * (k % 2)
                if k % 2 == 0:
                    chunk(cc)
                for t in range(T):
                    ts = slice(t * P, (t + 1) * P)
                    mm3(PS[:, 1 + t, 0:384], XTH[:, k, ts], XTL[:, k, ts],
                        WH[:, cc % WS, u:u + 384], WL[:, cc % WS, u:u + 384], k == 0, k == KD - 1)
                w = slice(u + 320, u + 448)
                x = mm3(PS[:, 5, :], WH[:, cc % WS, w], WL[:, cc % WS, w], XTH[:, k, :], XTL[:, k, :],
                        k == 0, k == KD - 1)
                if k % 2:
                    x.then_inc(chunk_used, 1)
            pe.wait_ge(evac, 3)
            pe.wait_ge(lat_normed, 1)
            for f in range(5):
                for t in range(T):
                    x = pe.transpose(PS[:, f, t * P:(t + 1) * P], CQ[:, t, f * P:(f + 1) * P], IDENT[:, :])
                x.then_inc(lat_turned, 1)
            pe.wait_ge(lat_lo, 5)
            for n in range(6):
                half, k = n // 3, n % 3
                cc, u = FIRST["uq"] + n // 2, UNIT * (n % 2)
                if n % 2 == 0:
                    chunk(cc)
                for m in range(4):
                    w = slice(u + P * m, u + P * (m + 1))
                    x = mm3(PS[:, 4 * half + m, :], WH[:, cc % WS, w], WL[:, cc % WS, w],
                            CTH[:, k, :], CTL[:, k, :], k == 0, k == 2)
                if n % 2:
                    x.then_inc(chunk_used, 1)
            pe.wait_ge(evac, 4)
            chunk(FIRST["kn"])
            for k in range(2):
                for m in range(4):
                    w = slice(UNIT * k + P * m, UNIT * k + P * (m + 1))
                    x = mm3(PS[:, m, :], WH[:, FIRST["kn"] % WS, w], WL[:, FIRST["kn"] % WS, w],
                            CTH[:, 3 + k, :], CTL[:, 3 + k, :], k == 0, k == 1)
            x.then_inc(chunk_used, 1)
            pe.wait_ge(evac, 5)
            tokens(FIRST["vm"], 4, CTH[:, 3:5, :], CTL[:, 3:5, :], 2)

            pe.wait_ge(evac, E_FIRST)
            qk(0, 0)
            qk(1, 0)
            for h in range(16):
                attend_step(h, 0, 15)

            def block_end(b, name_out, name_up, name_down, groups, g0, k_tiles, k0):
                outward(FIRST[name_out])
                boundary(b)
                if boundaries == b + 1:
                    return
                hidden(FIRST[name_up], groups, g0, b + 2)
                down(FIRST[name_down], k_tiles, groups, g0, k0)

            pe.wait_ge(o_lo, 16)
            pe.wait_ge(o_hi, 16)
            block_end(0, "out0", "up0", "down0", 8, 0, 32, 0)
            if boundaries <= 1:
                return
            boundary(1)
            if boundaries <= 2:
                return
            embedding(FIRST["ple0"], 0, 3)
            boundary(2)
            if boundaries <= 3:
                return

            chunk0 = FIRST["fox"]
            features(chunk0, 0, new=4)
            pe.wait_ge(gates_z, 1)
            for t in range(T):
                for k in range(KD):
                    ts = slice(t * P, (t + 1) * P)
                    x = mm3(PS[:, 4, RANK * t:RANK * (t + 1)], XTH[:, k, ts], XTL[:, k, ts],
                            SWH[:, k, :], SWL[:, k, :], k == 0, k == KD - 1)
            x.then_inc(gates_logit, 1)
            pe.wait_ge(gates_z, 2)
            features(chunk0 + 4, 4)
            pe.wait_ge(evac, 8)
            features(chunk0 + 8, 0)
            pe.wait_ge(evac, 9)
            pe.wait_ge(gates_log, 1)
            for t in range(T):
                mm(PS[0:RANK, 4, :], LF[:, RANK * t:RANK * (t + 1)],
                   STEPS[:, 3 * P - t * P:3 * P - t * P + S], t == 0, t == T - 1)
            for u in range(T):
                for t in range(u + 1):
                    x = mm(PS[:, 5, RANK * u:RANK * (u + 1)], STEPS[:, 3 * P + (u - t) * P:3 * P + (u - t + 1) * P],
                           LF[:, RANK * t:RANK * (t + 1)], t == 0, t == u)
            x.then_inc(gates_sum, 1)
            pe.wait_ge(gates_rows, 2)
            features(chunk0 + 12, 4)
            pe.wait_ge(evac, 10)
            tokens(chunk0 + 16, 0)
            pe.wait_ge(evac, 11)
            tokens(chunk0 + 20, 4)

            pe.wait_ge(evac, E_FOX)
            qk(FOX0, 0)
            qk(FOX0 + 1, 0)
            for h in (FOX0, FOX0 + 1):
                attend_step(h, 0, FOX0 + 15)
            with pe.Fori(0, 3) as r:
                for h in range(FOX0 + 2, FOX0 + 6):
                    attend_step(h, r, FOX0 + 15)
            for h in (FOX0 + 14, FOX0 + 15):
                attend_step(h, 0, FOX0 + 15)
            pe.wait_ge(o_lo, 32)
            pe.wait_ge(o_hi, 32)
            block_end(3, "out1", "up1", "down1", 8, 8, 32, 32)
            if boundaries <= 4:
                return
            boundary(4)
            if boundaries <= 5:
                return
            embedding(FIRST["ple1"], 1, 6)
            boundary(5)
            if boundaries <= 6:
                return
            c = FIRST["gla"]
            features(c, 0, new=7)
            pe.wait_ge(gla_prep, 1)
            for t in range(T):
                for k in range(KD):
                    ts = slice(t * P, (t + 1) * P)
                    x = mm3(PS[:, 4, RANK * t:RANK * (t + 1)], XTH[:, k, ts], XTL[:, k, ts],
                            TWH[:, k, :], TWL[:, k, :], k == 0, k == KD - 1)
            x.then_inc(gla_small, 1)
            pe.wait_ge(gla_prep, 2)
            for t in range(T):
                x = pe.transpose(PS[0:RANK, 5, t * P:(t + 1) * P], PA[:, t, :], IDENT[:, :])
            x.then_inc(gla_small, 1)
            pe.wait_ge(gla_prep, 3)
            tokens(c + 4, 4)
            pe.wait_ge(evac, 14)
            for t in range(T):
                x = mm(PSF[:, 2 * P * t:2 * P * (t + 1)], PAT[0:RANK + 1, t * P:(t + 1) * P],
                       WG[:, :], True, True)
            x.then_inc(gla_small, 1)
            pe.wait_ge(gla_prep, 4)
            tokens(c + 8, 0)
            pe.wait_ge(evac, 15)
            pe.wait_ge(gla_prep, 6)
            for f in range(2):
                for t in range(T):
                    o = PS[:, 4 + f, t * P:(t + 1) * P]
                    mm(o, GLH[:, t, f * P:(f + 1) * P], CHUNKTRI_R[:, :], True, False)
                    x = mm(o, GLL[:, t, f * P:(f + 1) * P], CHUNKTRI_R[:, :], False, True)
            x.then_inc(gla_small, 1)
            pe.wait_ge(gla_prep, 7)
            features(c + 12, 4)
            pe.wait_ge(evac, 16)
            features(c + 16, 0)
            pe.wait_ge(evac, 17)
            features(c + 20, 4)
            pe.wait_ge(evac, 19)
            for t in range(T):
                pe.wait_ge(gla_ve, 3 * t + 1)
                for h in range(GLA_H):
                    rows, p = slice(DK * (h % 2), DK * (h % 2 + 1)), h // 2
                    mm3(PS[:, h % 2, P * p:P * (p + 1)], KIH[rows, p, :], KIL[rows, p, :],
                        QIH[rows, p, :], QIL[rows, p, :], True, True)
                for p in range(2):
                    x = pe.transpose(PS[:, 1, P * (p + 2):P * (p + 3)], KK[:, p, t * P:(t + 1) * P], IDENT[:, :])
                x.then_inc(gla_pe, 1)
                pe.wait_ge(gla_ve, 3 * t + 2)
                for e in range(2):
                    rows = slice(GCH * e, GCH * (e + 1))
                    for p in range(2):
                        w = slice(2 * DV * p, 2 * DV * (p + 1))
                        x = mm3(PS[:, 2 + e, w], KTH[rows, P * p:P * (p + 1)], KTL[rows, P * p:P * (p + 1)],
                                VH[rows, t, w], VL[rows, t, w], True, True)
                x.then_inc(gla_pe, 1)
                pe.wait_ge(gla_ve, 3 * t + 3)
                for p in range(2):
                    w = slice(2 * DV * p, 2 * DV * (p + 1))
                    for e in range(2):
                        mm3(PS[:, 4 + t, w], QEH[:, e, p, :], QEL[:, e, p, :],
                            STH[:, e, p, :], STL[:, e, p, :], e == 0, False)
                    for h in (2 * p, 2 * p + 1):
                        w = slice(DV * h, DV * (h + 1))
                        x = mm3(PS[:, 4 + t, w], SMH[:, w], SML[:, w], VH[:, t, w], VL[:, t, w],
                                False, h % 2 == 1)
                x.then_inc(gla_pe, 1)
            pe.wait_ge(gla_ve, 13)
            for f in range(GLA_H):
                for t in range(T):
                    x = pe.transpose(PS[:, f, t * P:(t + 1) * P], CV[:, t, f * P:(f + 1) * P], IDENT[:, :])
            x.then_inc(gla_pe, 1)
            pe.wait_ge(conv_lo, 1)
            pe.wait_ge(gla_ve, 14)
            outward(FIRST["out2"])
            boundary(6)
            if boundaries <= 7:
                return
            hidden(FIRST["ffn"], 11, 16, 8)
            down(FIRST["down2"], 22, 11, 16, 64)

        @block.vector
        def _(ve):
            own = Order(ve, ve_own)
            M, A, SUB, MAX, MIN = ALU.mult, ALU.add, ALU.subtract, ALU.max, ALU.min

            def spread(ap, n, at=1):
                shape = list(ap.shape)
                return ap.unsqueeze(at).to_broadcast(shape[:at] + [n] + shape[at:])

            ve.memset(EPS[:, 0:1], LN_EPS)
            ve.memset(EPS[:, 1:2], RMS_EPS)
            ve.wait_ge(const_landed, CONST_ALL)
            ve.tensor_copy(IDENT_R[:, :], IDENT[:, :])
            ve.tensor_copy(TRI_R[:, :], TRI)
            ve.tensor_copy(CHUNKTRI_R[:, :], CHUNKTRI[:, :])
            ve.tensor_scalar(NSINK[:, :], SINK[:, :], -1.0, None, M).then_inc(consts_made, 1)
            for j in range(4):
                w = slice(2 * j, 2 * j + 2)
                ve.wait_ge(xt_hi, j + 1)
                ve.tensor_tensor(XTL[:, w, :], XS[:, w, :], XTH[:, w, :].bitcast(F32), SUB).then_inc(xt_ready, 2)
            ve.wait_ge(proj, 1)
            ve.tensor_scalar(QM[:, :, 0:3 * P], PS[:, :, 0:3 * P], -1.0, None, M).then_inc(bias_out, 1)

            ve.wait_ge(chunk_used, FIRST["cq"])
            ve.tensor_scalar(QS[:, :, :], PS[:, 0:4, :], -HD ** -0.5, None, M).then_inc(evac, 1)
            ve.wait_ge(chunk_used, FIRST["ckv"])
            ve.tensor_copy(KS[:, :], PS[:, 0, :])
            ve.tensor_copy(CQ[:, :, 0:Q_LORA], PS[:, 4:8, 0:Q_LORA]).then_inc(evac, 1)
            ve.wait_ge(evac, 2)
            for t in range(T):
                ve.bn_stats(CBN[:, t, :], CQ[:, t, 0:Q_LORA])
            ve.wait_ge(chunk_used, FIRST["uq"])
            rope_k, rope_s = ROPET[HD:96, :], ROPET[96:P, :]
            ve.tensor_copy(VS[:, :, :], PS[:, 1:5, KV_LORA:384])
            ve.tensor_tensor(ROT[HD:96, 0, :], PS[HD:96, 5, :], rope_k, M)
            ve.tensor_tensor(ROT[HD:96, 1, :], PS[96:P, 5, :], rope_s, M)
            ve.tensor_copy(CQ[:, :, Q_LORA:], PS[:, 1:5, 0:KV_LORA]).then_inc(evac, 1)
            ve.wait_ge(evac, 3)
            ve.wait_ge(bias_landed, 16)
            ve.tensor_tensor(KM[HD:96, :, :], spread(ROT[HD:96, 0, :], MLA_H), spread(ROT[HD:96, 1, :], MLA_H), A)
            for t in range(T):
                x = ve.bn_stats(CBN[:, T + t, :], CQ[:, t, Q_LORA:])
            own(x)
            for j in range(8):
                x = ve.bn_aggr(CMV[:, j, :], CBN[:, j, :])
            own(x)
            own(ve.tensor_tensor(CMV[:, :, 0], CMV[:, :, 0], CMV[:, :, 0], M))
            ve.tensor_tensor(CMV[:, :, 1], CMV[:, :, 0], CMV[:, :, 1], A).then_inc(lat_sq, 1)
            ve.wait_ge(lat_std, 1)
            own(ve.reciprocal(CRS[:, :], CSTD[:, :]))
            for j in range(8):
                w = slice(0, Q_LORA) if j < T else slice(Q_LORA, Q_LORA + KV_LORA)
                x = ve.tensor_scalar(CQ[:, j % T, w], CQ[:, j % T, w], CRS[:, j:j + 1], None, M)
            x.then_inc(lat_normed, 1)
            for f in range(5):
                ve.wait_ge(lat_hi, f + 1)
                ve.scalar_tensor_tensor(CTL[:, f, :], PS[:, f, :], GAIN[:, f:f + 1],
                                        CTH[:, f, :].bitcast(F32), M, SUB).then_inc(lat_lo, 1)
            for half in range(2):
                ve.wait_ge(chunk_used, FIRST["uq"] + 2 + half)
                b, hs = slice(4 * half, 4 * half + 4), slice(4 * half, 4 * half + 4)
                ve.tensor_scalar(QM[0:HD, hs, :], PS[0:HD, b, :], -MLA_SCALE, None, M)
                ve.scalar_tensor_tensor(ROT[HD:96, :, :], PS[96:P, b, :], -MLA_SCALE, spread(rope_s, 4), M, M)
                own(ve.scalar_tensor_tensor(QM[HD:96, hs, :], PS[HD:96, b, :], -MLA_SCALE, spread(rope_k, 4), M, M))
                ve.tensor_tensor(QM[HD:96, hs, :], QM[HD:96, hs, :], ROT[HD:96, :, :], A).then_inc(evac, 1)
                if half == 0:
                    ve.wait_ge(evac, 4)
            ve.wait_ge(chunk_used, FIRST["vm"])
            for e in range(2):
                x = ve.tensor_copy(KM[0:HD, e::2, :], PS[HD * e:HD * (e + 1), 0:4, :])
            x.then_inc(evac, 1)
            ve.wait_ge(chunk_used, FIRST["out0"])
            ve.tensor_copy(VM[:, :, :], PS[:, 4:8, :]).then_inc(evac, 1)

            def sums(h, r):
                kind, s = kind_of(h), h % prob_slots(h)
                ve.wait_ge(expd, 4 * (h + 1) + 16 * r)
                if kind == "swa":
                    ve.wait_ge(sunk, h - 7)
                    own(ve.tensor_tensor(SM[:, s, :], SM[:, s, :], ES[:, s, :], A))
                own.mark(ve.reciprocal(SM[:, s, :], SM[:, s, :]))

            def mask(h, r):
                kind, s = kind_of(h), h % prob_slots(h)
                if h >= FOX0 + 4:
                    ve.wait_ge(turned, h - 3 + 4 * r)
                elif h >= 3:
                    ve.wait_ge(turned, min(h - 2, FOX0))
                if kind == "fox":
                    ve.wait_ge(bc_landed[h % 2], 16 * ((h - FOX0) // 2 + 1) + 32 * r)
                for i, in_bank in block_order(kind):
                    n = min(i + 1, 2) * P if kind == "swa" else (i + 1) * P
                    at = (WINDOW_AT if kind == "swa" else CAUSAL_AT)[i]
                    bank, col = (WINDOW_S if kind == "swa" else CAUSAL_S)[i]
                    init = 3e38
                    if kind == "mla":
                        other = MASKROW[:, S - n:S]
                    elif kind == "swa":
                        g = swa_head(h)
                        other, init = BIAS[:, g, 2 * P - n:2 * P], NSINK[:, g:g + 1]
                    else:
                        other = BC[:, h % 2, 0:n]
                    ve.wait_ge(scored, 4 * h + in_bank + 16 * r)
                    if kind == "fox":
                        own.stand()
                    x = ve.tensor_tensor_reduce(out=probs(h)[:, at:at + n], in0=PS[:, bank, col:col + n],
                                                in1=other, scale=1.0, scalar=init, op0=A, op1=MIN,
                                                accum_out=MN[:, s, i:i + 1])
                    x.then_inc(masked, 1)

            def exp_bias(h, r):
                if h >= FOX0:
                    s = h % prob_slots(h)
                    ve.wait_ge(masked, 4 * (h + 1) + 16 * r)
                    cq = CTOK[:, :, bass.ds(h - FOX0 + 4 * r, 1)]
                    nb, mn = (v[:, s, :].unsqueeze(2) for v in (NB, MN))
                    own(ve.tensor_tensor(nb, mn, cq, SUB))
                    ve.tensor_tensor(nb, nb, cq, A).then_inc(biased, 1)

            def normalise(h, r):
                kind, s = kind_of(h), h % prob_slots(h)
                own.settled()
                at = (WINDOW_AT + [896]) if kind == "swa" else (CAUSAL_AT + [1280])
                for i in range(T):
                    p = probs(h)[:, at[i]:at[i + 1]]
                    x = ve.tensor_scalar(p, p, SM[:, s, i:i + 1], None, M)
                x.then_inc(normed, 1)

            def probs_lo(h, r):
                n = 896 if kind_of(h) == "swa" else 1280
                ve.wait_ge(pt_hi, h + 1 + 4 * r)
                ve.tensor_tensor(PTL[:, h % 2, 0:n], PSF[:, 3 * S:3 * S + n],
                                 PTH[:, h % 2, 0:n].bitcast(F32), SUB).then_inc(pt_lo, 1)

            def out_lo(h, r):
                rows, tile = slice(HD * (h % 2), HD * (h % 2 + 1)), out_tile(h)
                ve.wait_ge(o_hi, h + 1 + 4 * r)
                ve.tensor_tensor(XTL[rows, tile + 2 * r, :], PS[rows, 6 + h % 2, :],
                                 XTH[rows, tile + 2 * r, :].bitcast(F32), SUB).then_inc(o_lo, 1)

            def attend_step(h, r, last):
                if h + 2 <= last:
                    mask(h + 2, r)
                if h not in (0, 1, FOX0, FOX0 + 1):
                    out_lo(h - 2, r)
                if h < last:
                    sums(h + 1, r)
                if h + 2 <= last:
                    exp_bias(h + 2, r)
                probs_lo(h, r)
                if h < last:
                    normalise(h + 1, r)
                if h == last:
                    out_lo(h - 1, r)
                    out_lo(h, r)

            mask(0, 0)
            mask(1, 0)
            sums(0, 0)
            normalise(0, 0)
            for h in range(16):
                attend_step(h, 0, 15)

            added = [0]

            def boundary(b, end):
                add, kind, n = BOUND[b]
                layer = kind == "layer"

                def residual(t):
                    if add:
                        if t < T - 1:
                            ve.wait_ge(tile_done, 3 * added[0] + t + 1)
                        else:
                            ve.wait_ge(chunk_used, end)
                        a = ALPHA if layer else 1.0
                        own(ve.scalar_tensor_tensor(X[:, t, :], X[:, t, :], a,
                                                    PSF[:, D * t:D * (t + 1)], M, A))
                    for j in range(2):
                        x = ve.bn_stats(BNS[:, t, 6 * j:6 * j + 6], X[:, t, UNIT * j:UNIT * (j + 1)])
                    own(x)
                    x = ve.bn_aggr(MV[:, t, :], BNS[:, t, :])
                    if not layer:
                        own(x)
                        x = ve.scalar_tensor_tensor(MV[:, t, 1:2], MV[:, t, 0:1], MV[:, t, 0:1],
                                                    MV[:, t, 1:2], M, A)
                    x.then_inc(var_ready, 1)

                def scale(t):
                    ve.wait_ge(std_ready, 4 * n + t + 1)
                    x = ve.reciprocal(RSTD[:, t:t + 1], STD[:, t:t + 1])
                    if layer:
                        own(x)
                        x = ve.tensor_scalar(NMR[:, t:t + 1], MV[:, t, 0:1], RSTD[:, t:t + 1], -1.0, M, M)
                    x.then_inc(scale_ready, 1)

                if kind:
                    for t in range(T):
                        residual(t)
                        if t:
                            scale(t - 1)
                    scale(T - 1)
                if b < 7:
                    for k in range(KD):
                        if kind:
                            ve.wait_ge(yt_ready, KD * n + k + 1)
                        else:
                            ve.wait_ge(yt_copied, 4 * (b + 1))
                        own(ve.tensor_copy(XTH[:, k, :], YT[:, k, :]))
                        ve.tensor_tensor(XTL[:, k, :], YT[:, k, :], XTH[:, k, :].bitcast(F32),
                                         SUB).then_inc(xt_ready, 1)
                if layer or b == 7:
                    ve.wait_ge(vec_landed, 32 * (n + 1) if layer else 144)
                    for t in range(T):
                        ve.wait_ge(centred, 4 * n + t + 1)
                        x = ve.tensor_tensor(X[:, t, :], X[:, t, :], G[:, 0, :], M)
                        if layer:
                            own(x)
                            x = ve.tensor_tensor(X[:, t, :], X[:, t, :], G[:, 1, :], A)
                        x.then_inc(y_ready, 1)
                    ve.wait_ge(y_ready, Y_BASE[b] + T)
                added[0] += add

            def squares(c, r0, g, r):
                ve.wait_ge(chunk_used, c + 4 * (g + 1) + 8 * r)
                h = HT[:, bass.ds(4 * g + 8 * r, 4), :]
                ve.tensor_scalar(h, PS[:, 4 * (g % 2):4 * (g % 2) + 4, :], 0.0, None, MAX).then_inc(relued, 1)
                ve.wait_ge(relued, r0 + g + 1 + 2 * r)
                own(ve.tensor_tensor(h, h, h, M))

            def hidden(c, r0):
                with ve.Fori(0, 3) as r:
                    own.extra = 2 * r
                    squares(c, r0, 0, r)
                    squares(c, r0, 1, r)
                own.extra = 0
                own.n += 4
                squares(c, r0, 6, 0)
                split_tile(0)
                split_tile(1)
                squares(c, r0, 7, 0)

            def gated_hidden(c, r0):
                def one(g, bank, r):
                    ve.wait_ge(gated, g + 1 + 2 * r)
                    h = HT[:, bass.ds(2 * g + 4 * r, 2), :]
                    ve.tensor_tensor(h, PS[:, bank + 2:bank + 4, :], GT[:, :, :], M).then_inc(relued, 1)

                one(0, 0, 0)
                with ve.Fori(0, 4) as r:
                    one(1, 4, r)
                    one(2, 0, r)
                one(9, 4, 0)
                ve.wait_ge(relued, r0 + 10)
                split_tile(0)
                split_tile(1)
                one(10, 0, 0)
                ve.wait_ge(relued, r0 + 11)

            def split_tile(k, r=0):
                h = HT[:, k + 2 * r, :]
                own(ve.tensor_copy(HSH[:, k % 2, :], h))
                ve.tensor_tensor(HSL[:, k % 2, :], h, HSH[:, k % 2, :].bitcast(F32), SUB).then_inc(hs_ready, 1)

            def split_hidden(c, k_tiles):
                with ve.Fori(0, k_tiles // 2 - 1) as r:
                    own.extra = 2 * r
                    for k in (2, 3):
                        ve.wait_ge(chunk_used, c + k - 1 + 2 * r)
                        split_tile(k, r)
                own.extra = 0
                own.n += k_tiles - 4

            def embedding(c, layer):
                ve.wait_ge(gate_landed, 32 * (layer + 1))
                own(ve.tensor_copy(EH[:, :, :], ER[:, :, :]))
                ve.tensor_tensor(EL[:, :, :], ER[:, :, :], EH[:, :, :].bitcast(F32), SUB).then_inc(emb_ready, 1)
                for half in range(2):
                    w = slice(UNIT * half, UNIT * (half + 1))
                    n = 8 * layer + 4 * half
                    ve.wait_ge(chunk_used, c + 5 * half + 4)
                    for t in range(T):
                        ve.tensor_tensor(SG[:, t, :], PS[:, t, :], BG[:, w], A).then_inc(emb_z, 1)
                    for t in range(T):
                        ve.wait_ge(emb_tile, n + t + 1)
                        ve.wait_ge(emb_sig, n + t + 1)
                        x = ve.tensor_tensor(SG[:, t, :], SG[:, t, :], PS[:, 4 + t, :], M)
                        if t < T - 1:
                            own(x)
                        else:
                            x.then_inc(emb_x, 1)
                            ve.wait_ge(emb_x, 2 * layer + half + 1)
                        x = ve.tensor_tensor(X[:, t, w], X[:, t, w], SG[:, t, :], A)
                        if half and layer == 0:
                            x.then_inc(y_ready, 1)
                    if half == 0 or layer:
                        own(x)
                if layer == 0:
                    ve.wait_ge(y_ready, Y_BASE[2] + T)

            boundary(0, FIRST["up0"])
            if boundaries <= 1:
                return
            hidden(FIRST["up0"], 0)
            split_hidden(FIRST["down0"], 32)
            boundary(1, FIRST["ple0"])
            if boundaries <= 2:
                return
            embedding(FIRST["ple0"], 0)
            boundary(2, 0)
            if boundaries <= 3:
                return

            ve.wait_ge(fox_landed, 48)
            own(ve.tensor_copy(SWH[:, :, :], SWR[:, :, :]))
            ve.tensor_tensor(SWL[:, :, :], SWR[:, :, :], SWH[:, :, :].bitcast(F32), SUB).then_inc(gates_z, 1)
            ve.wait_ge(gates_logit, 1)
            lz = LZ[:, :].rearrange("p (t h) -> p t h", t=T)
            own(ve.tensor_tensor(lz, PS[:, 4, 0:T * RANK].rearrange("p (t h) -> p t h", t=T),
                                 spread(BF[:, :], T), A))
            ve.scalar_tensor_tensor(LA[:, :], LZ[:, :], -1.0, LZ[:, :], M, MAX).then_inc(gates_z, 1)
            ve.wait_ge(gates_ln, 1)
            ve.scalar_tensor_tensor(LF[:, :], LZ[:, :], 0.0, LA[:, :], MIN, SUB).then_inc(gates_log, 1)
            c = FIRST["fox"]
            ve.wait_ge(chunk_used, c + 4)
            ve.tensor_scalar(QF[:, 0:4, :], PS[:, 0:4, :], -HD ** -0.5, None, M).then_inc(evac, 1)
            ve.wait_ge(chunk_used, c + 8)
            ve.tensor_scalar(QF[:, 4:8, :], PS[:, 4:8, :], -HD ** -0.5, None, M).then_inc(evac, 1)
            ve.wait_ge(gates_sum, 1)
            ve.tensor_copy(CC_ROWS[:, :], PS[0:RANK, 4, :]).then_inc(gates_rows, 1)
            ve.tensor_copy(CTOK[:, :, :].rearrange("p t h -> p (t h)"), PS[:, 5, 0:T * RANK]).then_inc(gates_rows, 1)
            ve.wait_ge(chunk_used, c + 12)
            ve.tensor_copy(KF[:, 0:4, :], PS[:, 0:4, :]).then_inc(evac, 1)
            ve.wait_ge(chunk_used, c + 16)
            ve.tensor_copy(KF[:, 4:8, :], PS[:, 4:8, :]).then_inc(evac, 1)
            for n in range(2):
                ve.wait_ge(chunk_used, c + 20 + 4 * n)
                ve.tensor_copy(VF[:, :, UNIT * n:UNIT * (n + 1)], PS[:, 4 * n:4 * n + 4, :]).then_inc(evac, 1)
            mask(FOX0, 0)
            mask(FOX0 + 1, 0)
            exp_bias(FOX0, 0)
            exp_bias(FOX0 + 1, 0)
            sums(FOX0, 0)
            normalise(FOX0, 0)
            for h in (FOX0, FOX0 + 1):
                attend_step(h, 0, FOX0 + 15)
            n = own.n
            with ve.Fori(0, 3) as r:
                own.extra = 24 * r
                for h in range(FOX0 + 2, FOX0 + 6):
                    attend_step(h, r, FOX0 + 15)
            own.extra = 0
            assert own.n - n == 24
            own.n += 48
            for h in (FOX0 + 14, FOX0 + 15):
                attend_step(h, 0, FOX0 + 15)
            boundary(3, FIRST["up1"])
            if boundaries <= 4:
                return
            hidden(FIRST["up1"], 8)
            split_hidden(FIRST["down1"], 32)
            boundary(4, FIRST["ple1"])
            if boundaries <= 5:
                return
            embedding(FIRST["ple1"], 1)
            boundary(5, 0)
            if boundaries <= 6:
                return

            c = FIRST["gla"]
            ve.wait_ge(x_turned, 24)
            ve.wait_ge(gla_const, 64)
            own(ve.tensor_copy(TWH[:, :, :], TWR[:, :, :]))
            ve.tensor_tensor(TWL[:, :, :], TWR[:, :, :], TWH[:, :, :].bitcast(F32), SUB).then_inc(gla_prep, 1)
            ve.memset(QEH[:, :, :, :].bitcast(F32), 0.0)
            ve.memset(QEL[:, :, :, :].bitcast(F32), 0.0)
            ve.memset(ST[:, :, :], 0.0)
            ve.memset(U[:, :, 0:2], 0.0)
            own(ve.memset(PAT[:, :], 1.0))
            ve.wait_ge(gla_small, 1)
            ve.tensor_copy(PA[:, :, :].rearrange("p t a -> p (t a)"), PS[:, 4, 0:T * RANK]).then_inc(gla_prep, 1)
            ve.wait_ge(gla_small, 2)
            ve.tensor_copy(PAT[0:RANK, :], PS[0:RANK, 5, :]).then_inc(gla_prep, 1)
            ve.wait_ge(chunk_used, c + 4)
            ve.tensor_scalar(QG[:, :, :], PS[:, 0:2, :], DK ** -0.5, None, M)
            ve.tensor_copy(KG[:, :, :], PS[:, 2:4, :]).then_inc(evac, 1)
            ve.wait_ge(gla_small, 3)
            gl = GL[:, :, :].rearrange("p t n -> p (t n)")
            ga = GA[:, :, :].rearrange("p t n -> p (t n)")
            own(ve.tensor_copy(gl, PSF[:, 0:T * 2 * P]))
            x = ve.scalar_tensor_tensor(ga, gl, -1.0, gl, M, MAX)
            x.then_inc(gla_prep, 1)
            ve.wait_ge(chunk_used, c + 8)
            own(ve.tensor_copy(VH[:, :, :], PS[:, 4:8, :]))
            ve.tensor_tensor(VL[:, :, :], PS[:, 4:8, :], VH[:, :, :].bitcast(F32), SUB).then_inc(evac, 1)
            ve.wait_ge(gla_act, 1)
            own(ve.scalar_tensor_tensor(gl, gl, 0.0, ga, MIN, SUB))
            own(ve.tensor_scalar(gl, gl, 1.0 / GATE_NORM, None, M))
            own(ve.tensor_copy(GLH[:, :, :], GL[:, :, :]))
            ve.tensor_tensor(GLL[:, :, :], GL[:, :, :], GLH[:, :, :].bitcast(F32), SUB).then_inc(gla_prep, 2)
            ve.wait_ge(chunk_used, c + 12)
            ve.tensor_copy(GG[:, :, :], PS[:, 0:4, :]).then_inc(evac, 1)
            ve.wait_ge(gla_small, 4)
            own(ve.tensor_copy(BT[:, :, :], PS[:, 4:6, :]))
            by_chunk = lambda v: v.rearrange("p f (n c) -> p f n c", c=GCH)
            ends = by_chunk(BT[:, :, :])[:, :, :, GCH - 1:GCH]
            ve.tensor_tensor(by_chunk(KK[:, :, :]), ends.to_broadcast([P, 2, NCH, GCH]),
                             by_chunk(BT[:, :, :]), SUB).then_inc(gla_prep, 1)
            ve.wait_ge(gla_act, 2)
            ve.tensor_tensor(QI[:, :, :], QI[:, :, :], QG[:, :, :], M)
            ve.tensor_tensor(KI[:, :, :], KI[:, :, :], KG[:, :, :], M)
            own(ve.tensor_tensor(KK[:, :, :], KK[:, :, :], KG[:, :, :], M))
            ve.wait_ge(chunk_used, c + 16)
            ve.tensor_copy(CB[:, :, :], PS[:, 4:8, :]).then_inc(evac, 1)
            ve.wait_ge(chunk_used, c + 20)
            ve.tensor_copy(CV[:, :, :], PS[:, 0:4, :]).then_inc(evac, 1)
            ve.wait_ge(evac, 18)
            ve.wait_ge(chunk_used, c + 24)
            ve.tensor_tensor(U[:, :, 2:S + 2], PS[:, 4:8, :], CV[:, :, :], M).then_inc(evac, 1)

            def tile_operands(t):
                w = slice(t * P, (t + 1) * P)
                if t:
                    ve.wait_ge(gla_pe, 3 * t)
                ve.tensor_copy(KIH[:, :, :], KI[:, :, w])
                own(ve.tensor_copy(QIH[:, :, :], QI[:, :, w]))
                ve.tensor_tensor(KIL[:, :, :], KI[:, :, w], KIH[:, :, :].bitcast(F32), SUB)
                own(ve.tensor_tensor(QIL[:, :, :], QI[:, :, w], QIH[:, :, :].bitcast(F32), SUB))
                for e in range(2):
                    k = slice(GCH * e, GCH * (e + 1))
                    ve.tensor_copy(QEH[:, e, :, k], QIH[:, :, k].bitcast(F32))
                    x = ve.tensor_copy(QEL[:, e, :, k], QIL[:, :, k].bitcast(F32))
                x.then_inc(gla_ve, 1)

            ve.wait_ge(evac, 19)
            tile_operands(0)
            for f in range(T):
                own(ve.tensor_scalar(CV[:, f, :], U[:, f, 0:S], CW[:, f, 0:1], None, M))
                for j in (1, 2):
                    own(ve.scalar_tensor_tensor(CV[:, f, :], U[:, f, j:j + S], CW[:, f, j:j + 1],
                                                CV[:, f, :], M, A))
            ve.tensor_tensor(CV[:, :, :], CV[:, :, :], CB[:, :, :], M).then_inc(gla_prep, 1)
            ve.wait_ge(conv_hi, 1)
            ve.tensor_tensor(XTL[:, 4:8, :], CV[:, :, :], XTH[:, 4:8, :].bitcast(F32), SUB).then_inc(conv_lo, 1)
            for t in range(T):
                if t:
                    tile_operands(t)
                ve.wait_ge(gla_pe, 3 * t + 1)
                causal = CHUNKTRI[:, :].unsqueeze(1).unsqueeze(1).to_broadcast([P, 2, 2, P])
                own(ve.tensor_tensor(SMF[:, :].rearrange("p (i j n) -> p i j n", i=2, j=2),
                                     PS[:, 0:2, 0:2 * P].rearrange("p j (i n) -> p i j n", i=2), causal, M))
                ve.tensor_copy(KTH[:, :], PS[:, 1, 2 * P:4 * P])
                own(ve.tensor_copy(SMH[:, :], SMF[:, :]))
                ve.tensor_tensor(KTL[:, :], PS[:, 1, 2 * P:4 * P], KTH[:, :].bitcast(F32), SUB)
                ve.tensor_tensor(SML[:, :], SMF[:, :], SMH[:, :].bitcast(F32), SUB).then_inc(gla_ve, 1)
                ve.wait_ge(gla_pe, 3 * t + 2)
                for e in range(2):
                    own(ve.tensor_copy(STH[:, e, :, :], ST[:, :, :]))
                    x = ve.tensor_tensor(STL[:, e, :, :], ST[:, :, :], STH[:, e, :, :].bitcast(F32), SUB)
                    if e:
                        x.then_inc(gla_ve, 1)
                        ve.wait_ge(gla_ve, 3 * t + 3)
                    else:
                        own(x)
                    for p in range(2):
                        for j in range(2):
                            rows, w = slice(DK * j, DK * (j + 1)), slice(DV * j, DV * (j + 1))
                            x = ve.scalar_tensor_tensor(
                                ST[rows, p, w], ST[rows, p, w], DEC[rows, p, 2 * t + e:2 * t + e + 1],
                                PS[rows, 2 + e, 2 * DV * p + DV * j:2 * DV * p + DV * (j + 1)], M, A)
                    own(x)
            ve.wait_ge(gla_pe, 12)
            own(ve.tensor_copy(CV[:, :, :], PS[:, 4:8, :]))
            for t in range(T):
                for h in range(GLA_H):
                    x = ve.bn_stats(OBN[:, 4 * t + h, :], CV[:, t, DV * h:DV * (h + 1)])
            own(x)
            for j in range(16):
                x = ve.bn_aggr(OMV[:, j, :], OBN[:, j, :])
            own(x)
            own(ve.tensor_tensor(OMV[:, :, 0], OMV[:, :, 0], OMV[:, :, 0], M))
            ve.tensor_tensor(OMV[:, :, 1], OMV[:, :, 0], OMV[:, :, 1], A).then_inc(gla_prep, 1)
            ve.wait_ge(gla_act, 4)
            own(ve.reciprocal(ORS[:, :], OSTD[:, :]))
            for t in range(T):
                for h in range(GLA_H):
                    w = slice(DV * h, DV * (h + 1))
                    x = ve.scalar_tensor_tensor(CV[:, t, w], CV[:, t, w], ORS[:, 4 * t + h:4 * t + h + 1],
                                                GN[:, :], M, M)
            own(x)
            ve.tensor_tensor(CV[:, :, :], CV[:, :, :], GG[:, :, :], M).then_inc(gla_ve, 1)
            ve.wait_ge(gla_act, 5)
            ve.tensor_tensor(XTL[:, 0:4, :], PS[:, 0:4, :], XTH[:, 0:4, :].bitcast(F32), SUB).then_inc(gla_ve, 1)
            boundary(6, FIRST["ffn"])
            if boundaries <= 7:
                return
            gated_hidden(FIRST["ffn"], 16)
            split_hidden(FIRST["down2"], 22)
            boundary(7, CHUNKS)

        @block.scalar
        def _(act):
            own = Order(act, act_own)
            F = ACT

            def load(o, i, done):
                act.dma_start(o, i).then_inc(done, 16)

            load(ONEHOT[:, :], d["onehot"], const_landed)
            load(REL[:, :], d["rel"], const_landed)
            load(XS[:, :, :], d["xt"], const_landed)
            load(IDENT[:, :], d["ident"], const_landed)
            load(MASKROW[:, :], d["maskrow"], const_landed)
            load(CHUNKTRI[:, :], d["chunktri"], const_landed)
            load(ROPET[:, :], d["rope"], const_landed)
            load(GAIN[:, :], d["gains"], const_landed)
            load(GAINS[:, :, :], d["gain_cols"], const_landed)
            load(BIASES[:, :, :], d["bias_cols"], const_landed)
            load(SINK[:, :], d["sinks"].to_broadcast([P, SWA_H]), const_landed)
            load(X[:, :, :], d["x"], const_landed)
            act.wait_ge(const_landed, CONST_ALL)
            for j in range(4):
                w = slice(2 * j, 2 * j + 2)
                act.copy(XTH[:, w, :], XS[:, w, :]).then_inc(xt_hi, 1)
            act.wait_ge(bias_out, 1)
            act.dma_start(d["bias_rows"], QM[:, :, 0:3 * P]).then_inc(bias_stored, 16)
            act.wait_ge(bias_stored, 16)
            load(BIAS[:, :, :], d["bias_skew"], bias_landed)
            act.wait_ge(lat_sq, 1)
            act.wait_ge(bias_landed, 16)
            act.activation(CSTD[:, :], CMV[:, :, 1], F.Sqrt, bias=EPS[:, 0:1]).then_inc(lat_std, 1)
            for f in range(5):
                act.wait_ge(lat_turned, f + 1)
                act.activation(CTH[:, f, :], PS[:, f, :], F.Copy, scale=GAIN[:, f:f + 1]).then_inc(lat_hi, 1)

            def exps(h, r):
                kind, s = kind_of(h), h % prob_slots(h)
                at = (WINDOW_AT + [896]) if kind == "swa" else (CAUSAL_AT + [1280])
                bias = NB if kind == "fox" else MN
                if kind == "fox":
                    act.wait_ge(biased, h + 1 - FOX0 + 4 * r)
                for done, (i, _) in enumerate(block_order(kind)):
                    if kind != "fox":
                        act.wait_ge(masked, 4 * h + done + 1)
                    p = probs(h)[:, at[i]:at[i + 1]]
                    act.activation(p, p, F.Exp, bias=bias[:, s, i:i + 1], scale=-1.0,
                                   accum_out=SM[:, s, i:i + 1]).then_inc(expd, 1)
                if kind == "swa":
                    g = swa_head(h)
                    act.activation(ES[:, s, :], MN[:, s, :], F.Exp, bias=SINK[:, g:g + 1]).then_inc(sunk, 1)

            def probs_hi(h, r):
                n = 896 if kind_of(h) == "swa" else 1280
                act.wait_ge(turned, h + 1 + 4 * r)
                if h >= 2:
                    act.wait_ge(o_ready, h - 1 + 4 * r)
                act.copy(PTH[:, h % 2, 0:n], PSF[:, 3 * S:3 * S + n]).then_inc(pt_hi, 1)

            def out_hi(h, r):
                rows, tile = slice(HD * (h % 2), HD * (h % 2 + 1)), out_tile(h)
                act.wait_ge(o_ready, h + 1 + 4 * r)
                act.copy(XTH[rows, tile + 2 * r, :], PS[rows, 6 + h % 2, :]).then_inc(o_hi, 1)

            def attend_step(h, r, last):
                if h not in (0, 1, FOX0, FOX0 + 1):
                    out_hi(h - 2, r)
                probs_hi(h, r)
                if h + 2 <= last:
                    exps(h + 2, r)
                if h == last:
                    out_hi(h - 1, r)
                    out_hi(h, r)

            exps(0, 0)
            exps(1, 0)
            for h in range(16):
                attend_step(h, 0, 15)

            def vectors(b):
                n = BOUND[b][2]
                load(G[:, 0, :], d["gain_rows"][n:n + 1, :].to_broadcast([P, D]), vec_landed)
                if BOUND[b][1] == "layer":
                    load(G[:, 1, :], d["bias_vecs"][n:n + 1, :].to_broadcast([P, D]), vec_landed)

            def boundary(b):
                add, kind, n = BOUND[b]
                layer = kind == "layer"

                def deviation(t):
                    act.wait_ge(var_ready, 4 * n + t + 1)
                    act.activation(STD[:, t:t + 1], MV[:, t, 1:2], F.Sqrt,
                                   bias=EPS[:, 0 if layer else 1:1 if layer else 2]).then_inc(std_ready, 1)

                def centre(t):
                    act.wait_ge(scale_ready, 4 * n + t + 1)
                    if layer:
                        x = act.activation(X[:, t, :], X[:, t, :], F.Identity, bias=NMR[:, t:t + 1],
                                           scale=RSTD[:, t:t + 1])
                    else:
                        x = act.activation(YN[:, t, :] if b < 7 else X[:, t, :], X[:, t, :], F.Copy,
                                           scale=RSTD[:, t:t + 1])
                    x.then_inc(centred, 1)

                def copy_out(t):
                    act.wait_ge(x_turned, 4 * b + t + 1)
                    act.copy(YT[:, :, t * P:(t + 1) * P],
                             PSF[:, D * t:D * (t + 1)].rearrange("p (k n) -> p k n", k=KD)).then_inc(yt_copied, 1)

                for t in range(T + 1):
                    if kind and t < T:
                        deviation(t)
                    if kind and t:
                        centre(t - 1)
                    if b < 7 and t >= 2:
                        copy_out(t - 2)
                if b < 7:
                    copy_out(T - 1)
                    if kind:
                        act.wait_ge(yt_copied, 4 * (b + 1))
                        for k in range(KD):
                            y = YT[:, k, :]
                            if layer:
                                x = act.activation(y, y, F.Identity, bias=BIASES[:, n, k:k + 1],
                                                   scale=GAINS[:, n, k:k + 1])
                            else:
                                x = act.activation(y, y, F.Copy, scale=GAINS[:, n, k:k + 1])
                            x.then_inc(yt_ready, 1)

            def embedding_inputs(layer, tiles_split):
                act.wait_ge(hs_ready, tiles_split)
                load(ER[:, :, :], d["pt"][layer], gate_landed)
                load(BG[:, :], d["gate_bias"][layer:layer + 1, :].to_broadcast([P, D]), gate_landed)

            def embedding(layer):
                for half in range(2):
                    for t in range(T):
                        act.wait_ge(emb_z, 8 * layer + 4 * half + t + 1)
                        act.activation(SG[:, t, :], SG[:, t, :], F.Sigmoid).then_inc(emb_sig, 1)

            act.wait_ge(o_lo, 16)
            vectors(0)
            boundary(0)
            if boundaries <= 1:
                return
            act.wait_ge(y_ready, 4)
            vectors(1)
            embedding_inputs(0, 32)
            boundary(1)
            if boundaries <= 2:
                return
            embedding(0)
            boundary(2)
            if boundaries <= 3:
                return
            act.wait_ge(xt_ready, 4 * KD)
            load(SWR[:, :, :], d["w_forget"], fox_landed)
            load(BF[:, :], d["b_forget"].to_broadcast([P, RANK]), fox_landed)
            load(STEPS[:, :], d["steps"], fox_landed)
            act.wait_ge(gates_z, 2)
            own(act.activation(LA[:, :], LA[:, :], F.Exp, scale=-1.0))
            act.activation(LA[:, :], LA[:, :], F.Ln, bias=1.0).then_inc(gates_ln, 1)
            act.wait_ge(gates_rows, 1)
            act.dma_start(d["gate_rows"], CC_ROWS[:, :]).then_inc(rows_stored, 16)
            exps(FOX0, 0)
            exps(FOX0 + 1, 0)
            for h in (FOX0, FOX0 + 1):
                attend_step(h, 0, FOX0 + 15)
            with act.Fori(0, 3) as r:
                for h in range(FOX0 + 2, FOX0 + 6):
                    attend_step(h, r, FOX0 + 15)
            for h in (FOX0 + 14, FOX0 + 15):
                attend_step(h, 0, FOX0 + 15)
            act.wait_ge(o_lo, 32)
            vectors(3)
            boundary(3)
            if boundaries <= 4:
                return
            act.wait_ge(y_ready, 16)
            vectors(4)
            embedding_inputs(1, 64)
            boundary(4)
            if boundaries <= 5:
                return
            embedding(1)
            boundary(5)
            if boundaries <= 6:
                return
            act.wait_ge(xt_ready, 7 * KD)
            load(TWR[:, :, :], d["w_gate"], gla_const)
            load(WG[:, :], d["w_gate_up"], gla_const)
            load(CW[:, :, :], d["conv_w"], gla_const)
            load(GN[:, :], d["gla_gain"].to_broadcast([P, DV]), gla_const)
            act.wait_ge(gla_prep, 4)
            own(act.activation(GA[:, :, :], GA[:, :, :], F.Exp, scale=-1.0))
            act.activation(GA[:, :, :], GA[:, :, :], F.Ln, bias=1.0).then_inc(gla_act, 1)
            act.wait_ge(gla_prep, 7)
            ends = BT[:, :, :].rearrange("p f (n c) -> p f n c", c=GCH)[:, :, :, GCH - 1]
            act.activation(QI[:, :, :], BT[:, :, :], F.Exp)
            act.activation(KI[:, :, :], BT[:, :, :], F.Exp, scale=-1.0)
            act.activation(DEC[:, :, :], ends, F.Exp)
            act.activation(KK[:, :, :], KK[:, :, :], F.Exp).then_inc(gla_act, 1)
            act.wait_ge(evac, 16)
            act.activation(GG[:, :, :], GG[:, :, :], F.Silu).then_inc(gla_act, 1)
            act.wait_ge(gla_prep, 8)
            act.copy(XTH[:, 4:8, :], CV[:, :, :]).then_inc(conv_hi, 1)
            act.wait_ge(gla_prep, 9)
            act.activation(OSTD[:, :], OMV[:, :, 1], F.Sqrt, bias=EPS[:, 1:2]).then_inc(gla_act, 1)
            act.wait_ge(gla_pe, 13)
            act.copy(XTH[:, 0:4, :], PS[:, 0:4, :]).then_inc(gla_act, 1)
            act.wait_ge(gla_ve, 14)
            boundary(6)
            if boundaries <= 7:
                return
            vectors(7)

            def gate(g, bank, r):
                if g:
                    act.wait_ge(relued, 16 + g + 2 * r)
                act.wait_ge(chunk_used, FIRST["ffn"] + 4 * (g + 1) + 8 * r)
                act.activation(GT[:, :, :], PS[:, bank:bank + 2, :], F.Silu).then_inc(gated, 1)

            gate(0, 0, 0)
            with act.Fori(0, 5) as r:
                gate(1, 4, r)
                gate(2, 0, r)
            boundary(7)


def units(w):
    r, n = w.shape
    return w.reshape(r // P, P, n // UNIT, UNIT).transpose(0, 2, 1, 3)


def by_group(w):
    return units(w).transpose(1, 0, 2, 3).reshape(-1, P, UNIT)


def by_row(w):
    return units(w).reshape(-1, P, UNIT)


def stream_of(i):
    w = i["ev_w_in"][0]
    c_q, c_kv, k_r, q_s, k_s, v_s = np.split(w, np.cumsum([Q_LORA, KV_LORA, ROPE, 512, P]), axis=1)
    swap = lambda v: np.concatenate([v[..., ROPE // 2:], v[..., :ROPE // 2]], -1)
    pairs = lambda v, ax: np.take(v, [j for p in range(4) for j in (p, p + 4)], axis=ax)
    q_s = pairs(q_s.reshape(D, SWA_H, HD), 1).reshape(D, 512)
    pad = np.zeros((D, 64), w.dtype)
    parts = [by_group(q_s), by_group(np.concatenate([c_q, k_s], 1)),
             by_group(np.concatenate([c_kv, v_s, k_r, swap(k_r), pad], 1))]
    uq = i["ev_w_uq"][0].reshape(Q_LORA, MLA_H, HD + ROPE)
    uq = np.concatenate([uq, swap(uq[..., HD:])], -1).reshape(Q_LORA, MLA_H * P)
    ukv = i["ev_w_ukv"][0].reshape(KV_LORA, MLA_H, 2, HD)
    parts += [by_group(uq), by_group(ukv[:, :, 0].reshape(KV_LORA, 512)),
              by_group(ukv[:, :, 1].reshape(KV_LORA, 512))]
    wo = i["ev_w_out"][0]
    wo = np.concatenate([wo[:512], pairs(wo[512:].reshape(SWA_H, HD, D), 0).reshape(512, D)], 0)

    def dense(layer):
        up, down = i["w_up"][layer], i["w_down"][layer]
        g, e = i["ple_w_gate"][layer], i["ple_w_proj"][layer]
        out = [by_group(up), by_row(down)]
        for half in range(2):
            w = slice(UNIT * half, UNIT * (half + 1))
            out += [by_group(g[:, w]), by_group(e[:, w])]
        return out

    parts += [by_row(wo)] + dense(0)
    parts += [by_group(i["od_w_in"][0][:, :3 * D]), by_row(i["od_w_out"][0])] + dense(1)
    w = i["w_in_2"][0]
    parts += [by_group(np.concatenate([w[:, :1536], w[:, 1552:]], 1)), by_row(i["w_out_2"][0])]
    gate, up = (i[n][0].reshape(D, D_FF2 // 256, 256) for n in ("w_ffn_gate_2", "w_ffn_up_2"))
    parts += [by_group(np.concatenate([gate, up], 2).reshape(D, 2 * D_FF2)), by_row(i["w_ffn_down_2"][0])]
    s = np.concatenate(parts, 0)
    return np.ascontiguousarray(s.reshape(CHUNKS, 2, P, UNIT).transpose(0, 2, 1, 3).reshape(CHUNKS, P, CHUNK))


def shape_constants():
    f = np.float32
    p, j = np.arange(P)[:, None], np.arange(P)[None, :]
    maskrow = np.zeros((P, S), f)
    maskrow[:, S - P:] = np.where(j > p, f(BIG), f(0))
    chunktri = ((p <= j) & (p // GCH == j // GCH)).astype(f)
    steps = (np.arange(7 * P)[None, :] - 3 * P >= p).astype(f)
    inv = (1.0 / (10000.0 ** (np.arange(0, ROPE, 2, dtype=f) / ROPE))).astype(f)
    ang = inv[:, None] * np.arange(S, dtype=f)[None, :]
    rope = np.zeros((P, S), f)
    rope[64:96] = np.tile(np.cos(ang), (2, 1))
    rope[96:128] = np.concatenate([-np.sin(ang), np.sin(ang)])
    dist = 2 * P - 1 - np.arange(3 * P)
    exact = BUCKETS // 2
    dd = np.maximum(dist, 1).astype(f)
    large = exact + (np.log(dd / f(exact)) / f(np.log(MAX_DIST / exact)) * f(BUCKETS - exact)).astype(np.int32)
    bucket = np.where(dist < exact, np.maximum(dist, 0), np.minimum(large, BUCKETS - 1))
    inside = (dist >= 0) & (dist < WINDOW)
    onehot = np.zeros((BUCKETS + 1, 3 * P), f)
    onehot[bucket[inside], np.nonzero(inside)[0]] = 1
    onehot[BUCKETS, ~inside] = 1
    return {"ident": np.eye(P, dtype=f), "maskrow": maskrow, "chunktri": chunktri, "steps": steps,
            "rope": rope, "onehot": onehot}


def kernel(**inputs):
    import concourse.bacc as bacc
    from concourse.bass_utils import run_bass_kernel_spmd

    i = {k: np.asarray(v) for k, v in inputs.items()}
    f = np.float32
    tiled = lambda w: np.ascontiguousarray(w.reshape(-1, P, w.shape[-1]).transpose(1, 0, 2))
    arrays = dict(shape_constants())
    arrays["stream"] = stream_of(i)
    arrays["x"] = tiled(i["x"][0])
    arrays["xt"] = tiled(i["x"][0].T)
    arrays["pt"] = np.stack([tiled(i["p"][layer, 0].T) for layer in range(DEPTH)])
    arrays["rel"] = np.concatenate([i["rel_bias"], np.full((1, SWA_H), -BIG, f)])
    arrays["sinks"] = i["ev_sinks"]
    arrays["gains"] = np.ascontiguousarray(
        np.concatenate([i["ev_q_norm"][0], i["ev_kv_norm"][0]]).reshape(5, P).T)
    arrays["gain_rows"] = np.stack([i["ln1_g"][0], i["ln2_g"][0], i["ln1_g"][1], i["ln2_g"][1],
                                    i["norm1_g_2"][0], i["norm2_g_2"][0], i["norm_f_g_2"]])
    arrays["bias_vecs"] = np.stack([i["ln1_b"][0], i["ln2_b"][0], i["ln1_b"][1], i["ln2_b"][1]])
    by_feature = lambda v: np.ascontiguousarray(v.reshape(-1, KD, P).transpose(2, 0, 1))
    arrays["gain_cols"] = by_feature(arrays["gain_rows"])
    arrays["bias_cols"] = by_feature(arrays["bias_vecs"])
    arrays["gate_bias"] = i["ple_b_gate"]
    arrays["w_forget"] = tiled(i["od_w_in"][0][:, 3 * D:])
    arrays["b_forget"] = i["od_b_f"]
    arrays["w_gate"] = tiled(i["w_in_2"][0][:, 1536:1552])
    arrays["w_gate_up"] = np.concatenate([i["w_gate_up_2"][0], i["b_gate_2"]])
    arrays["conv_w"] = np.ascontiguousarray(i["conv_w_2"][0].reshape(3, T, P).transpose(2, 1, 0))
    arrays["gla_gain"] = i["gla_norm_g_2"]
    nc = bacc.Bacc("TRN2", target_bir_lowering=False, num_devices=1)
    d = {n: nc.dram_tensor(n, a.shape, F32, kind="ExternalInput").ap() for n, a in arrays.items()}
    rows = nc.dram_tensor("bias_rows", (P, SWA_H, 3 * P), F32, kind="Internal").ap()
    d["bias_rows"] = rows
    pitch = SWA_H * 3 * P
    d["bias_skew"] = bass.AP(tensor=rows.tensor, offset=P - 1,
                             ap=[[pitch - 1, P], [3 * P, SWA_H], [1, 2 * P]])
    d["gate_rows"] = nc.dram_tensor("gate_rows", (RANK, S), F32, kind="Internal").ap()
    out = nc.dram_tensor("out", (P, T, D), F32, kind="ExternalOutput").ap()
    program(nc, d, out)
    r = run_bass_kernel_spmd(nc, [arrays], core_ids=[0])
    return np.ascontiguousarray(r.results[0]["out"].transpose(1, 0, 2)).reshape(1, S, D)
```

```python
from contextlib import ExitStack

import numpy as np

import concourse.bass as bass
from concourse import mybir

F32 = mybir.dt.float32
F32R = mybir.dt.float32r
ALU = mybir.AluOpType
ACT = mybir.ActivationFunctionType

P = 128
S = 512
T = S // P
D = 1024
KD = D // P
UNIT = 512
CHUNK = 2 * UNIT
RAW = 4
WS = 2
DEPTH = 2
ALPHA = (2 * DEPTH) ** 0.25
LN_EPS, RMS_EPS = 1e-5, 1e-6
BIG = 1e30
HD = 64
MLA_H, SWA_H, FOX_H = 8, 8, 16
ROPE = 32
MLA_SCALE = (HD + ROPE) ** -0.5
Q_LORA, KV_LORA = 384, 256
BUCKETS, MAX_DIST, WINDOW = 32, 128, 128
D_FF, D_FF2 = 4096, 2816
HT_TILES = D_FF // P
PLE_K = 2
GLA_H, DK, DV, GCH = 4, 64, 128, 64
NCH = S // GCH
RANK = 16
GATE_NORM = 16.0

STAGES = [("cq", 4), ("ckv", 4), ("qs", 4), ("uq", 3), ("kn", 1), ("vm", 1), ("out0", 8),
          ("up0", 32), ("down0", 32), ("ple0", 10),
          ("fox", 24), ("out1", 8), ("up1", 32), ("down1", 32), ("ple1", 10),
          ("gla", 24), ("out2", 8), ("ffn", 44), ("down2", 22)]
FIRST, CHUNKS = {}, 0
for _name, _n in STAGES:
    FIRST[_name] = CHUNKS
    CHUNKS += _n

CAUSAL_AT = [0, 128, 384, 768]
WINDOW_AT = [0, 128, 384, 640]
CAUSAL_S = [(0, 0), (2, 0), (0, 128), (1, 0)]
WINDOW_S = [(0, 0), (0, 128), (1, 0), (1, 256)]
CAUSAL_ORDER = [(3, 1), (0, 3), (2, 3), (1, 4)]
WINDOW_ORDER = [(0, 2), (1, 2), (2, 4), (3, 4)]
CAUSAL_T = [0, 512, 1024, 896]
WINDOW_T = [0, 256, 512, 768]


CONST_ALL = 16 * 10
E_FIRST = 6
E_FOX = 12
FOX0 = 16


def kind_of(h):
    return "mla" if h < MLA_H else "swa" if h < FOX0 else "fox"


def block_order(kind):
    return WINDOW_ORDER if kind == "swa" else CAUSAL_ORDER


def item_slot(h):
    return h % 2 if h < MLA_H else h // 2 % 2


def prob_slots(h):
    return 3 if h < FOX0 else 4


def staged_count(h):
    return 2 * h if h < MLA_H else 2 * (MLA_H + (h - MLA_H) // 2)


def swa_head(h):
    j = (h - MLA_H) // 2
    return j + 4 * (h % 2)


def out_tile(h):
    return h // 2 if h < FOX0 else (h - FOX0) // 2


class Order:

    def __init__(self, engine, sem):
        self.engine, self.sem, self.n, self.extra = engine, sem, 0, 0

    def __call__(self, instruction):
        self.n += 1
        instruction.then_inc(self.sem, 1)
        self.engine.wait_ge(self.sem, self.n + self.extra)

    def mark(self, instruction):
        self.n += 1
        instruction.then_inc(self.sem, 1)

    def settled(self):
        self.engine.wait_ge(self.sem, self.n + self.extra)

    def stand(self):
        self.n += 1
        self.engine.sem_inc(self.sem, 1)


def over_chunks(engine, a, b, body):
    n = (b - a) // RAW
    if n > 1:
        with engine.Fori(0, n) as i:
            for j in range(a, a + RAW):
                body(i, j)
    elif n:
        for j in range(a, a + RAW):
            body(0, j)
    for j in range(a + n * RAW, b):
        body(0, j)


def program(nc, d, out, stop=None):
    ctx = ExitStack()
    with ctx:
        def sb(name, shape, dt=F32, at=ctx):
            return at.enter_context(nc.sbuf_tensor(name, shape, dt))

        def sem(name):
            return ctx.enter_context(nc.semaphore(name))

        X = sb("X", [P, T, D])
        XTH = sb("XTH", [P, KD, S], F32R)
        XTL = sb("XTL", [P, KD, S], F32R)
        RW = sb("RW", [P, RAW, CHUNK])
        WH = sb("WH", [P, WS, CHUNK], F32R)
        WL = sb("WL", [P, WS, CHUNK], F32R)
        IDENT = sb("IDENT", [P, P])
        MASKROW = sb("MASKROW", [P, S])
        CHUNKTRI = sb("CHUNKTRI", [P, P])
        IDENT_R = sb("IDENT_R", [P, P], F32R)
        TRI_R = sb("TRI_R", [P, P], F32R)
        CHUNKTRI_R = sb("CHUNKTRI_R", [P, P], F32R)
        EPS = sb("EPS", [P, 2])
        GAINS = sb("GAINS", [P, 7, KD])
        BIASES = sb("BIASES", [P, 4, KD])
        ONE = sb("ONE", [P, 1])
        MV = sb("MV", [P, T, 2])
        BNS = sb("BNS", [P, T, 12])
        STD = sb("STD", [P, T])
        RSTD = sb("RSTD", [P, T])
        NMR = sb("NMR", [P, T])
        MN = sb("MN", [P, 4, T])
        SM = sb("SM", [P, 4, T])
        ES = sb("ES", [P, 4, T])
        NB = sb("NB", [P, 4, T])
        PS = ctx.enter_context(nc.psum_tensor("PS", [P, 8, S], F32))
        PSF = PS[:, :, :].rearrange("p b n -> p (b n)")
        TRI = MASKROW[:, S - P:S]

        prepare = ExitStack()
        XS = sb("XS", [P, KD, S], at=prepare)
        CQ = sb("CQ", [P, T, Q_LORA + KV_LORA], at=prepare)
        CTH = sb("CTH", [P, 5, S], F32R, at=prepare)
        CTL = sb("CTL", [P, 5, S], F32R, at=prepare)
        ROT = sb("ROT", [P, 4, S], at=prepare)
        ONEHOT = sb("ONEHOT", [BUCKETS + 1, 3 * P], at=prepare)
        REL = sb("REL", [BUCKETS + 1, SWA_H], at=prepare)
        ROPET = sb("ROPET", [P, S], at=prepare)
        prepare.close()
        gates = ExitStack()
        STEPS = sb("STEPS", [P, 7 * P], at=gates)
        SWR = sb("SWR", [P, KD, RANK], at=gates)
        SWH = sb("SWH", [P, KD, P], F32R, at=gates)
        SWL = sb("SWL", [P, KD, P], F32R, at=gates)
        ZT = sb("ZT", [RANK, S], at=gates)
        BF = sb("BF", [P, RANK], at=gates)
        LZ = sb("LZ", [P, T * RANK], at=gates)
        LA = sb("LA", [P, T * RANK], at=gates)
        LF = sb("LF", [P, T * RANK], at=gates)
        gates.close()
        attend = ExitStack()
        AQH = sb("AQH", [P, 2, S], F32R, at=attend)
        AQL = sb("AQL", [P, 2, S], F32R, at=attend)
        AKH = sb("AKH", [P, 2, S], F32R, at=attend)
        AKL = sb("AKL", [P, 2, S], F32R, at=attend)
        AVH = sb("AVH", [P, 2, T, P], F32R, at=attend)
        AVL = sb("AVL", [P, 2, T, P], F32R, at=attend)
        PTH = sb("PTH", [P, 2, 1280], F32R, at=attend)
        PTL = sb("PTL", [P, 2, 1280], F32R, at=attend)
        first = ExitStack()
        PB1 = sb("PB1", [P, 3, 1280], at=first)
        QM = sb("QM", [P, MLA_H, S], at=first)
        KM = sb("KM", [P, MLA_H, S], at=first)
        VM = sb("VM", [P, T, 512], at=first)
        QS = sb("QS", [P, T, S], at=first)
        KS = sb("KS", [P, S], at=first)
        VS = sb("VS", [P, T, P], at=first)
        BIAS = sb("BIAS", [P, SWA_H, 2 * P], at=first)
        GAIN = sb("GAIN", [P, 5], at=first)
        SINK = sb("SINK", [P, SWA_H], at=first)
        NSINK = sb("NSINK", [P, SWA_H], at=first)
        CMV = sb("CMV", [P, 8, 2], at=first)
        CBN = sb("CBN", [P, 8, 6], at=first)
        CSTD = sb("CSTD", [P, 8], at=first)
        CRS = sb("CRS", [P, 8], at=first)
        first.close()
        second = ExitStack()
        QF = sb("QF", [P, KD, S], at=second)
        KF = sb("KF", [P, KD, S], at=second)
        VF = sb("VF", [P, T, D], at=second)
        PB2 = sb("PB2", [P, 4, 1280], at=second)
        BC = sb("BC", [P, 2, S], at=second)
        CC_ROWS = sb("CC_ROWS", [RANK, S], at=second)
        CTOK = sb("CTOK", [P, T, RANK], at=second)
        second.close()
        attend.close()
        dense = ExitStack()
        G = sb("G", [P, 2, D], at=dense)
        BG = sb("BG", [P, D], at=dense)
        HT = sb("HT", [P, HT_TILES, S], at=dense)
        HSH = sb("HSH", [P, 2, S], F32R, at=dense)
        HSL = sb("HSL", [P, 2, S], F32R, at=dense)
        GT = sb("GT", [P, 2, S], at=dense)
        YN = HT[:, 16:24, :].rearrange("p (t k) n -> p t (k n)", t=T)
        YT = HT[:, 24:32, :]
        dense.close()
        embed = ExitStack()
        _keep = sb("KEEP_DENSE", [P, 3, D], at=embed)
        SG = sb("SG", [P, T, S], at=embed)
        ER = sb("ER", [P, PLE_K, S], at=embed)
        EH = sb("EH", [P, PLE_K, S], F32R, at=embed)
        EL = sb("EL", [P, PLE_K, S], F32R, at=embed)
        embed.close()
        third = ExitStack()
        QK = sb("QK", [P, 4, S], at=third)
        QG, KG = QK[:, 0:2, :], QK[:, 2:4, :]
        VH = sb("VH", [P, T, 512], F32R, at=third)
        VL = sb("VL", [P, T, 512], F32R, at=third)
        GG = sb("GG", [P, T, 512], at=third)
        OT = sb("OT", [P, T, 512], at=third)
        CW = sb("CW", [P, T, 3], at=third)
        U = sb("U", [P, T, S + 2], at=third)
        CV = sb("CV", [P, T, S], at=third)
        TWR = sb("TWR", [P, KD, RANK], at=third)
        PAT = sb("PAT", [32, S], at=third)
        WG = sb("WG", [RANK + 1, 2 * P], at=third)
        BT = sb("BT", [P, 2, S], at=third)
        QI = sb("QI", [P, 2, S], at=third)
        KI = sb("KI", [P, 2, S], at=third)
        KK = sb("KK", [P, 2, S], at=third)
        QIH = sb("QIH", [P, 2, P], F32R, at=third)
        QIL = sb("QIL", [P, 2, P], F32R, at=third)
        QEH = sb("QEH", [P, 2, 2, P], F32R, at=third)
        QEL = sb("QEL", [P, 2, 2, P], F32R, at=third)
        KIH = sb("KIH", [P, 2, P], F32R, at=third)
        KIL = sb("KIL", [P, 2, P], F32R, at=third)
        SMF = sb("SMF", [P, 512], at=third)
        SMH = sb("SMH", [P, 512], F32R, at=third)
        SML = sb("SML", [P, 512], F32R, at=third)
        KTH = sb("KTH", [P, 2 * P], F32R, at=third)
        KTL = sb("KTL", [P, 2 * P], F32R, at=third)
        DEC = sb("DEC", [P, 2, NCH], at=third)
        ST = sb("ST", [P, 2, 2 * DV], at=third)
        STH = sb("STH", [P, 2, 2, 2 * DV], F32R, at=third)
        STL = sb("STL", [P, 2, 2, 2 * DV], F32R, at=third)
        GN = sb("GN", [P, DV], at=third)
        OBN = sb("OBN", [P, GLA_H, 6], at=third)
        OMV = sb("OMV", [P, GLA_H, 2], at=third)
        OSTD = sb("OSTD", [P, GLA_H], at=third)
        ORS = sb("ORS", [P, GLA_H], at=third)
        decays = ExitStack()
        GL = sb("GL", [P, T, 2 * P], at=decays)
        GA = sb("GA", [P, T, 2 * P], at=decays)
        GLH = sb("GLH", [P, T, 2 * P], F32R, at=decays)
        GLL = sb("GLL", [P, T, 2 * P], F32R, at=decays)
        decays.close()
        narrow = ExitStack()
        _gl_ga = sb("KEEP_GL_GA", [P, 2 * T, 2 * P], at=narrow)
        TWH = sb("TWH", [P, KD, P], F32R, at=narrow)
        TWL = sb("TWL", [P, KD, P], F32R, at=narrow)
        narrow.close()
        OH = sb("OH", [P, 4, S], F32R, at=third)
        OL = sb("OL", [P, 4, S], F32R, at=third)
        third.close()

        def probs(h):
            return (PB1 if h < FOX0 else PB2)[:, h % prob_slots(h), :]

        landed = [sem(f"raw_landed{j}") for j in range(RAW)]
        hi_split = sem("hi_split")
        lo_split = sem("lo_split")
        chunk_used = sem("chunk_used")
        const_landed = sem("const_landed")
        xs_landed = [sem(f"first_input_landed{j}") for j in range(4)]
        x_landed = sem("residual_landed")
        vec_landed = sem("vec_landed")
        gate_landed = sem("gate_landed")
        bias_out = sem("bias_out")
        bias_stored = sem("bias_stored")
        bias_landed = sem("bias_landed")
        consts_made = sem("consts_made")
        xt_hi = sem("xt_hi")
        xt_ready = sem("xt_ready")
        yt_copied = sem("yt_copied")
        yt_ready = sem("yt_ready")
        bias_made = sem("bias_made")
        evac = sem("evacuated")
        lat_sq = sem("latent_squares")
        lat_std = sem("latent_std")
        lat_normed = sem("latent_normed")
        lat_turned = sem("latent_turned")
        lat_hi = sem("latent_hi")
        lat_lo = sem("latent_lo")
        plain_out = sem("plain_out")
        first_staged = sem("first_staged")
        staged = sem("staged")
        vstaged = sem("values_staged")
        scored = sem("scored")
        masked = sem("masked")
        sunk = sem("sinks_exp")
        biased = sem("exp_biases")
        expd = sem("exponentials")
        summed = sem("exp_sums")
        normed = sem("normalised")
        last_normed = sem("last_normalised")
        turned = sem("probs_turned")
        pt_hi = sem("probs_hi")
        pt_lo = sem("probs_lo")
        o_ready = sem("head_out")
        o_hi = sem("head_out_hi")
        o_lo = sem("head_out_lo")
        bc_landed = [sem(f"bc_landed{j}") for j in range(2)]
        gates_logit = sem("fgate_logits")
        gates_ln = sem("fgate_ln")
        gates_z = sem("fgate_z")
        gates_log = sem("fgate_log")
        gates_sum = sem("fgate_sums")
        gates_rows = sem("fgate_rows")
        rows_stored = sem("fgate_rows_stored")
        fox_landed = sem("fgate_weights_landed")
        tile_done = sem("tile_done")
        var_ready = sem("var_ready")
        std_ready = sem("std_ready")
        scale_ready = sem("scale_ready")
        centred = sem("centred")
        last_centred = sem("last_centred")
        y_ready = sem("y_ready")
        x_turned = sem("x_turned")
        gated = sem("gated")
        relued = sem("hidden_out")
        hs_ready = sem("hidden_ready")
        emb_ready = sem("emb_ready")
        emb_tile = sem("emb_tile")
        emb_z = sem("emb_z")
        emb_sig = sem("emb_sig")
        emb_x = sem("emb_x")
        gla_const = sem("gla_landed")
        gla_small = sem("gla_small")
        gla_prep = sem("gla_prep")
        gla_act = sem("gla_act")
        mix_out = sem("mix_out")
        gla_ops = sem("gla_operands")
        gla_scored = sem("gla_scored")
        gla_cut = sem("gla_cut")
        gla_kv = sem("gla_kv")
        gla_states = sem("gla_states")
        gla_out = sem("gla_out")
        out_copied = sem("out_copied")
        out_sq = sem("out_squares")
        out_std = sem("out_std")
        out_gated = sem("out_gated")
        out_turned = sem("out_turned")
        gla_hi = sem("gla_hi")
        out_cut = sem("out_cut")
        conv_done = sem("conv_done")
        conv_hi = sem("conv_hi")
        conv_lo = sem("conv_lo")
        out_stored = sem("out_stored")
        act_own = sem("act_own")
        ve_own = sem("ve_own")
        pool_own = sem("pool_own")

        block = ctx.enter_context(nc.Block())
        boundaries = 8 if stop is None else stop + 1

        BOUND = [(True, "layer", 0), (True, "layer", 1), (False, None, None), (True, "layer", 2),
                 (True, "layer", 3), (False, "rms", 4), (True, "rms", 5), (True, "rms", 6)]
        NORMS = [b for b in range(8) if BOUND[b][1]]
        Y_BASE = [0, 4, 8, 12, 16, 20, 20, 20]

        def fox_heads(engine, body):
            for h in (FOX0, FOX0 + 1):
                body(h, 0)
            with engine.Fori(0, 3) as r:
                for h in range(FOX0 + 2, FOX0 + 6):
                    body(h, r)
            for h in (FOX0 + 14, FOX0 + 15):
                body(h, 0)

        @block.sync
        def _(sp):
            def load(i, j):
                if j >= RAW:
                    sp.wait_ge(lo_split, j - RAW + 1 + RAW * i)
                sp.dma_start(RW[:, j % RAW, :], d["stream"][RAW * i + j]).then_inc(landed[j % RAW], 16)

            for j in range(RAW):
                load(0, j)
            ends = [FIRST["out0"], FIRST["up0"], FIRST["ple0"], FIRST["fox"], FIRST["up1"], FIRST["ple1"],
                    FIRST["gla"], FIRST["ffn"], CHUNKS]
            last = ends[boundaries] if boundaries < 8 else CHUNKS
            cut = FIRST["out1"] + RAW
            over_chunks(sp, RAW, min(cut, last), load)
            if boundaries > 3:
                def load_row(h, r):
                    if h == FOX0:
                        sp.wait_ge(rows_stored, 16)
                    if h >= FOX0 + 2:
                        sp.wait_ge(masked, 4 * (h - 1) + 16 * r)
                    src = d["gate_rows"][bass.ds(h - FOX0 + 4 * r, 1), :].to_broadcast([P, S])
                    sp.dma_start(BC[:, h % 2, :], src).then_inc(bc_landed[h % 2], 16)

                fox_heads(sp, load_row)
                over_chunks(sp, cut, last, load)
            if boundaries == 8:
                for t in range(T):
                    sp.wait_ge(y_ready, Y_BASE[7] + t + 1)
                    sp.dma_start(out[:, t, :], X[:, t, :]).then_inc(out_stored, 16)
                sp.wait_ge(out_stored, 16 * T)
            if stop is not None:
                if boundaries in (2, 5):
                    sp.wait_ge(gate_landed, 32 if boundaries == 2 else 64)
                sp.wait_ge(y_ready, Y_BASE[boundaries])
                sp.wait_ge(xt_ready, KD * (boundaries + 1))
                sp.wait_ge(centred, 3 * sum(b < boundaries for b in NORMS))
                sp.dma_start(out, X[:, :, :]).then_inc(out_stored, 16)
                sp.wait_ge(out_stored, 16)

        @block.gpsimd
        def _(pool):
            own = Order(pool, pool_own)

            def cut(i, j):
                pool.wait_ge(landed[j % RAW], 16 * (j // RAW + 1) + 16 * i)
                if j >= WS:
                    pool.wait_ge(chunk_used, j - WS + 1 + RAW * i)
                pool.sem_inc(hi_split, 1)
                pool.tensor_scalar(WH[:, j % WS, :], RW[:, j % RAW, :], 1.0, 1.0,
                                   ALU.mult, ALU.mult).then_inc(hi_split, 1)
                pool.wait_ge(hi_split, 2 * (j + 1) + 2 * RAW * i)
                pool.tensor_tensor(WL[:, j % WS, :], RW[:, j % RAW, :], WH[:, j % WS, :].bitcast(F32),
                                   ALU.subtract).then_inc(lo_split, 1)

            def stage(hi, lo, src, done):
                own(pool.tensor_scalar(hi, src, 1.0, 1.0, ALU.mult, ALU.mult))
                pool.tensor_tensor(lo, src, hi.bitcast(F32), ALU.subtract).then_inc(done, 1)

            def stage_looped(hi, lo, src, done):
                own.stand()
                own(pool.tensor_tensor(hi, src, ONE[:, 0:1].to_broadcast([P, S]), ALU.mult))
                own.stand()
                pool.tensor_tensor(lo, src, hi.bitcast(F32), ALU.subtract).then_inc(done, 1)

            def stage_mla(h):
                s = h % 2
                stage(AQH[0:96, s, :], AQL[0:96, s, :], QM[0:96, h, :], staged)
                stage(AKH[0:96, s, :], AKL[0:96, s, :], KM[0:96, h, :], staged)

            def stage_pair(s, q, k):
                stage(AQH[:, s, :], AQL[:, s, :], q, staged)
                stage(AKH[:, s, :], AKL[:, s, :], k, staged)

            def stage_values(s, v):
                stage(AVH[:, s, :, :], AVL[:, s, :, :], v, vstaged)

            own(pool.memset(ONE[:, :], 1.0))
            for j in range(RAW):
                cut(0, j)
            over_chunks(pool, RAW, FIRST["out0"] + WS - 1, cut)
            pool.wait_ge(plain_out, 4)
            pool.wait_ge(evac, 5)
            pool.wait_ge(first_staged, 1)
            stage_mla(1)
            pool.wait_ge(evac, E_FIRST)
            stage_values(0, VM[:, :, 0:P])
            for h in range(16):
                if h % 2 == 0 and h >= 6 and h < 14:
                    pool.wait_ge(scored, 4 * (h + 1) if h == 6 else 4 * h)
                    stage_pair(h // 2 % 2 ^ 1, QS[:, (h - 6) // 2, :], KS[:, :])
                elif h < 6:
                    pool.wait_ge(scored, 4 * (h + 1))
                    stage_mla(h + 2)
                if h % 2 == 0 and h >= 2:
                    if h >= 4:
                        pool.wait_ge(o_ready, h - 2)
                    p = h // 2
                    stage_values(p % 2, VM[:, :, p * P:(p + 1) * P] if p < 4 else VS[:, :, :])
            if boundaries <= 3:
                over_chunks(pool, FIRST["out0"] + WS - 1,
                            [0, FIRST["up0"], FIRST["ple0"], FIRST["fox"]][boundaries], cut)
                return
            over_chunks(pool, FIRST["out0"] + WS - 1, FIRST["out1"] + WS - 1, cut)
            pool.wait_ge(evac, E_FOX - 2)
            stage_pair(0, QF[:, 0, :], KF[:, 0, :])
            pool.wait_ge(evac, E_FOX)
            stage_values(0, VF[:, :, 0:P])

            def fox_stage(h, r):
                if h % 2 == 0 and h < FOX0 + 14:
                    n = (h + 2 - FOX0) // 2
                    if h > FOX0:
                        pool.wait_ge(scored, 4 * h + 16 * r)
                    s = n % 2
                    stage_looped(AQH[:, s, :], AQL[:, s, :], QF[:, n + 2 * r, :], staged)
                    stage_looped(AKH[:, s, :], AKL[:, s, :], KF[:, n + 2 * r, :], staged)
                if h % 2 == 0 and h > FOX0:
                    pool.wait_ge(o_ready, h - 2 + 4 * r)
                    n = (h - FOX0) // 2
                    s, v = n % 2, VF[:, :, bass.ds(n * P + 2 * P * r, P)]
                    own.stand()
                    own(pool.tensor_tensor(AVH[:, s, :, :], v, ONE[:, 0:1].unsqueeze(1).to_broadcast([P, T, P]), ALU.mult))
                    own.stand()
                    pool.tensor_tensor(AVL[:, s, :, :], v, AVH[:, s, :, :].bitcast(F32), ALU.subtract).then_inc(vstaged, 1)

            for h in (FOX0, FOX0 + 1):
                fox_stage(h, 0)
            n1 = own.n
            with pool.Fori(0, 3) as r:
                own.extra = 18 * r
                for h in range(FOX0 + 2, FOX0 + 6):
                    fox_stage(h, r)
            own.extra = 0
            assert own.n == n1 + 18
            own.n += 36
            for h in (FOX0 + 14, FOX0 + 15):
                fox_stage(h, 0)
            last = [FIRST["up1"], FIRST["ple1"], FIRST["gla"], FIRST["ffn"], CHUNKS][boundaries - 4]
            over_chunks(pool, FIRST["out1"] + WS - 1, last, cut)

        @block.tensor
        def _(pe):
            def mm(o, a, b, start, stop):
                return pe.matmul(o, a, b, start=start, stop=stop)

            def mm3(o, ah, al, bh, bl, start, stop):
                mm(o, ah, bh, start, False)
                mm(o, ah, bl, False, False)
                return mm(o, al, bh, False, stop)

            def chunk(c, r=0, ready=True):
                if ready:
                    pe.wait_ge(lo_split, c + 1 + r)

            def features(c, bank, r=0, new=0, freed=None, steps=None):
                columns, k_tiles = (0, P, 2 * P, 3 * P), KD
                for k in range(k_tiles):
                    cc, u = c + k // 2, UNIT * (k % 2)
                    if new:
                        pe.wait_ge(xt_ready, KD * (new - 1) + k + 1)
                    if k % 2 == 0:
                        chunk(cc, r)
                    for m, col in enumerate(columns):
                        if freed is not None and k == 0:
                            pe.wait_ge(mix_out, freed + m + 1)
                        w = slice(u + col, u + col + P)
                        x = mm3(PS[:, bank + m, :], WH[:, cc % WS, w], WL[:, cc % WS, w],
                                XTH[:, k, :], XTL[:, k, :], k == 0, k == k_tiles - 1)
                    if k % 2:
                        x.then_inc(chunk_used, 1)
                        if steps:
                            for step, t in steps[k // 2]:
                                step(t)

            def tokens(c, bank, h=XTH, l=XTL, k_tiles=KD, new=0, steps=None):
                for k in range(k_tiles):
                    cc, u = c + k // 2, UNIT * (k % 2)
                    if new:
                        pe.wait_ge(xt_ready, KD * (new - 1) + k + 1)
                    if k % 2 == 0:
                        chunk(cc)
                    for t in range(T):
                        ts = slice(t * P, (t + 1) * P)
                        w = slice(u, u + UNIT)
                        x = mm3(PS[:, bank + t, :], h[:, k, ts], l[:, k, ts],
                                WH[:, cc % WS, w], WL[:, cc % WS, w], k == 0, k == k_tiles - 1)
                    if k % 2:
                        x.then_inc(chunk_used, 1)
                        if steps:
                            for step, t in steps[k // 2]:
                                step(t)

            def wide(c, r, h, l, first, order=(0, 1, 2, 3), late=None):
                chunk(c, r)
                for t in order:
                    if late and t == order[2]:
                        pe.wait_ge(*late)
                    x = wide_tile(t, c, h, l, first, False)
                x.then_inc(chunk_used, 1)

            def wide_tile(t, c, h, l, first, last):
                ts = slice(t * P, (t + 1) * P)
                for n in range(2):
                    w = slice(UNIT * n, UNIT * (n + 1))
                    x = mm3(PS[:, 2 * t + n, :], h[:, ts], l[:, ts],
                            WH[:, c % WS, w], WL[:, c % WS, w], first, last)
                return x

            def wide_end(c, a, b, parts_ready=None):
                chunk(c)
                for t in (0, 1):
                    wide_tile(t, c, *a, False, False)
                if parts_ready:
                    pe.wait_ge(hs_ready, parts_ready)
                chunk(c + 1)
                for t in range(T):
                    if t >= 2:
                        wide_tile(t, c, *a, False, False)
                    x = wide_tile(t, c + 1, *b, False, True)
                    x.then_inc(*((tile_done, 1) if t < T - 1 else (chunk_used, 2)))

            def outward(c, heads):
                for k in range(KD - 2):
                    wide(c + k, 0, XTH[:, k, :], XTL[:, k, :], k == 0,
                         late=(o_lo, heads) if k == 0 else None)
                wide_end(c + KD - 2, *((XTH[:, k, :], XTL[:, k, :]) for k in (KD - 2, KD - 1)))

            def input_ready(n):
                pe.wait_ge(xt_ready, KD * n)

            def qk(h, r):
                kind, s = kind_of(h), item_slot(h)
                if h:
                    pe.wait_ge(staged, staged_count(h) + (4 * r if h >= FOX0 else 0))
                else:
                    pe.wait_ge(first_staged, 2)
                if h:
                    pe.wait_ge(masked, 4 * h + 16 * r)
                a = 0 if kind == "mla" else HD * (h % 2)
                rows = slice(a, a + (96 if kind == "mla" else HD))
                for i, _ in block_order(kind):
                    k0 = max(0, i - 1) * P if kind == "swa" else 0
                    n = (i + 1) * P - k0
                    bank, col = (WINDOW_S if kind == "swa" else CAUSAL_S)[i]
                    q = slice(i * P, (i + 1) * P)
                    o = PS[:, bank, col:col + n]
                    x = mm3(o, AQH[rows, s, q], AQL[rows, s, q], AKH[rows, s, k0:k0 + n],
                            AKL[rows, s, k0:k0 + n], True, kind != "fox")
                    if kind == "fox":
                        x = mm(PS[:, bank, col + n - P:col + n], IDENT_R[:, :], TRI_R[:, :], False, True)
                    x.then_inc(scored, 1)

            def turn(h, r):
                window = kind_of(h) == "swa"
                pe.wait_ge(normed, h + 1 + 4 * r)
                if not window:
                    pe.wait_ge(last_normed, (h + 1 if h < MLA_H else h + 1 - SWA_H) + 4 * r)
                if h:
                    pe.wait_ge(pt_lo, h + 4 * r)
                at, to = (WINDOW_AT, WINDOW_T) if window else (CAUSAL_AT, CAUSAL_T)
                for i in range(T):
                    k0 = max(0, i - 1) if window else 0
                    for kb in range(k0, i + 1):
                        o = 3 * S + to[kb] + P * (i - kb)
                        p = at[i] + P * (kb - k0)
                        x = pe.transpose(PSF[:, o:o + P], probs(h)[:, p:p + P], IDENT[:, :])
                x.then_inc(turned, 1)

            def pv(h, r):
                window = kind_of(h) == "swa"
                s, v, bank = h % 2, h // 2 % 2, 6 + h % 2
                pe.wait_ge(pt_lo, h + 1 + 4 * r)
                pe.wait_ge(vstaged, h // 2 + 1 + 2 * r)
                if h >= 2:
                    pe.wait_ge(o_lo, h - 1 + 4 * r)
                if window:
                    for i in range(T):
                        for kb in range(max(0, i - 1), i + 1):
                            p = slice(WINDOW_T[kb] + P * (i - kb), WINDOW_T[kb] + P * (i - kb + 1))
                            x = mm3(PS[:, bank, i * P:(i + 1) * P], AVH[:, v, kb, :], AVL[:, v, kb, :],
                                    PTH[:, s, p], PTL[:, s, p], kb == max(0, i - 1), kb == i)
                else:
                    for kb in range(T):
                        n = S - kb * P
                        p = slice(CAUSAL_T[kb], CAUSAL_T[kb] + n)
                        x = mm3(PS[:, bank, kb * P:S], AVH[:, v, kb, :], AVL[:, v, kb, :],
                                PTH[:, s, p], PTL[:, s, p], kb == 0, kb == T - 1)
                x.then_inc(o_ready, 1)

            def attend_step(h, r, last):
                if h + 2 <= last:
                    qk(h + 2, r)
                turn(h, r)
                if h not in (0, FOX0):
                    pv(h - 1, r)
                if h == last:
                    pv(h, r)

            def boundary(b):
                add, kind, n = BOUND[b]
                for t in range(T):
                    if kind and t < T - 1:
                        pe.wait_ge(centred, 3 * n + t + 1)
                    elif kind:
                        pe.wait_ge(last_centred, n + 1)
                    else:
                        pe.wait_ge(y_ready, Y_BASE[b] + t + 1)
                    src = YN[:, t, :] if kind == "rms" else X[:, t, :]
                    for k in range(KD):
                        x = pe.transpose(PS[:, 2 * t + k // 4, P * (k % 4):P * (k % 4 + 1)],
                                         src[:, k * P:(k + 1) * P], IDENT[:, :])
                    x.then_inc(x_turned, 1)
                pe.wait_ge(yt_copied, 5 * b + 2)

            def hidden(c, groups, g0, new):
                def one(g, r):
                    if g >= 2:
                        pe.wait_ge(relued, g0 + g - 1 + 2 * r)
                    features(c + 4 * g, 4 * (g % 2), 8 * r, new if g == 0 else 0)

                n = 2 + groups % 2
                for g in range(n):
                    one(g, 0)
                with pe.Fori(0, (groups - n) // 2) as r:
                    one(n, r)
                    one(n + 1, r)

            def down(c, k_tiles, groups, g0, k0):
                order = (0, 1, 2, 3) if groups % 2 == 0 else (2, 3, 0, 1)
                pe.wait_ge(relued, g0 + groups - 1)

                def one(k, r):
                    pe.wait_ge(hs_ready, k0 + k + 1 + 4 * r)
                    wide(c + k, 4 * r, HSH[:, k % 2, :], HSL[:, k % 2, :], k == 0,
                         order, (relued, g0 + groups) if k == 0 else None)

                for k in range(4):
                    one(k, 0)
                n = (k_tiles - 8) // 4
                with pe.Fori(0, n) as r:
                    for k in range(4, 8):
                        one(k, r)
                for k in range(4 + 4 * n, k_tiles - 2):
                    one(k, 0)
                pe.wait_ge(hs_ready, k0 + k_tiles - 1)
                wide_end(c + k_tiles - 2, *((HSH[:, k, :], HSL[:, k, :]) for k in (0, 1)),
                         parts_ready=k0 + k_tiles)

            def embedding(c, layer, new):
                for half in range(2):
                    c0 = c + 5 * half
                    if half:
                        pe.wait_ge(emb_z, 8 * layer + 4)
                    tokens(c0, 0, new=0 if half else new)
                    if half:
                        pe.wait_ge(emb_x, 8 * layer + 4)
                    else:
                        pe.wait_ge(emb_ready, layer + 1)
                    chunk(c0 + 4)
                    for t in range(T):
                        ts = slice(t * P, (t + 1) * P)
                        for k in range(PLE_K):
                            w = slice(UNIT * k, UNIT * (k + 1))
                            x = mm3(PS[:, 4 + t, :], EH[:, k, ts], EL[:, k, ts],
                                    WH[:, (c0 + 4) % WS, w], WL[:, (c0 + 4) % WS, w], k == 0, k == 1)
                        x.then_inc(emb_tile, 1)
                    pe.wait_ge(emb_tile, 8 * layer + 4 * half + 4)
                    pe.sem_inc(chunk_used, 1)

            def biases(n):
                pe.wait_ge(evac, 1)
                pe.wait_ge(const_landed, CONST_ALL)
                pe.wait_ge(consts_made, 1)
                if n:
                    pe.wait_ge(bias_out, n)
                for e in range(2):
                    h = 2 * n + e
                    x = mm(PS[:, 6 + e, 0:3 * P], REL[:, h:h + 1].to_broadcast([BUCKETS + 1, P]),
                           ONEHOT[:, :], True, True)
                x.then_inc(bias_made, 1)

            c = FIRST["cq"]
            for k in range(KD):
                cc, u = c + k // 2, UNIT * (k % 2)
                pe.wait_ge(xt_ready, k + 1)
                if k % 2 == 0:
                    chunk(cc)
                for t in range(T):
                    ts = slice(t * P, (t + 1) * P)
                    mm3(PS[:, 4 + t, 0:Q_LORA], XTH[:, k, ts], XTL[:, k, ts],
                        WH[:, cc % WS, u:u + Q_LORA], WL[:, cc % WS, u:u + Q_LORA], k == 0, k == KD - 1)
                w = slice(u + Q_LORA, u + UNIT)
                x = mm3(PS[:, 0, :], WH[:, cc % WS, w], WL[:, cc % WS, w], XTH[:, k, :], XTL[:, k, :],
                        k == 0, k == KD - 1)
                if k % 2:
                    x.then_inc(chunk_used, 1)
            c = FIRST["ckv"]
            for k in range(KD):
                cc, u = c + k // 2, UNIT * (k % 2)
                if k % 2 == 0:
                    chunk(cc)
                for t in range(T):
                    if k == 0 and t == 3:
                        pe.wait_ge(evac, 1)
                    ts = slice(t * P, (t + 1) * P)
                    mm3(PS[:, 1 + t, 0:384], XTH[:, k, ts], XTL[:, k, ts],
                        WH[:, cc % WS, u:u + 384], WL[:, cc % WS, u:u + 384], k == 0, k == KD - 1)
                w = slice(u + 320, u + 448)
                x = mm3(PS[:, 5, :], WH[:, cc % WS, w], WL[:, cc % WS, w], XTH[:, k, :], XTL[:, k, :],
                        k == 0, k == KD - 1)
                if k % 2:
                    x.then_inc(chunk_used, 1)
                    biases(k // 2)
            c = FIRST["qs"]
            pe.wait_ge(bias_out, 4)
            for k in range(KD):
                cc, u = c + k // 2, UNIT * (k % 2)
                if k % 2 == 0:
                    chunk(cc)
                for m in range(4):
                    if k == 0 and m == 3:
                        pe.wait_ge(evac, 2)
                    w = slice(u + P * m, u + P * (m + 1))
                    x = mm3(PS[:, (6 + m) % 8, :], WH[:, cc % WS, w], WL[:, cc % WS, w],
                            XTH[:, k, :], XTL[:, k, :], k == 0, k == KD - 1)
                if k % 2:
                    x.then_inc(chunk_used, 1)
            pe.wait_ge(evac, 2)
            pe.wait_ge(lat_normed, 1)
            for f in range(5):
                if f == 4:
                    pe.wait_ge(evac, 3)
                for t in range(T):
                    x = pe.transpose(PS[:, 2 + f, t * P:(t + 1) * P], CQ[:, t, f * P:(f + 1) * P], IDENT[:, :])
                x.then_inc(lat_turned, 1)
            for n in range(6):
                half, k = n // 3, n % 3
                cc, u = FIRST["uq"] + n // 2, UNIT * (n % 2)
                if k == 0:
                    pe.wait_ge(lat_lo, 5 if half else 3)
                if n % 2 == 0:
                    chunk(cc)
                for m in range(4):
                    w = slice(u + P * m, u + P * (m + 1))
                    x = mm3(PS[:, 4 * half + m, :], WH[:, cc % WS, w], WL[:, cc % WS, w],
                            CTH[:, k, :], CTL[:, k, :], k == 0, k == 2)
                if n % 2:
                    x.then_inc(chunk_used, 1)
            pe.wait_ge(evac, 4)
            pe.wait_ge(plain_out, 1)
            chunk(FIRST["kn"])
            for k in range(2):
                for m in range(4):
                    w = slice(UNIT * k + P * m, UNIT * k + P * (m + 1))
                    x = mm3(PS[:, m, :], WH[:, FIRST["kn"] % WS, w], WL[:, FIRST["kn"] % WS, w],
                            CTH[:, 3 + k, :], CTL[:, 3 + k, :], k == 0, k == 1)
            x.then_inc(chunk_used, 1)
            pe.wait_ge(evac, 5)
            pe.wait_ge(plain_out, 2)
            tokens(FIRST["vm"], 4, CTH[:, 3:5, :], CTL[:, 3:5, :], 2)

            pe.wait_ge(plain_out, 4)
            qk(0, 0)
            qk(1, 0)
            for h in range(16):
                attend_step(h, 0, 15)

            def block_end(b, name_out, name_up, name_down, groups, g0, k_tiles, k0):
                outward(FIRST[name_out], 16 if b == 0 else 32)
                boundary(b)
                if boundaries == b + 1:
                    return
                hidden(FIRST[name_up], groups, g0, b + 2)
                down(FIRST[name_down], k_tiles, groups, g0, k0)

            block_end(0, "out0", "up0", "down0", 8, 0, 32, 0)
            if boundaries <= 1:
                return
            boundary(1)
            if boundaries <= 2:
                return
            embedding(FIRST["ple0"], 0, 3)
            boundary(2)
            if boundaries <= 3:
                return

            chunk0 = FIRST["fox"]
            features(chunk0, 0, new=4)

            def forget_logits(_):
                pe.wait_ge(evac, 7)
                pe.wait_ge(gates_z, 1)
                for k in range(KD):
                    x = mm3(PS[:, 0, :], SWH[:, k, :], SWL[:, k, :], XTH[:, k, :], XTL[:, k, :],
                            k == 0, k == KD - 1)
                x.then_inc(gates_logit, 1)

            def turn_logits(_):
                pe.wait_ge(gates_z, 2)
                for t in range(T):
                    x = pe.transpose(PS[:, 1, RANK * t:RANK * (t + 1)], ZT[:, t * P:(t + 1) * P],
                                     IDENT[0:RANK, 0:RANK])
                x.then_inc(gates_logit, 1)

            def forget_sums(_):
                pe.wait_ge(evac, 8)
                pe.wait_ge(gates_log, 1)
                for t in range(T):
                    mm(PS[0:RANK, 4, :], LF[:, RANK * t:RANK * (t + 1)],
                       STEPS[:, 3 * P - t * P:3 * P - t * P + S], t == 0, t == T - 1)
                for u in range(T):
                    for t in range(u + 1):
                        x = mm(PS[:, 5, RANK * u:RANK * (u + 1)],
                               STEPS[:, 3 * P + (u - t) * P:3 * P + (u - t + 1) * P],
                               LF[:, RANK * t:RANK * (t + 1)], t == 0, t == u)
                x.then_inc(gates_sum, 1)

            features(chunk0 + 4, 4, steps=[[], [(forget_logits, 0)], [(turn_logits, 0)], []])
            pe.wait_ge(gates_z, 3)
            features(chunk0 + 8, 0, steps=[[], [(forget_sums, 0)], [], []])
            pe.wait_ge(gates_rows, 2)
            features(chunk0 + 12, 4)
            pe.wait_ge(evac, 9)
            tokens(chunk0 + 16, 0)
            pe.wait_ge(evac, 10)
            tokens(chunk0 + 20, 4)

            pe.wait_ge(evac, E_FOX - 1)
            qk(FOX0, 0)
            qk(FOX0 + 1, 0)
            for h in (FOX0, FOX0 + 1):
                attend_step(h, 0, FOX0 + 15)
            with pe.Fori(0, 3) as r:
                for h in range(FOX0 + 2, FOX0 + 6):
                    attend_step(h, r, FOX0 + 15)
            for h in (FOX0 + 14, FOX0 + 15):
                attend_step(h, 0, FOX0 + 15)
            block_end(3, "out1", "up1", "down1", 8, 8, 32, 32)
            if boundaries <= 4:
                return
            boundary(4)
            if boundaries <= 5:
                return
            embedding(FIRST["ple1"], 1, 6)
            boundary(5)
            if boundaries <= 6:
                return
            c = FIRST["gla"]
            features(c, 0, new=7)

            def low_rank(_):
                pe.wait_ge(evac, 13)
                pe.wait_ge(gla_prep, 1)
                for k in range(KD):
                    x = mm3(PS[:, 2, :], TWH[:, k, :], TWL[:, k, :], XTH[:, k, :], XTL[:, k, :],
                            k == 0, k == KD - 1)
                x.then_inc(gla_small, 1)

            def gates(_):
                pe.wait_ge(gla_prep, 2)
                for t in range(T):
                    x = mm(PSF[:, 2 * P * t:2 * P * (t + 1)], PAT[0:RANK + 1, t * P:(t + 1) * P],
                           WG[:, :], True, True)
                x.then_inc(gla_small, 1)

            tokens(c + 4, 4, steps=[[], [(low_rank, 0)], [(gates, 0)], []])
            pe.wait_ge(gla_prep, 3)
            tokens(c + 8, 0)
            pe.wait_ge(evac, 14)
            pe.wait_ge(gla_prep, 4)
            for f in range(2):
                for t in range(T):
                    o = PS[:, 4 + f, t * P:(t + 1) * P]
                    mm(o, GLH[:, t, f * P:(f + 1) * P], CHUNKTRI_R[:, :], True, False)
                    x = mm(o, GLL[:, t, f * P:(f + 1) * P], CHUNKTRI_R[:, :], False, True)
            x.then_inc(gla_small, 1)

            def score(t):
                pe.wait_ge(gla_ops, t + 1)
                if t >= 2:
                    pe.wait_ge(out_cut, t - 1)
                for h in range(GLA_H):
                    rows, p = slice(DK * (h % 2), DK * (h % 2 + 1)), h // 2
                    mm3(PS[:, 4 + h % 2, P * p:P * (p + 1)], KIH[rows, p, :], KIL[rows, p, :],
                        QIH[rows, p, :], QIL[rows, p, :], True, True)
                for p in range(2):
                    x = pe.transpose(PS[:, 5, P * (p + 2):P * (p + 3)], KK[:, p, t * P:(t + 1) * P], IDENT[:, :])
                x.then_inc(gla_scored, 1)

            def key_values(t):
                pe.wait_ge(gla_cut, t + 1)
                if t:
                    pe.wait_ge(out_copied, t)
                for e in range(2):
                    rows = slice(GCH * e, GCH * (e + 1))
                    for p in range(2):
                        w = slice(2 * DV * p, 2 * DV * (p + 1))
                        x = mm3(PS[:, 6 + e, w], KTH[rows, P * p:P * (p + 1)], KTL[rows, P * p:P * (p + 1)],
                                VH[rows, t, w], VL[rows, t, w], True, True)
                x.then_inc(gla_kv, 1)

            def output(t):
                pe.wait_ge(gla_states, t + 1)
                for p in range(2):
                    w = slice(2 * DV * p, 2 * DV * (p + 1))
                    for e in range(2):
                        mm3(PS[:, 6, w], QEH[:, e, p, :], QEL[:, e, p, :],
                            STH[:, e, p, :], STL[:, e, p, :], e == 0, False)
                    for h in (2 * p, 2 * p + 1):
                        w = slice(DV * h, DV * (h + 1))
                        x = mm3(PS[:, 6, w], SMH[:, w], SML[:, w], VH[:, t, w], VL[:, t, w],
                                False, h % 2 == 1)
                x.then_inc(gla_out, 1)

            def turn_output(t):
                pe.wait_ge(out_gated, t + 1)
                if t < T - 1:
                    pe.wait_ge(gla_cut, t + 2)
                for f in range(GLA_H):
                    x = pe.transpose(PS[:, 5, f * P:(f + 1) * P], OT[:, t, f * P:(f + 1) * P], IDENT[:, :])
                x.then_inc(out_turned, 1)

            s, v, o, f = score, key_values, output, turn_output
            features(c + 12, 0, freed=0, steps=[[], [(s, 0)], [(v, 0)], [(o, 0), (s, 1)]])
            features(c + 16, 0, freed=4, steps=[[(v, 1)], [(f, 0), (o, 1), (s, 2)], [(v, 2)],
                                                [(f, 1), (o, 2), (s, 3)]])
            features(c + 20, 0, freed=8, steps=[[(v, 3)], [(f, 2), (o, 3)], [], [(f, 3)]])
            pe.wait_ge(out_cut, 4)
            c = FIRST["out2"]
            for k in range(4):
                wide(c + k, 0, OH[:, k, :], OL[:, k, :], k == 0, (2, 3, 0, 1),
                     (mix_out, 16) if k == 0 else None)
            pe.wait_ge(conv_lo, 4)
            for k in (4, 5):
                wide(c + k, 0, XTH[:, k, :], XTL[:, k, :], False)
            wide_end(c + 6, *((XTH[:, k, :], XTL[:, k, :]) for k in (6, 7)))
            boundary(6)
            if boundaries <= 7:
                return
            hidden(FIRST["ffn"], 11, 16, 8)
            down(FIRST["down2"], 22, 11, 16, 64)

        @block.vector
        def _(ve):
            own = Order(ve, ve_own)
            M, A, SUB, MAX, MIN = ALU.mult, ALU.add, ALU.subtract, ALU.max, ALU.min

            def spread(ap, n, at=1):
                shape = list(ap.shape)
                return ap.unsqueeze(at).to_broadcast(shape[:at] + [n] + shape[at:])

            ve.memset(EPS[:, 0:1], LN_EPS)
            ve.memset(EPS[:, 1:2], RMS_EPS)
            for j in range(4):
                w = slice(2 * j, 2 * j + 2)
                ve.wait_ge(xt_hi, j + 1)
                ve.tensor_tensor(XTL[:, w, :], XS[:, w, :], XTH[:, w, :].bitcast(F32), SUB).then_inc(xt_ready, 2)
            ve.wait_ge(const_landed, CONST_ALL)
            ve.tensor_copy(IDENT_R[:, :], IDENT[:, :])
            ve.tensor_copy(TRI_R[:, :], TRI)
            ve.tensor_copy(CHUNKTRI_R[:, :], CHUNKTRI[:, :])
            ve.tensor_scalar(NSINK[:, :], SINK[:, :], -1.0, None, M).then_inc(consts_made, 1)

            ve.wait_ge(chunk_used, FIRST["ckv"])
            ve.tensor_copy(KS[:, :], PS[:, 0, :])
            ve.tensor_copy(CQ[:, :, 0:Q_LORA], PS[:, 4:8, 0:Q_LORA]).then_inc(evac, 1)
            ve.wait_ge(evac, 1)
            for t in range(T):
                ve.bn_stats(CBN[:, t, :], CQ[:, t, 0:Q_LORA])
            for n in range(4):
                ve.wait_ge(bias_made, n + 1)
                ve.tensor_scalar(QM[:, 2 * n:2 * n + 2, 0:3 * P], PS[:, 6:8, 0:3 * P], -1.0, None,
                                 M).then_inc(bias_out, 1)
            ve.wait_ge(chunk_used, FIRST["qs"])
            rope_k, rope_s = ROPET[HD:96, :], ROPET[96:P, :]
            ve.tensor_copy(VS[:, :, :], PS[:, 1:5, KV_LORA:384])
            ve.tensor_tensor(ROT[HD:96, 0, :], PS[HD:96, 5, :], rope_k, M)
            ve.tensor_tensor(ROT[HD:96, 1, :], PS[96:P, 5, :], rope_s, M)
            ve.tensor_copy(CQ[:, :, Q_LORA:], PS[:, 1:5, 0:KV_LORA]).then_inc(evac, 1)
            ve.wait_ge(evac, 2)
            ve.wait_ge(bias_landed, 16)
            ve.tensor_tensor(KM[HD:96, :, :], spread(ROT[HD:96, 0, :], MLA_H), spread(ROT[HD:96, 1, :], MLA_H), A)
            for t in range(T):
                x = ve.bn_stats(CBN[:, T + t, :], CQ[:, t, Q_LORA:])
            own(x)
            for j in range(8):
                x = ve.bn_aggr(CMV[:, j, :], CBN[:, j, :])
            own(x)
            own(ve.tensor_tensor(CMV[:, :, 0], CMV[:, :, 0], CMV[:, :, 0], M))
            ve.tensor_tensor(CMV[:, :, 1], CMV[:, :, 0], CMV[:, :, 1], A).then_inc(lat_sq, 1)
            ve.wait_ge(lat_std, 1)
            own(ve.reciprocal(CRS[:, :], CSTD[:, :]))
            for j in range(8):
                w = slice(0, Q_LORA) if j < T else slice(Q_LORA, Q_LORA + KV_LORA)
                x = ve.tensor_scalar(CQ[:, j % T, w], CQ[:, j % T, w], CRS[:, j:j + 1], None, M)
            x.then_inc(lat_normed, 1)
            ve.wait_ge(chunk_used, FIRST["uq"])
            ve.tensor_scalar(QS[:, 2:4, :], PS[:, 0:2, :], -HD ** -0.5, None, M)
            ve.tensor_scalar(QS[:, 0:2, :], PS[:, 6:8, :], -HD ** -0.5, None, M).then_inc(evac, 1)
            for f in range(5):
                ve.wait_ge(lat_hi, f + 1)
                ve.scalar_tensor_tensor(CTL[:, f, :], PS[:, 2 + f, :], GAIN[:, f:f + 1],
                                        CTH[:, f, :].bitcast(F32), M, SUB).then_inc(lat_lo, 1)
            for half in range(2):
                ve.wait_ge(chunk_used, FIRST["uq"] + 2 + half)
                b, hs = slice(4 * half, 4 * half + 4), slice(4 * half, 4 * half + 4)
                own.mark(ve.scalar_tensor_tensor(ROT[HD:96, :, :], PS[96:P, b, :], -MLA_SCALE,
                                                 spread(rope_s, 4), M, M))
                ve.scalar_tensor_tensor(QM[HD:96, hs, :], PS[HD:96, b, :], -MLA_SCALE, spread(rope_k, 4),
                                        M, M).then_inc(evac, 1)
                own.settled()
                ve.wait_ge(evac, 4 + half)
                own(ve.tensor_tensor(QM[HD:96, hs, :], QM[HD:96, hs, :], ROT[HD:96, :, :], A))
            ve.wait_ge(chunk_used, FIRST["out0"])
            ve.wait_ge(plain_out, 3)
            for n, (hi, lo, src) in enumerate(((AQH, AQL, QM), (AKH, AKL, KM))):
                if n:
                    ve.wait_ge(plain_out, 4)
                own(ve.tensor_copy(hi[0:96, 0, :], src[0:96, 0, :]))
                ve.tensor_tensor(lo[0:96, 0, :], src[0:96, 0, :], hi[0:96, 0, :].bitcast(F32),
                                 SUB).then_inc(first_staged, 1)
            ve.tensor_copy(VM[:, :, :], PS[:, 4:8, :]).then_inc(evac, 1)

            def sums(h, r):
                kind, s = kind_of(h), h % prob_slots(h)
                ve.wait_ge(expd, 4 * (h + 1) + 16 * r)
                if kind == "swa":
                    ve.wait_ge(sunk, h - 7)
                    own(ve.tensor_tensor(SM[:, s, :], SM[:, s, :], ES[:, s, :], A))
                ve.reciprocal(SM[:, s, :], SM[:, s, :]).then_inc(summed, 1)

            def mask(h, r):
                kind, s = kind_of(h), h % prob_slots(h)
                if h >= FOX0 + 4:
                    ve.wait_ge(turned, h - 3 + 4 * r)
                elif h >= 3:
                    ve.wait_ge(turned, min(h - 2, FOX0))
                if kind == "fox":
                    ve.wait_ge(bc_landed[h % 2], 16 * ((h - FOX0) // 2 + 1) + 32 * r)
                for i, in_bank in block_order(kind):
                    n = min(i + 1, 2) * P if kind == "swa" else (i + 1) * P
                    at = (WINDOW_AT if kind == "swa" else CAUSAL_AT)[i]
                    bank, col = (WINDOW_S if kind == "swa" else CAUSAL_S)[i]
                    init = 3e38
                    if kind == "mla":
                        other = MASKROW[:, S - n:S]
                    elif kind == "swa":
                        g = swa_head(h)
                        other, init = BIAS[:, g, 2 * P - n:2 * P], NSINK[:, g:g + 1]
                    else:
                        other = BC[:, h % 2, 0:n]
                    ve.wait_ge(scored, 4 * h + in_bank + 16 * r)
                    if kind == "fox":
                        own.stand()
                    x = ve.tensor_tensor_reduce(out=probs(h)[:, at:at + n], in0=PS[:, bank, col:col + n],
                                                in1=other, scale=1.0, scalar=init, op0=A, op1=MIN,
                                                accum_out=MN[:, s, i:i + 1])
                    x.then_inc(masked, 1)

            def exp_bias(h, r):
                if h >= FOX0:
                    s = h % prob_slots(h)
                    ve.wait_ge(masked, 4 * (h + 1) + 16 * r)
                    cq = CTOK[:, :, bass.ds(h - FOX0 + 4 * r, 1)]
                    nb, mn = (v[:, s, :].unsqueeze(2) for v in (NB, MN))
                    own(ve.tensor_tensor(nb, mn, cq, SUB))
                    ve.tensor_tensor(nb, nb, cq, A).then_inc(biased, 1)

            def normalise(h, r):
                kind, s = kind_of(h), h % prob_slots(h)
                ve.wait_ge(summed, h + 1 + 4 * r)
                at = (WINDOW_AT + [896]) if kind == "swa" else (CAUSAL_AT + [1280])
                for i in range(T if kind == "swa" else T - 1):
                    p = probs(h)[:, at[i]:at[i + 1]]
                    x = ve.tensor_scalar(p, p, SM[:, s, i:i + 1], None, M)
                x.then_inc(normed, 1)

            def probs_lo(h, r):
                n = 896 if kind_of(h) == "swa" else 1280
                ve.wait_ge(pt_hi, h + 1 + 4 * r)
                ve.tensor_tensor(PTL[:, h % 2, 0:n], PSF[:, 3 * S:3 * S + n],
                                 PTH[:, h % 2, 0:n].bitcast(F32), SUB).then_inc(pt_lo, 1)

            def out_lo(h, r):
                rows, tile = slice(HD * (h % 2), HD * (h % 2 + 1)), out_tile(h)
                ve.wait_ge(o_hi, h + 1 + 4 * r)
                ve.tensor_tensor(XTL[rows, tile + 2 * r, :], PS[rows, 6 + h % 2, :],
                                 XTH[rows, tile + 2 * r, :].bitcast(F32), SUB).then_inc(o_lo, 1)

            def attend_step(h, r, last):
                if h + 2 <= last:
                    mask(h + 2, r)
                if h not in (0, 1, FOX0, FOX0 + 1):
                    out_lo(h - 2, r)
                if h < last:
                    sums(h + 1, r)
                if h + 2 <= last:
                    exp_bias(h + 2, r)
                probs_lo(h, r)
                if h < last:
                    normalise(h + 1, r)
                if h == last:
                    out_lo(h - 1, r)
                    out_lo(h, r)

            mask(0, 0)
            mask(1, 0)
            sums(0, 0)
            normalise(0, 0)
            for h in range(16):
                attend_step(h, 0, 15)

            added = [0]

            def boundary(b, end):
                add, kind, n = BOUND[b]
                layer = kind == "layer"

                def residual(t):
                    if add:
                        if t < T - 1:
                            ve.wait_ge(tile_done, 3 * added[0] + t + 1)
                        else:
                            ve.wait_ge(chunk_used, end)
                        a = ALPHA if layer else 1.0
                        x = ve.scalar_tensor_tensor(X[:, t, :], X[:, t, :], a,
                                                    PSF[:, D * t:D * (t + 1)], M, A)
                        if layer:
                            own.mark(x)
                        else:
                            x.then_inc(var_ready, 1)

                def variance(t):
                    own.settled()
                    for j in range(2):
                        x = ve.bn_stats(BNS[:, t, 6 * j:6 * j + 6], X[:, t, UNIT * j:UNIT * (j + 1)])
                    own(x)
                    ve.bn_aggr(MV[:, t, :], BNS[:, t, :]).then_inc(var_ready, 1)

                def scale(t):
                    ve.wait_ge(std_ready, 4 * n + t + 1)
                    x = ve.reciprocal(RSTD[:, t:t + 1], STD[:, t:t + 1])
                    if layer and t < T - 1:
                        own(x)
                        x = ve.tensor_scalar(NMR[:, t:t + 1], MV[:, t, 0:1], RSTD[:, t:t + 1], -1.0, M, M)
                    if layer and t < T - 1:
                        x.then_inc(scale_ready, 1)
                    else:
                        own(x)
                        normed_tile(t)

                def normed_tile(t):
                    x, scale_t, done = X[:, t, :], RSTD[:, t:t + 1], last_centred if t == T - 1 else centred
                    if layer:
                        ve.tensor_scalar(x, x, MV[:, t, 0:1], scale_t, SUB, M).then_inc(done, 1)
                    elif b < 7:
                        ve.wait_ge(var_ready, 4 * n + t + 1)
                        ve.tensor_scalar(YN[:, t, :], x, scale_t, None, M).then_inc(done, 1)
                    else:
                        ve.wait_ge(vec_landed, 144)
                        ve.wait_ge(var_ready, 4 * n + t + 1)
                        ve.scalar_tensor_tensor(x, x, scale_t, G[:, 0, :], M, M).then_inc(y_ready, 1)

                if kind:
                    for t in range(T):
                        residual(t)
                        if t:
                            scale(t - 1)
                        if layer:
                            variance(t)
                    scale(T - 1)
                if b < 7:
                    for k in range(KD):
                        if k == 0:
                            ve.wait_ge(yt_copied, 5 * b + 4)
                            if layer:
                                own(ve.tensor_scalar(YT[:, 0, :], YT[:, 0, :], GAINS[:, n, 0:1],
                                                     BIASES[:, n, 0:1], M, A))
                            elif kind:
                                own(ve.tensor_scalar(YT[:, 0, :], YT[:, 0, :], GAINS[:, n, 0:1], None, M))
                        elif kind:
                            ve.wait_ge(yt_ready, (KD - 1) * n + k)
                        else:
                            ve.wait_ge(yt_copied, 5 * b + 5)
                        own(ve.tensor_copy(XTH[:, k, :], YT[:, k, :]))
                        ve.tensor_tensor(XTL[:, k, :], YT[:, k, :], XTH[:, k, :].bitcast(F32),
                                         SUB).then_inc(xt_ready, 1)
                if layer:
                    ve.wait_ge(vec_landed, 32 * (n + 1))
                    for t in range(T):
                        if t < T - 1:
                            ve.wait_ge(centred, 3 * n + t + 1)
                        else:
                            ve.wait_ge(last_centred, n + 1)
                        own(ve.tensor_tensor(X[:, t, :], X[:, t, :], G[:, 0, :], M))
                        ve.tensor_tensor(X[:, t, :], X[:, t, :], G[:, 1, :], A).then_inc(y_ready, 1)
                    ve.wait_ge(y_ready, Y_BASE[b] + T)
                added[0] += add

            def squares(c, r0, g, r):
                ve.wait_ge(chunk_used, c + 4 * (g + 1) + 8 * r)
                h = HT[:, bass.ds(4 * g + 8 * r, 4), :]
                ve.tensor_scalar(h, PS[:, 4 * (g % 2):4 * (g % 2) + 4, :], 0.0, None, MAX).then_inc(relued, 1)
                ve.wait_ge(relued, r0 + g + 1 + 2 * r)
                own(ve.tensor_tensor(h, h, h, M))

            def hidden(c, r0):
                with ve.Fori(0, 3) as r:
                    own.extra = 2 * r
                    squares(c, r0, 0, r)
                    squares(c, r0, 1, r)
                own.extra = 0
                own.n += 4
                squares(c, r0, 6, 0)
                split_tile(0)
                split_tile(1)
                squares(c, r0, 7, 0)

            def gated_hidden(c, r0):
                def one(g, bank, r):
                    ve.wait_ge(gated, g + 1 + 2 * r)
                    h = HT[:, bass.ds(2 * g + 4 * r, 2), :]
                    ve.tensor_tensor(h, PS[:, bank + 2:bank + 4, :], GT[:, :, :], M).then_inc(relued, 1)

                one(0, 0, 0)
                with ve.Fori(0, 4) as r:
                    one(1, 4, r)
                    one(2, 0, r)
                one(9, 4, 0)
                ve.wait_ge(relued, r0 + 10)
                split_tile(0)
                split_tile(1)
                one(10, 0, 0)
                ve.wait_ge(relued, r0 + 11)

            def split_tile(k, r=0):
                h = HT[:, k + 2 * r, :]
                own(ve.tensor_copy(HSH[:, k % 2, :], h))
                ve.tensor_tensor(HSL[:, k % 2, :], h, HSH[:, k % 2, :].bitcast(F32), SUB).then_inc(hs_ready, 1)

            def split_hidden(c, k_tiles):
                with ve.Fori(0, k_tiles // 2 - 1) as r:
                    own.extra = 2 * r
                    for k in (2, 3):
                        ve.wait_ge(chunk_used, c + k - 1 + 2 * r)
                        split_tile(k, r)
                own.extra = 0
                own.n += k_tiles - 4

            def add_embedding(t, w, n, layer, half):
                ve.wait_ge(emb_x, n + t + 1)
                x = ve.tensor_tensor(X[:, t, w], X[:, t, w], SG[:, t, :], A)
                if half:
                    x.then_inc(var_ready if layer else y_ready, 1)
                return x

            def embedding(c, layer):
                ve.wait_ge(gate_landed, 32 * (layer + 1))
                own(ve.tensor_copy(EH[:, :, :], ER[:, :, :]))
                ve.tensor_tensor(EL[:, :, :], ER[:, :, :], EH[:, :, :].bitcast(F32), SUB).then_inc(emb_ready, 1)
                for half in range(2):
                    w = slice(UNIT * half, UNIT * (half + 1))
                    n = 8 * layer + 4 * half
                    ve.wait_ge(chunk_used, c + 5 * half + 4)
                    for t in range(T):
                        ve.tensor_tensor(SG[:, t, :], PS[:, t, :], BG[:, w], A).then_inc(emb_z, 1)
                    for t in range(T):
                        ve.wait_ge(emb_tile, n + t + 1)
                        ve.wait_ge(emb_sig, n + t + 1)
                        ve.tensor_tensor(SG[:, t, :], SG[:, t, :], PS[:, 4 + t, :], M).then_inc(emb_x, 1)
                        if t:
                            add_embedding(t - 1, w, n, layer, half)
                    x = add_embedding(T - 1, w, n, layer, half)
                    if half == 0:
                        own(x)
                if layer:
                    ve.wait_ge(var_ready, 20)
                else:
                    ve.wait_ge(y_ready, Y_BASE[2] + T)

            ve.wait_ge(x_landed, 16)
            boundary(0, FIRST["up0"])
            if boundaries <= 1:
                return
            hidden(FIRST["up0"], 0)
            split_hidden(FIRST["down0"], 32)
            boundary(1, FIRST["ple0"])
            if boundaries <= 2:
                return
            embedding(FIRST["ple0"], 0)
            boundary(2, 0)
            if boundaries <= 3:
                return

            def pad_parts(hi, lo, src, done):
                for v in (hi, lo):
                    ve.memset(v[:, :, RANK:].bitcast(F32), 0.0)
                own(ve.tensor_copy(hi[:, :, 0:RANK], src[:, :, :]))
                ve.tensor_tensor(lo[:, :, 0:RANK], src[:, :, :], hi[:, :, 0:RANK].bitcast(F32), SUB).then_inc(done, 1)

            ve.wait_ge(fox_landed, 48)
            pad_parts(SWH, SWL, SWR, gates_z)
            c = FIRST["fox"]
            ve.wait_ge(chunk_used, c + 4)
            ve.tensor_scalar(QF[:, 0:4, :], PS[:, 0:4, :], -HD ** -0.5, None, M).then_inc(evac, 1)
            ve.wait_ge(gates_logit, 1)
            ve.tensor_copy(ZT[:, :], PS[0:RANK, 0, :]).then_inc(gates_z, 1)
            ve.wait_ge(gates_logit, 2)
            lz = LZ[:, :].rearrange("p (t h) -> p t h", t=T)
            own(ve.tensor_tensor(lz, PS[:, 1, 0:T * RANK].rearrange("p (t h) -> p t h", t=T),
                                 spread(BF[:, :], T), A))
            ve.scalar_tensor_tensor(LA[:, :], LZ[:, :], -1.0, LZ[:, :], M, MAX).then_inc(gates_z, 1)
            ve.wait_ge(gates_ln, 1)
            ve.scalar_tensor_tensor(LF[:, :], LZ[:, :], 0.0, LA[:, :], MIN, SUB).then_inc(gates_log, 1)
            ve.wait_ge(chunk_used, c + 8)
            ve.tensor_scalar(QF[:, 4:8, :], PS[:, 4:8, :], -HD ** -0.5, None, M).then_inc(evac, 1)
            ve.wait_ge(gates_sum, 1)
            ve.tensor_copy(CC_ROWS[:, :], PS[0:RANK, 4, :]).then_inc(gates_rows, 1)
            ve.tensor_copy(CTOK[:, :, :].rearrange("p t h -> p (t h)"), PS[:, 5, 0:T * RANK]).then_inc(gates_rows, 1)
            ve.wait_ge(chunk_used, c + 12)
            ve.tensor_copy(KF[:, 0:4, :], PS[:, 0:4, :]).then_inc(evac, 1)
            ve.wait_ge(chunk_used, c + 16)
            ve.tensor_copy(KF[:, 4:8, :], PS[:, 4:8, :]).then_inc(evac, 1)
            for n in range(2):
                ve.wait_ge(chunk_used, c + 20 + 4 * n)
                ve.tensor_copy(VF[:, :, UNIT * n:UNIT * (n + 1)], PS[:, 4 * n:4 * n + 4, :]).then_inc(evac, 1)
            mask(FOX0, 0)
            mask(FOX0 + 1, 0)
            exp_bias(FOX0, 0)
            exp_bias(FOX0 + 1, 0)
            sums(FOX0, 0)
            normalise(FOX0, 0)
            for h in (FOX0, FOX0 + 1):
                attend_step(h, 0, FOX0 + 15)
            n = own.n
            with ve.Fori(0, 3) as r:
                own.extra = 20 * r
                for h in range(FOX0 + 2, FOX0 + 6):
                    attend_step(h, r, FOX0 + 15)
            own.extra = 0
            assert own.n - n == 20
            own.n += 40
            for h in (FOX0 + 14, FOX0 + 15):
                attend_step(h, 0, FOX0 + 15)
            boundary(3, FIRST["up1"])
            if boundaries <= 4:
                return
            hidden(FIRST["up1"], 8)
            split_hidden(FIRST["down1"], 32)
            boundary(4, FIRST["ple1"])
            if boundaries <= 5:
                return
            embedding(FIRST["ple1"], 1)
            boundary(5, 0)
            if boundaries <= 6:
                return

            c = FIRST["gla"]
            ve.wait_ge(x_turned, 24)
            ve.wait_ge(gla_const, 64)
            pad_parts(TWH, TWL, TWR, gla_prep)
            ve.memset(QEH[:, :, :, :].bitcast(F32), 0.0)
            ve.memset(QEL[:, :, :, :].bitcast(F32), 0.0)
            ve.memset(ST[:, :, :], 0.0)
            ve.memset(U[:, :, 0:2], 0.0)
            own(ve.memset(PAT[:, :], 1.0))
            ve.wait_ge(chunk_used, c + 4)
            ve.tensor_scalar(QG[:, :, :], PS[:, 0:2, :], DK ** -0.5, None, M)
            ve.tensor_copy(KG[:, :, :], PS[:, 2:4, :]).then_inc(evac, 1)
            ve.wait_ge(gla_small, 1)
            ve.tensor_copy(PAT[0:RANK, :], PS[0:RANK, 2, :]).then_inc(gla_prep, 1)
            ve.wait_ge(gla_small, 2)
            gl = GL[:, :, :].rearrange("p t n -> p (t n)")
            ga = GA[:, :, :].rearrange("p t n -> p (t n)")
            own(ve.tensor_copy(gl, PSF[:, 0:T * 2 * P]))
            x = ve.scalar_tensor_tensor(ga, gl, -1.0, gl, M, MAX)
            x.then_inc(gla_prep, 1)
            ve.wait_ge(chunk_used, c + 8)
            own(ve.tensor_copy(VH[:, :, :], PS[:, 4:8, :]))
            ve.tensor_tensor(VL[:, :, :], PS[:, 4:8, :], VH[:, :, :].bitcast(F32), SUB).then_inc(evac, 1)
            ve.wait_ge(gla_act, 1)
            own(ve.scalar_tensor_tensor(gl, gl, 0.0, ga, MIN, SUB))
            own(ve.tensor_scalar(gl, gl, 1.0 / GATE_NORM, None, M))
            own(ve.tensor_copy(GLH[:, :, :], GL[:, :, :]))
            ve.tensor_tensor(GLL[:, :, :], GL[:, :, :], GLH[:, :, :].bitcast(F32), SUB).then_inc(gla_prep, 1)
            ve.wait_ge(gla_small, 3)
            own(ve.tensor_copy(BT[:, :, :], PS[:, 4:6, :]))
            by_chunk = lambda v: v.rearrange("p f (n c) -> p f n c", c=GCH)
            ends = by_chunk(BT[:, :, :])[:, :, :, GCH - 1:GCH]
            ve.tensor_tensor(by_chunk(KK[:, :, :]), ends.to_broadcast([P, 2, NCH, GCH]),
                             by_chunk(BT[:, :, :]), SUB).then_inc(gla_prep, 1)
            for n, (o, src) in enumerate(((QI, QG), (KI, KG), (KK, KG))):
                ve.wait_ge(gla_act, n + 2)
                x = ve.tensor_tensor(o[:, :, :], o[:, :, :], src, M)
            own(x)

            def operands(t):
                w = slice(t * P, (t + 1) * P)
                own.mark(ve.tensor_copy(KIH[:, :, :], KI[:, :, w]))
                own(ve.tensor_copy(QIH[:, :, :], QI[:, :, w]))
                ve.tensor_tensor(KIL[:, :, :], KI[:, :, w], KIH[:, :, :].bitcast(F32), SUB)
                ve.tensor_tensor(QIL[:, :, :], QI[:, :, w], QIH[:, :, :].bitcast(F32), SUB).then_inc(gla_ops, 1)

            def cut_scores(t):
                ve.wait_ge(gla_scored, t + 1)
                if t:
                    ve.wait_ge(gla_out, t)
                causal = CHUNKTRI[:, :].unsqueeze(1).unsqueeze(1).to_broadcast([P, 2, 2, P])
                own.mark(ve.tensor_tensor(SMF[:, :].rearrange("p (i j n) -> p i j n", i=2, j=2),
                                          PS[:, 4:6, 0:2 * P].rearrange("p j (i n) -> p i j n", i=2), causal, M))
                own(ve.tensor_copy(KTH[:, :], PS[:, 5, 2 * P:4 * P]))
                own.mark(ve.tensor_copy(SMH[:, :], SMF[:, :]))
                ve.tensor_tensor(KTL[:, :], PS[:, 5, 2 * P:4 * P], KTH[:, :].bitcast(F32), SUB)
                own.settled()
                ve.tensor_tensor(SML[:, :], SMF[:, :], SMH[:, :].bitcast(F32), SUB).then_inc(gla_cut, 1)
                ve.wait_ge(gla_ops, t + 1)
                for e in range(2):
                    k = slice(GCH * e, GCH * (e + 1))
                    ve.tensor_copy(QEH[:, e, :, k], QIH[:, :, k].bitcast(F32))
                    x = ve.tensor_copy(QEL[:, e, :, k], QIL[:, :, k].bitcast(F32))
                own(x)

            def states(t):
                ve.wait_ge(gla_kv, t + 1)
                for e in range(2):
                    own(ve.tensor_copy(STH[:, e, :, :], ST[:, :, :]))
                    x = ve.tensor_tensor(STL[:, e, :, :], ST[:, :, :], STH[:, e, :, :].bitcast(F32), SUB)
                    if e:
                        x.then_inc(gla_states, 1)
                        ve.wait_ge(gla_states, t + 1)
                    else:
                        own(x)
                    for p in range(2):
                        for j in range(2):
                            rows, w = slice(DK * j, DK * (j + 1)), slice(DV * j, DV * (j + 1))
                            x = ve.scalar_tensor_tensor(
                                ST[rows, p, w], ST[rows, p, w], DEC[rows, p, 2 * t + e:2 * t + e + 1],
                                PS[rows, 6 + e, 2 * DV * p + DV * j:2 * DV * p + DV * (j + 1)], M, A)
                    own(x)

            def norm_output(t):
                ve.wait_ge(out_copied, t + 1)
                for h in range(GLA_H):
                    x = ve.bn_stats(OBN[:, h, :], OT[:, t, DV * h:DV * (h + 1)])
                own(x)
                for h in range(GLA_H):
                    x = ve.bn_aggr(OMV[:, h, :], OBN[:, h, :])
                own(x)
                own(ve.tensor_tensor(OMV[:, :, 0], OMV[:, :, 0], OMV[:, :, 0], M))
                ve.tensor_tensor(OMV[:, :, 1], OMV[:, :, 0], OMV[:, :, 1], A).then_inc(out_sq, 1)
                ve.wait_ge(out_std, t + 1)
                own(ve.reciprocal(ORS[:, :], OSTD[:, :]))
                for h in range(GLA_H):
                    w = slice(DV * h, DV * (h + 1))
                    x = ve.scalar_tensor_tensor(OT[:, t, w], OT[:, t, w], ORS[:, h:h + 1], GN[:, :], M, M)
                own(x)
                ve.tensor_tensor(OT[:, t, :], OT[:, t, :], GG[:, t, :], M).then_inc(out_gated, 1)

            def output_lo(t):
                ve.wait_ge(gla_hi, t + 1)
                w = slice(t * P, (t + 1) * P)
                ve.tensor_tensor(OL[:, :, w], PS[:, 5, :].rearrange("p (f n) -> p f n", f=4),
                                 OH[:, :, w].bitcast(F32), SUB).then_inc(out_cut, 1)

            operands(0)
            for t in range(T):
                cut_scores(t)
                if t < T - 1:
                    operands(t + 1)
                if t:
                    norm_output(t - 1)
                states(t)
                if t:
                    output_lo(t - 1)
            ve.wait_ge(mix_out, 12)
            own(ve.tensor_tensor(U[:, :, 2:S + 2], U[:, :, 2:S + 2], CV[:, :, :], M))

            def taps(j):
                for f in range(T):
                    x = ve.scalar_tensor_tensor(CV[:, f, :], U[:, f, j:j + S], CW[:, f, j:j + 1],
                                                CV[:, f, :], M, A)
                own(x)

            for f in range(T):
                x = ve.tensor_scalar(CV[:, f, :], U[:, f, 0:S], CW[:, f, 0:1], None, M)
            own(x)
            taps(1)
            norm_output(T - 1)
            taps(2)
            output_lo(T - 1)
            for f in range(T):
                ve.wait_ge(mix_out, 12 + f + 1)
                ve.tensor_tensor(CV[:, f, :], CV[:, f, :], QK[:, f, :], M).then_inc(conv_done, 1)
            for f in range(T):
                ve.wait_ge(conv_hi, f + 1)
                ve.tensor_tensor(XTL[:, 4 + f, :], CV[:, f, :], XTH[:, 4 + f, :].bitcast(F32), SUB).then_inc(conv_lo, 1)
            boundary(6, FIRST["ffn"])
            if boundaries <= 7:
                return
            gated_hidden(FIRST["ffn"], 16)
            split_hidden(FIRST["down2"], 22)
            boundary(7, CHUNKS)

        @block.scalar
        def _(act):
            own = Order(act, act_own)
            F = ACT

            def load(o, i, done):
                act.dma_start(o, i).then_inc(done, 16)

            for j in range(4):
                w = slice(2 * j, 2 * j + 2)
                load(XS[:, w, :], d["xt"][:, w, :], xs_landed[j])
            load(ONEHOT[:, :], d["onehot"], const_landed)
            load(REL[:, :], d["rel"], const_landed)
            load(IDENT[:, :], d["ident"], const_landed)
            load(MASKROW[:, :], d["maskrow"], const_landed)
            load(CHUNKTRI[:, :], d["chunktri"], const_landed)
            load(ROPET[:, :], d["rope"], const_landed)
            load(GAIN[:, :], d["gains"], const_landed)
            load(GAINS[:, :, :], d["gain_cols"], const_landed)
            load(BIASES[:, :, :], d["bias_cols"], const_landed)
            load(SINK[:, :], d["sinks"].to_broadcast([P, SWA_H]), const_landed)
            for j in range(4):
                w = slice(2 * j, 2 * j + 2)
                act.wait_ge(xs_landed[j], 16)
                act.copy(XTH[:, w, :], XS[:, w, :]).then_inc(xt_hi, 1)
            load(X[:, :, :], d["x"], x_landed)
            act.wait_ge(bias_out, 4)
            act.dma_start(d["bias_rows"], QM[:, :, 0:3 * P]).then_inc(bias_stored, 16)
            act.wait_ge(bias_stored, 16)
            load(BIAS[:, :, :], d["bias_skew"], bias_landed)
            act.wait_ge(lat_sq, 1)
            act.wait_ge(bias_landed, 16)
            act.activation(CSTD[:, :], CMV[:, :, 1], F.Sqrt, bias=EPS[:, 0:1]).then_inc(lat_std, 1)
            for f in range(5):
                act.wait_ge(lat_turned, f + 1)
                act.activation(CTH[:, f, :], PS[:, 2 + f, :], F.Copy, scale=GAIN[:, f:f + 1]).then_inc(lat_hi, 1)

            for half in range(2):
                b = slice(4 * half, 4 * half + 4)
                act.wait_ge(chunk_used, FIRST["uq"] + 2 + half)
                act.activation(QM[0:HD, b, :], PS[0:HD, b, :], F.Copy, scale=-MLA_SCALE).then_inc(plain_out, 1)
            act.wait_ge(chunk_used, FIRST["vm"])
            for e in range(2):
                act.copy(KM[0:HD, e::2, :], PS[HD * e:HD * (e + 1), 0:4, :]).then_inc(plain_out, 1)

            def exps(h, r):
                kind, s = kind_of(h), h % prob_slots(h)
                at = (WINDOW_AT + [896]) if kind == "swa" else (CAUSAL_AT + [1280])
                bias = NB if kind == "fox" else MN
                if kind == "fox":
                    act.wait_ge(biased, h + 1 - FOX0 + 4 * r)
                for done, (i, _) in enumerate(block_order(kind)):
                    if kind != "fox":
                        act.wait_ge(masked, 4 * h + done + 1)
                    p = probs(h)[:, at[i]:at[i + 1]]
                    act.activation(p, p, F.Exp, bias=bias[:, s, i:i + 1], scale=-1.0,
                                   accum_out=SM[:, s, i:i + 1]).then_inc(expd, 1)
                if kind == "swa":
                    g = swa_head(h)
                    act.activation(ES[:, s, :], MN[:, s, :], F.Exp, bias=SINK[:, g:g + 1]).then_inc(sunk, 1)

            def normalise_last(h, r):
                if kind_of(h) != "swa":
                    act.wait_ge(summed, h + 1 + 4 * r)
                    p = probs(h)[:, CAUSAL_AT[T - 1]:1280]
                    act.activation(p, p, F.Copy,
                                   scale=SM[:, h % prob_slots(h), T - 1:T]).then_inc(last_normed, 1)

            def probs_hi(h, r):
                n = 896 if kind_of(h) == "swa" else 1280
                act.wait_ge(turned, h + 1 + 4 * r)
                if h >= 2:
                    act.wait_ge(o_ready, h - 1 + 4 * r)
                act.copy(PTH[:, h % 2, 0:n], PSF[:, 3 * S:3 * S + n]).then_inc(pt_hi, 1)

            def out_hi(h, r):
                rows, tile = slice(HD * (h % 2), HD * (h % 2 + 1)), out_tile(h)
                act.wait_ge(o_ready, h + 1 + 4 * r)
                act.copy(XTH[rows, tile + 2 * r, :], PS[rows, 6 + h % 2, :]).then_inc(o_hi, 1)

            def attend_step(h, r, last):
                if h not in (0, 1, FOX0, FOX0 + 1):
                    out_hi(h - 2, r)
                probs_hi(h, r)
                if h + 2 <= last:
                    exps(h + 2, r)
                if h < last:
                    normalise_last(h + 1, r)
                if h == last:
                    out_hi(h - 1, r)
                    out_hi(h, r)

            exps(0, 0)
            exps(1, 0)
            normalise_last(0, 0)
            for h in range(16):
                attend_step(h, 0, 15)

            def vectors(b):
                n = BOUND[b][2]
                load(G[:, 0, :], d["gain_rows"][n:n + 1, :].to_broadcast([P, D]), vec_landed)
                if BOUND[b][1] == "layer":
                    load(G[:, 1, :], d["bias_vecs"][n:n + 1, :].to_broadcast([P, D]), vec_landed)

            def boundary(b):
                add, kind, n = BOUND[b]
                layer = kind == "layer"

                def deviation(t):
                    act.wait_ge(var_ready, 4 * n + t + 1)
                    if layer:
                        x = act.activation(STD[:, t:t + 1], MV[:, t, 1:2], F.Sqrt, bias=EPS[:, 0:1])
                    else:
                        own(act.activation(YN[:, t, :], X[:, t, :], F.Square, accum_out=MV[:, t, 1:2]))
                        x = act.activation(STD[:, t:t + 1], MV[:, t, 1:2], F.Sqrt, bias=EPS[:, 1:2], scale=1.0 / D)
                    x.then_inc(std_ready, 1)

                def centre(t):
                    act.wait_ge(scale_ready, 3 * n + t + 1)
                    act.activation(X[:, t, :], X[:, t, :], F.Identity, bias=NMR[:, t:t + 1],
                                   scale=RSTD[:, t:t + 1]).then_inc(centred, 1)

                def copy_out(t, ks=slice(0, KD)):
                    act.wait_ge(x_turned, 4 * b + t + 1)
                    src = PSF[:, D * t:D * (t + 1)].rearrange("p (k n) -> p k n", k=KD)
                    act.copy(YT[:, ks, t * P:(t + 1) * P], src[:, ks, :]).then_inc(yt_copied, 1)

                for t in range(T):
                    if layer and t:
                        centre(t - 1)
                    if kind:
                        deviation(t)
                    if b < 7 and t >= 2:
                        copy_out(t - 2)
                if b < 7:
                    copy_out(T - 2)
                    copy_out(T - 1, slice(0, KD // 2))
                    if kind:
                        act.wait_ge(yt_copied, 5 * b + 4)
                        for k in range(1, KD):
                            if k == 2:
                                copy_out(T - 1, slice(KD // 2, KD))
                                act.wait_ge(yt_copied, 5 * b + 5)
                            y = YT[:, k, :]
                            if layer:
                                x = act.activation(y, y, F.Identity, bias=BIASES[:, n, k:k + 1],
                                                   scale=GAINS[:, n, k:k + 1])
                            else:
                                x = act.activation(y, y, F.Copy, scale=GAINS[:, n, k:k + 1])
                            x.then_inc(yt_ready, 1)
                    else:
                        copy_out(T - 1, slice(KD // 2, KD))

            def embedding_inputs(layer, tiles_split):
                act.wait_ge(hs_ready, tiles_split)
                load(ER[:, :, :], d["pt"][layer], gate_landed)
                load(BG[:, :], d["gate_bias"][layer:layer + 1, :].to_broadcast([P, D]), gate_landed)

            def embedding(layer):
                for half in range(2):
                    for t in range(T):
                        act.wait_ge(emb_z, 8 * layer + 4 * half + t + 1)
                        act.activation(SG[:, t, :], SG[:, t, :], F.Sigmoid).then_inc(emb_sig, 1)

            act.wait_ge(o_lo, 16)
            vectors(0)
            boundary(0)
            if boundaries <= 1:
                return
            act.wait_ge(y_ready, 4)
            vectors(1)
            embedding_inputs(0, 32)
            boundary(1)
            if boundaries <= 2:
                return
            embedding(0)
            boundary(2)
            if boundaries <= 3:
                return
            act.wait_ge(xt_ready, 4 * KD)
            load(SWR[:, :, :], d["w_forget"], fox_landed)
            load(BF[:, :], d["b_forget"].to_broadcast([P, RANK]), fox_landed)
            load(STEPS[:, :], d["steps"], fox_landed)
            act.wait_ge(gates_z, 3)
            own(act.activation(LA[:, :], LA[:, :], F.Exp, scale=-1.0))
            act.activation(LA[:, :], LA[:, :], F.Ln, bias=1.0).then_inc(gates_ln, 1)
            act.wait_ge(gates_rows, 1)
            act.dma_start(d["gate_rows"], CC_ROWS[:, :]).then_inc(rows_stored, 16)
            exps(FOX0, 0)
            exps(FOX0 + 1, 0)
            normalise_last(FOX0, 0)
            for h in (FOX0, FOX0 + 1):
                attend_step(h, 0, FOX0 + 15)
            with act.Fori(0, 3) as r:
                for h in range(FOX0 + 2, FOX0 + 6):
                    attend_step(h, r, FOX0 + 15)
            for h in (FOX0 + 14, FOX0 + 15):
                attend_step(h, 0, FOX0 + 15)
            act.wait_ge(o_lo, 32)
            vectors(3)
            boundary(3)
            if boundaries <= 4:
                return
            act.wait_ge(y_ready, 16)
            vectors(4)
            embedding_inputs(1, 64)
            boundary(4)
            if boundaries <= 5:
                return
            embedding(1)
            boundary(5)
            if boundaries <= 6:
                return
            act.wait_ge(xt_ready, 7 * KD)
            load(TWR[:, :, :], d["w_gate"], gla_const)
            load(WG[:, :], d["w_gate_up"], gla_const)
            load(CW[:, :, :], d["conv_w"], gla_const)
            load(GN[:, :], d["gla_gain"].to_broadcast([P, DV]), gla_const)
            act.wait_ge(gla_prep, 3)
            own(act.activation(GA[:, :, :], GA[:, :, :], F.Exp, scale=-1.0))
            act.activation(GA[:, :, :], GA[:, :, :], F.Ln, bias=1.0).then_inc(gla_act, 1)
            act.wait_ge(chunk_used, FIRST["gla"] + 12)
            for t in range(T):
                act.activation(GG[:, t, :], PS[:, t, :], F.Silu).then_inc(mix_out, 1)
            act.wait_ge(gla_prep, 5)
            ends = BT[:, :, :].rearrange("p f (n c) -> p f n c", c=GCH)[:, :, :, GCH - 1]
            act.activation(QI[:, :, :], BT[:, :, :], F.Exp).then_inc(gla_act, 1)
            act.activation(DEC[:, :, :], ends, F.Exp)
            act.activation(KI[:, :, :], BT[:, :, :], F.Exp, scale=-1.0).then_inc(gla_act, 1)
            act.activation(KK[:, :, :], KK[:, :, :], F.Exp).then_inc(gla_act, 1)

            def copy_banks(o, chunks):
                act.wait_ge(chunk_used, chunks)
                for m in range(4):
                    act.copy(o[:, m, :], PS[:, m, :]).then_inc(mix_out, 1)

            def output_out(t):
                act.wait_ge(gla_out, t + 1)
                act.copy(OT[:, t, :], PS[:, 6, :]).then_inc(out_copied, 1)

            def output_std(t):
                act.wait_ge(out_sq, t + 1)
                act.activation(OSTD[:, :], OMV[:, :, 1], F.Sqrt, bias=EPS[:, 1:2]).then_inc(out_std, 1)

            def output_hi(t):
                act.wait_ge(out_turned, t + 1)
                act.copy(OH[:, :, t * P:(t + 1) * P],
                         PS[:, 5, :].rearrange("p (f n) -> p f n", f=4)).then_inc(gla_hi, 1)

            c = FIRST["gla"]
            copy_banks(CV, c + 16)
            for t in range(T):
                output_out(t)
                output_std(t)
                output_hi(t)
                if t == 1:
                    copy_banks(U[:, :, 2:S + 2], c + 20)
            copy_banks(QK, c + 24)
            for f in range(T):
                act.wait_ge(conv_done, f + 1)
                act.copy(XTH[:, 4 + f, :], CV[:, f, :]).then_inc(conv_hi, 1)
            boundary(6)
            if boundaries <= 7:
                return
            vectors(7)

            def gate(g, bank, r):
                if g:
                    act.wait_ge(relued, 16 + g + 2 * r)
                act.wait_ge(chunk_used, FIRST["ffn"] + 4 * (g + 1) + 8 * r)
                act.activation(GT[:, :, :], PS[:, bank:bank + 2, :], F.Silu).then_inc(gated, 1)

            gate(0, 0, 0)
            with act.Fori(0, 5) as r:
                gate(1, 4, r)
                gate(2, 0, r)
            boundary(7)


def units(w):
    r, n = w.shape
    return w.reshape(r // P, P, n // UNIT, UNIT).transpose(0, 2, 1, 3)


def by_group(w):
    return units(w).transpose(1, 0, 2, 3).reshape(-1, P, UNIT)


def by_row(w):
    return units(w).reshape(-1, P, UNIT)


def stream_of(i):
    w = i["ev_w_in"][0]
    c_q, c_kv, k_r, q_s, k_s, v_s = np.split(w, np.cumsum([Q_LORA, KV_LORA, ROPE, 512, P]), axis=1)
    swap = lambda v: np.concatenate([v[..., ROPE // 2:], v[..., :ROPE // 2]], -1)
    pairs = lambda v, ax: np.take(v, [j for p in range(4) for j in (p, p + 4)], axis=ax)
    q_s = pairs(q_s.reshape(D, SWA_H, HD), 1).reshape(D, 512)
    pad = np.zeros((D, 64), w.dtype)
    parts = [by_group(np.concatenate([c_q, k_s], 1)),
             by_group(np.concatenate([c_kv, v_s, k_r, swap(k_r), pad], 1)), by_group(q_s)]
    uq = i["ev_w_uq"][0].reshape(Q_LORA, MLA_H, HD + ROPE)
    uq = np.concatenate([uq, swap(uq[..., HD:])], -1).reshape(Q_LORA, MLA_H * P)
    ukv = i["ev_w_ukv"][0].reshape(KV_LORA, MLA_H, 2, HD)
    parts += [by_group(uq), by_group(ukv[:, :, 0].reshape(KV_LORA, 512)),
              by_group(ukv[:, :, 1].reshape(KV_LORA, 512))]
    wo = i["ev_w_out"][0]
    wo = np.concatenate([wo[:512], pairs(wo[512:].reshape(SWA_H, HD, D), 0).reshape(512, D)], 0)

    def dense(layer):
        up, down = i["w_up"][layer], i["w_down"][layer]
        g, e = i["ple_w_gate"][layer], i["ple_w_proj"][layer]
        out = [by_group(up), by_row(down)]
        for half in range(2):
            w = slice(UNIT * half, UNIT * (half + 1))
            out += [by_group(g[:, w]), by_group(e[:, w])]
        return out

    parts += [by_row(wo)] + dense(0)
    parts += [by_group(i["od_w_in"][0][:, :3 * D]), by_row(i["od_w_out"][0])] + dense(1)
    w = i["w_in_2"][0]
    parts += [by_group(np.concatenate([w[:, :1536], w[:, 2064:], w[:, 1552:2064]], 1)), by_row(i["w_out_2"][0])]
    gate, up = (i[n][0].reshape(D, D_FF2 // 256, 256) for n in ("w_ffn_gate_2", "w_ffn_up_2"))
    parts += [by_group(np.concatenate([gate, up], 2).reshape(D, 2 * D_FF2)), by_row(i["w_ffn_down_2"][0])]
    s = np.concatenate(parts, 0)
    return np.ascontiguousarray(s.reshape(CHUNKS, 2, P, UNIT).transpose(0, 2, 1, 3).reshape(CHUNKS, P, CHUNK))


def shape_constants():
    f = np.float32
    p, j = np.arange(P)[:, None], np.arange(P)[None, :]
    maskrow = np.zeros((P, S), f)
    maskrow[:, S - P:] = np.where(j > p, f(BIG), f(0))
    chunktri = ((p <= j) & (p // GCH == j // GCH)).astype(f)
    steps = (np.arange(7 * P)[None, :] - 3 * P >= p).astype(f)
    inv = (1.0 / (10000.0 ** (np.arange(0, ROPE, 2, dtype=f) / ROPE))).astype(f)
    ang = inv[:, None] * np.arange(S, dtype=f)[None, :]
    rope = np.zeros((P, S), f)
    rope[64:96] = np.tile(np.cos(ang), (2, 1))
    rope[96:128] = np.concatenate([-np.sin(ang), np.sin(ang)])
    dist = 2 * P - 1 - np.arange(3 * P)
    exact = BUCKETS // 2
    dd = np.maximum(dist, 1).astype(f)
    large = exact + (np.log(dd / f(exact)) / f(np.log(MAX_DIST / exact)) * f(BUCKETS - exact)).astype(np.int32)
    bucket = np.where(dist < exact, np.maximum(dist, 0), np.minimum(large, BUCKETS - 1))
    inside = (dist >= 0) & (dist < WINDOW)
    onehot = np.zeros((BUCKETS + 1, 3 * P), f)
    onehot[bucket[inside], np.nonzero(inside)[0]] = 1
    onehot[BUCKETS, ~inside] = 1
    return {"ident": np.eye(P, dtype=f), "maskrow": maskrow, "chunktri": chunktri, "steps": steps,
            "rope": rope, "onehot": onehot}


def kernel(**inputs):
    import concourse.bacc as bacc
    from concourse.bass_utils import run_bass_kernel_spmd

    i = {k: np.asarray(v) for k, v in inputs.items()}
    f = np.float32
    tiled = lambda w: np.ascontiguousarray(w.reshape(-1, P, w.shape[-1]).transpose(1, 0, 2))
    arrays = dict(shape_constants())
    arrays["stream"] = stream_of(i)
    arrays["x"] = tiled(i["x"][0])
    arrays["xt"] = tiled(i["x"][0].T)
    arrays["pt"] = np.stack([tiled(i["p"][layer, 0].T) for layer in range(DEPTH)])
    arrays["rel"] = np.concatenate([i["rel_bias"], np.full((1, SWA_H), -BIG, f)])
    arrays["sinks"] = i["ev_sinks"]
    arrays["gains"] = np.ascontiguousarray(
        np.concatenate([i["ev_q_norm"][0], i["ev_kv_norm"][0]]).reshape(5, P).T)
    arrays["gain_rows"] = np.stack([i["ln1_g"][0], i["ln2_g"][0], i["ln1_g"][1], i["ln2_g"][1],
                                    i["norm1_g_2"][0], i["norm2_g_2"][0], i["norm_f_g_2"]])
    arrays["bias_vecs"] = np.stack([i["ln1_b"][0], i["ln2_b"][0], i["ln1_b"][1], i["ln2_b"][1]])
    by_feature = lambda v: np.ascontiguousarray(v.reshape(-1, KD, P).transpose(2, 0, 1))
    arrays["gain_cols"] = by_feature(arrays["gain_rows"])
    arrays["bias_cols"] = by_feature(arrays["bias_vecs"])
    arrays["gate_bias"] = i["ple_b_gate"]
    arrays["w_forget"] = tiled(i["od_w_in"][0][:, 3 * D:])
    arrays["b_forget"] = i["od_b_f"]
    arrays["w_gate"] = tiled(i["w_in_2"][0][:, 1536:1552])
    arrays["w_gate_up"] = np.concatenate([i["w_gate_up_2"][0], i["b_gate_2"]])
    arrays["conv_w"] = np.ascontiguousarray(i["conv_w_2"][0].reshape(3, T, P).transpose(2, 1, 0))
    arrays["gla_gain"] = i["gla_norm_g_2"]
    nc = bacc.Bacc("TRN2", target_bir_lowering=False, num_devices=1)
    d = {n: nc.dram_tensor(n, a.shape, F32, kind="ExternalInput").ap() for n, a in arrays.items()}
    rows = nc.dram_tensor("bias_rows", (P, SWA_H, 3 * P), F32, kind="Internal").ap()
    d["bias_rows"] = rows
    pitch = SWA_H * 3 * P
    d["bias_skew"] = bass.AP(tensor=rows.tensor, offset=P - 1,
                             ap=[[pitch - 1, P], [3 * P, SWA_H], [1, 2 * P]])
    d["gate_rows"] = nc.dram_tensor("gate_rows", (RANK, S), F32, kind="Internal").ap()
    out = nc.dram_tensor("out", (P, T, D), F32, kind="ExternalOutput").ap()
    program(nc, d, out)
    r = run_bass_kernel_spmd(nc, [arrays], core_ids=[0])
    return np.ascontiguousarray(r.results[0]["out"].transpose(1, 0, 2)).reshape(1, S, D)
```
